# Optimizing a Trainium2 kernel written in Bass

```python
import math
import jax, jax.numpy as jnp
from jax import lax
import numpy as np

D_MODEL = 1024
BATCH = 1
SEQ = 512
DEPTH = 1
DEC_BATCH = 1
DEC_SEQ = 32
PAST_LEN = 128

CHUNK = 64
QBLOCK = 128
EPS = 1e-6
NEG_INF = -1e30

A_HEADS = 8
A_HEAD_DIM = 64
A_WIDTH = A_HEADS * A_HEAD_DIM
DECAY_LORA = 64
AAA_LORA = 64
GATE_LORA = 160
A_COLS = 3 * A_WIDTH + DECAY_LORA + AAA_LORA + GATE_LORA
GN_EPS = 64e-5
SPLIT_A = (A_WIDTH, 2 * A_WIDTH, 3 * A_WIDTH, 3 * A_WIDTH + DECAY_LORA,
           3 * A_WIDTH + DECAY_LORA + AAA_LORA)

B_HEADS = 4
B_HEAD_DIM = 64
B_VDIM = 2 * B_HEAD_DIM
B_QK_WIDTH = B_HEADS * 2 * B_HEAD_DIM
B_V_WIDTH = B_HEADS * B_VDIM
B_COLS = 2 * B_QK_WIDTH + B_V_WIDTH

GATE_COLS = 2 * D_MODEL
N_IN = A_COLS + B_COLS + GATE_COLS
SPLIT_IN = (A_COLS, A_COLS + B_QK_WIDTH, A_COLS + 2 * B_QK_WIDTH, A_COLS + B_COLS)

D_FF = ((8 * D_MODEL + 3 * 256 - 1) // (3 * 256)) * 256

kernel_name = 'rwkv7_diffattn_gated_streaming_encoder'

def _rmsnorm(x, g):
    xf = x.astype(jnp.float32)
    xf = xf * lax.rsqrt(jnp.mean(xf * xf, axis=-1, keepdims=True) + EPS)
    return (xf * g.astype(jnp.float32)).astype(x.dtype)

def _head_layernorm(y, w, b):
    mu = jnp.mean(y, axis=-1, keepdims=True)
    var = jnp.mean(jnp.square(y - mu), axis=-1, keepdims=True)
    yn = ((y - mu) * lax.rsqrt(var + GN_EPS)).reshape(y.shape[0], y.shape[1], -1)
    return yn * w.astype(jnp.float32) + b.astype(jnp.float32)

def _wkv_scan(r, decay, k, v, kk, b, s0):
    xs = tuple(jnp.moveaxis(z.astype(jnp.float32), 1, 0) for z in (r, decay, k, v, kk, b))

    def step(s, inp):
        r_t, d_t, k_t, v_t, kk_t, b_t = inp
        sa = jnp.einsum('bhvk,bhk->bhv', s, -kk_t)
        s = (s * d_t[:, :, None, :] + sa[..., None] * b_t[:, :, None, :]
             + v_t[..., None] * k_t[:, :, None, :])
        return s, jnp.einsum('bhvk,bhk->bhv', s, r_t)

    s_fin, ys = lax.scan(step, s0.astype(jnp.float32), xs)
    return jnp.moveaxis(ys, 0, 1), s_fin

def _rwkv7(c, shift_prev, s0, mu, w0, w2, a0, a2, g2, k_k, k_a, r_k, ln_w, ln_b):
    bsz, t = c.shape[0], c.shape[1]
    prev = jnp.concatenate([shift_prev.astype(c.dtype), c[:, :-1]], axis=1)
    xs = c + (prev - c) * mu
    r, k, v, wd, ad, gd = jnp.split(xs, SPLIT_A, axis=-1)
    w = -jax.nn.softplus(-(w0 + jnp.tanh(wd) @ w2)) - 0.5
    decay = jnp.exp(-jnp.exp(w.astype(jnp.float32)))
    a = jax.nn.sigmoid(a0 + ad @ a2)
    g = jax.nn.sigmoid(gd) @ g2
    hs = lambda z: z.reshape(bsz, t, A_HEADS, A_HEAD_DIM)
    kk = hs((k * k_k).astype(jnp.float32))
    kk = kk * lax.rsqrt(jnp.maximum(jnp.sum(kk * kk, axis=-1, keepdims=True), 1e-24))
    k = k * (1.0 + (a - 1.0) * k_a)
    r4, k4, v4, a4 = hs(r), hs(k), hs(v), hs(a)
    y, s_fin = _wkv_scan(r4, hs(decay), k4, v4, kk, kk * a4, s0)
    bonus = jnp.sum(r4 * k4 * r_k, axis=-1, keepdims=True) * v4
    y = _head_layernorm(y, ln_w, ln_b) + bonus.reshape(bsz, t, A_WIDTH).astype(jnp.float32)
    return (y * g.astype(jnp.float32)).astype(c.dtype), s_fin.astype(s0.dtype), c[:, -1:]

def _diff_core(q, k, v, lam, mask):
    s = jnp.einsum('bqhnd,bkhnd->bnhqk', q, k).astype(jnp.float32) * (B_HEAD_DIM ** -0.5)
    if mask is not None:
        s = jnp.where(mask, s, NEG_INF)
    p = jax.nn.softmax(s, axis=-1)
    attn = p[:, 0] - lam * p[:, 1]
    return jnp.einsum('bhqk,bkhe->bqhe', attn.astype(v.dtype), v)

def _diff_attn_chunk_causal(q, k, v, lam):
    bsz, t = q.shape[0], q.shape[1]
    nb = t // QBLOCK
    qb = jnp.moveaxis(q.reshape(bsz, nb, QBLOCK, B_HEADS, 2, B_HEAD_DIM), 1, 0)
    key_chunk = jnp.arange(t) // CHUNK

    def one_block(args):
        q_blk, blk = args
        q_chunk = (blk * QBLOCK + jnp.arange(QBLOCK)) // CHUNK
        mask = key_chunk[None, :] <= q_chunk[:, None]
        return _diff_core(q_blk, k, v, lam, mask)

    out = lax.map(one_block, (qb, jnp.arange(nb)))
    return jnp.moveaxis(out, 0, 1).reshape(bsz, t, B_HEADS, B_VDIM)

def _layer(x, shift_prev, s0, k_past, v_past, p, lam_init):
    bsz, t = x.shape[0], x.shape[1]
    h = _rmsnorm(x, p['norm_mix_pre'])
    c = h @ p['w_in']
    c_a, q, k, v, g_in = jnp.split(c, SPLIT_IN, axis=-1)
    y_a, s_new, shift_new = _rwkv7(c_a, shift_prev, s0, p['rwkv_mu'], p['rwkv_w0'], p['rwkv_w2'],
                                   p['rwkv_a0'], p['rwkv_a2'], p['rwkv_g2'], p['rwkv_k_k'],
                                   p['rwkv_k_a'], p['rwkv_r_k'], p['rwkv_ln_w'], p['rwkv_ln_b'])
    q = q.reshape(bsz, t, B_HEADS, 2, B_HEAD_DIM)
    k = k.reshape(bsz, t, B_HEADS, 2, B_HEAD_DIM)
    v = v.reshape(bsz, t, B_HEADS, B_VDIM)
    f32 = jnp.float32
    lam = (jnp.exp(jnp.sum(p['lq1'].astype(f32) * p['lk1'].astype(f32)))
           - jnp.exp(jnp.sum(p['lq2'].astype(f32) * p['lk2'].astype(f32))) + lam_init)
    if k_past is None:
        o = _diff_attn_chunk_causal(q, k, v, lam)
    else:
        k_all = jnp.concatenate([k_past.astype(k.dtype), k], axis=1)
        v_all = jnp.concatenate([v_past.astype(v.dtype), v], axis=1)
        o = _diff_core(q, k_all, v_all, lam, None)
    o = (_rmsnorm(o, p['subln']) * (1.0 - lam_init)).reshape(bsz, t, B_V_WIDTH)
    g_a, g_b = jnp.split(jax.nn.sigmoid(g_in + p['b_gate']), 2, axis=-1)
    mix = g_a * (y_a @ p['w_out_a']) + g_b * (o @ p['w_out_b'])
    x = x + _rmsnorm(mix @ p['w_o'], p['norm_mix_post'])
    u_g, u_v = jnp.split(_rmsnorm(x, p['norm_ffn_pre']) @ p['w_ffn_in'], 2, axis=-1)
    x = x + _rmsnorm((jax.nn.silu(u_g) * u_v) @ p['w_ffn_out'], p['norm_ffn_post'])
    return x, k, v, s_new, shift_new

def _nrm(k, shape, scale):
    return jax.random.normal(k, shape, jnp.float32) * scale

def setup_inputs(seed: int = 0) -> dict:
    key = jax.random.key(seed)
    ks = jax.random.split(key, 40)
    L = DEPTH
    return {
        'x_prompt': _nrm(ks[0], (BATCH, SEQ, D_MODEL), 1.0),
        'x_sample': _nrm(ks[1], (DEC_BATCH, DEC_SEQ, D_MODEL), 1.0),
        'cache_k': _nrm(ks[2], (L, DEC_BATCH, PAST_LEN, B_HEADS, 2, B_HEAD_DIM), 1.0),
        'cache_v': _nrm(ks[3], (L, DEC_BATCH, PAST_LEN, B_HEADS, B_VDIM), 1.0),
        'state_wkv': _nrm(ks[4], (L, DEC_BATCH, A_HEADS, A_HEAD_DIM, A_HEAD_DIM), 1.0),
        'state_shift': _nrm(ks[5], (L, DEC_BATCH, 1, A_COLS), 1.0),
        'norm_mix_pre': 1.0 + _nrm(ks[6], (L, D_MODEL), 0.05),
        'norm_mix_post': 1.0 + _nrm(ks[7], (L, D_MODEL), 0.05),
        'norm_ffn_pre': 1.0 + _nrm(ks[8], (L, D_MODEL), 0.05),
        'norm_ffn_post': 1.0 + _nrm(ks[9], (L, D_MODEL), 0.05),
        'w_in': _nrm(ks[10], (L, D_MODEL, N_IN), D_MODEL ** -0.5),
        'b_gate': _nrm(ks[11], (L, GATE_COLS), 0.1),
        'rwkv_mu': jax.random.uniform(ks[12], (L, A_COLS), jnp.float32, 0.0, 1.0),
        'rwkv_w0': jax.random.uniform(ks[13], (L, A_WIDTH), jnp.float32, -6.0, -1.0),
        'rwkv_w2': _nrm(ks[14], (L, DECAY_LORA, A_WIDTH), 0.5 * DECAY_LORA ** -0.5),
        'rwkv_a0': _nrm(ks[15], (L, A_WIDTH), 0.1),
        'rwkv_a2': _nrm(ks[16], (L, AAA_LORA, A_WIDTH), AAA_LORA ** -0.5),
        'rwkv_g2': _nrm(ks[17], (L, GATE_LORA, A_WIDTH), GATE_LORA ** -0.5),
        'rwkv_k_k': 0.85 + _nrm(ks[18], (L, A_WIDTH), 0.05),
        'rwkv_k_a': 1.0 + _nrm(ks[19], (L, A_WIDTH), 0.05),
        'rwkv_r_k': _nrm(ks[20], (L, A_HEADS, A_HEAD_DIM), 0.1),
        'rwkv_ln_w': 1.0 + _nrm(ks[21], (L, A_WIDTH), 0.05),
        'rwkv_ln_b': _nrm(ks[22], (L, A_WIDTH), 0.05),
        'diff_lq1': _nrm(ks[23], (L, B_HEAD_DIM), 0.1),
        'diff_lk1': _nrm(ks[24], (L, B_HEAD_DIM), 0.1),
        'diff_lq2': _nrm(ks[25], (L, B_HEAD_DIM), 0.1),
        'diff_lk2': _nrm(ks[26], (L, B_HEAD_DIM), 0.1),
        'diff_subln': 1.0 + _nrm(ks[27], (L, B_VDIM), 0.05),
        'w_out_a': _nrm(ks[28], (L, A_WIDTH, D_MODEL), A_WIDTH ** -0.5),
        'w_out_b': _nrm(ks[29], (L, B_V_WIDTH, D_MODEL), B_V_WIDTH ** -0.5),
        'w_o': _nrm(ks[30], (L, D_MODEL, D_MODEL), D_MODEL ** -0.5),
        'w_ffn_in': _nrm(ks[31], (L, D_MODEL, 2 * D_FF), D_MODEL ** -0.5),
        'w_ffn_out': _nrm(ks[32], (L, D_FF, D_MODEL), D_FF ** -0.5),
    }

def reference(x_prompt, x_sample, cache_k, cache_v, state_wkv, state_shift,
              norm_mix_pre, norm_mix_post, norm_ffn_pre, norm_ffn_post, w_in, b_gate,
              rwkv_mu, rwkv_w0, rwkv_w2, rwkv_a0, rwkv_a2, rwkv_g2, rwkv_k_k, rwkv_k_a,
              rwkv_r_k, rwkv_ln_w, rwkv_ln_b, diff_lq1, diff_lk1, diff_lq2, diff_lk2,
              diff_subln, w_out_a, w_out_b, w_o, w_ffn_in, w_ffn_out):
    yp, ys = x_prompt, x_sample
    bsz_p = x_prompt.shape[0]
    kp_l, vp_l, sp_l, hp_l = [], [], [], []
    ks_l, vs_l, ss_l, hs_l = [], [], [], []
    for l in range(DEPTH):
        lam_init = 0.8 - 0.6 * math.exp(-0.3 * l)
        p = dict(norm_mix_pre=norm_mix_pre[l], norm_mix_post=norm_mix_post[l],
                 norm_ffn_pre=norm_ffn_pre[l], norm_ffn_post=norm_ffn_post[l],
                 w_in=w_in[l], b_gate=b_gate[l], rwkv_mu=rwkv_mu[l], rwkv_w0=rwkv_w0[l],
                 rwkv_w2=rwkv_w2[l], rwkv_a0=rwkv_a0[l], rwkv_a2=rwkv_a2[l], rwkv_g2=rwkv_g2[l],
                 rwkv_k_k=rwkv_k_k[l], rwkv_k_a=rwkv_k_a[l], rwkv_r_k=rwkv_r_k[l],
                 rwkv_ln_w=rwkv_ln_w[l], rwkv_ln_b=rwkv_ln_b[l], lq1=diff_lq1[l], lk1=diff_lk1[l],
                 lq2=diff_lq2[l], lk2=diff_lk2[l], subln=diff_subln[l], w_out_a=w_out_a[l],
                 w_out_b=w_out_b[l], w_o=w_o[l], w_ffn_in=w_ffn_in[l], w_ffn_out=w_ffn_out[l])
        shift0 = jnp.zeros((bsz_p, 1, A_COLS), x_prompt.dtype)
        s0 = jnp.zeros((bsz_p, A_HEADS, A_HEAD_DIM, A_HEAD_DIM), x_prompt.dtype)
        yp, kp, vp, sp, hp = _layer(yp, shift0, s0, None, None, p, lam_init)
        ys, kn, vn, sn, hn = _layer(ys, state_shift[l], state_wkv[l], cache_k[l], cache_v[l], p, lam_init)
        kp_l.append(kp); vp_l.append(vp); sp_l.append(sp); hp_l.append(hp)
        ks_l.append(kn); vs_l.append(vn); ss_l.append(sn); hs_l.append(hn)
    return (yp, ys, jnp.stack(kp_l), jnp.stack(vp_l), jnp.stack(sp_l), jnp.stack(hp_l),
            jnp.stack(ks_l), jnp.stack(vs_l), jnp.stack(ss_l), jnp.stack(hs_l))


_drawn_inputs = setup_inputs


def setup_inputs(seed=0):
    import zlib

    import numpy as np

    out = dict(_drawn_inputs(seed))
    spreads = {}
    factors = {'diff_lk2': 3.241}
    for name, (base, spread) in spreads.items():
        noise = np.random.default_rng([zlib.crc32(name.encode()), seed]).standard_normal(out[name].shape)
        drawn = base * np.exp(spread * noise) if base else spread * noise
        out[name] = __import__('jax').numpy.asarray(drawn.astype(out[name].dtype))
    for name, factor in factors.items():
        out[name] = (out[name] * factor).astype(out[name].dtype)
    return out
```

```python
import math
from contextlib import ExitStack

import numpy as np

import concourse.bass as bass
from concourse import mybir

ALU = mybir.AluOpType
ACT = mybir.ActivationFunctionType
AX = mybir.AxisListType
F32 = mybir.dt.float32
F32R = mybir.dt.float32r

P = 128
D = 1024
KT = D // P
SEQ, DEC, PAST = 512, 32, 128
TOK = SEQ + DEC
HALF = TOK // 2
J = TOK + 1
JS = SEQ + 1
CHUNK = 64
NCH = SEQ // CHUNK
EPS = 1e-6
NEG = -1e30
AH, AD = 8, 64
AW = AH * AD
CT = AW // P
GATE_LORA = 160
A_COLS = 3 * AW + 64 + 64 + GATE_LORA
GN_EPS = 64e-5
BH, BD_, BV = 4, 64, 128
BW = BH * BV
N_IN = A_COLS + 3 * BW + 2 * D
D_FF = ((8 * D + 3 * 256 - 1) // (3 * 256)) * 256
FT = D_FF // P
LAM_INIT = 0.8 - 0.6 * math.exp(0.0)
SCALE = BD_ ** -0.5
DECAY = math.exp(-0.5)
LEVELS = [2, 4, 8, 16, 32]
TILES = [(t * P, P) for t in range(SEQ // P)] + [(SEQ, DEC)]
NT = len(TILES)
SAMPLE = NT - 1

NC = 15
CCOL = [min(P * i, A_COLS - P) for i in range(NC)]
CR, CK, CV, CWA, CG, CG2 = 0, 4, 8, 12, 13, 14
G2P = P - 32

PV_SHIFT, PV_MU, PV_W0, PV_A0, PV_KK, PV_KA, PV_RK, PV_LNW, PV_LNB, PV_BG = 0, 15, 30, 34, 38, 42, 46, 50, 54, 58
PV_N = PV_BG + 2 * KT

K_ID, K_SC = 0, P
K_M0 = K_SC + 2 * P
K_LV = K_M0 + P
K_BD = K_LV + len(LEVELS) * 64
K_I64 = K_BD + P
K_SCAN = K_I64 + 64
K_N = K_SCAN + J


def constants():
    c = np.zeros((P, K_N), np.float32)
    j, i = np.meshgrid(np.arange(P), np.arange(P), indexing="ij")
    same = j // CHUNK == i // CHUNK
    c[:, K_ID:K_ID + P] = np.eye(P)
    c[:, K_SC:K_SC + P] = (j < i) & same
    c[:, K_SC + P:K_SC + 2 * P] = (j <= i) & same
    c[:, K_M0:K_M0 + P] = (i == j + 1) & (j % 2 == 0)
    row, col = np.meshgrid(np.arange(P), np.arange(64), indexing="ij")
    for n, s in enumerate(LEVELS):
        c[:, K_LV + 64 * n:K_LV + 64 * (n + 1)] = (row // (2 * s) == col // s) & (row % (2 * s) >= s)
    c[:, K_BD:K_BD + P] = j // 64 == i // 64
    c[:, K_I64:K_I64 + 64] = row % 64 == col
    c[:, K_SCAN:K_SCAN + J] = 1.0
    for n in range(NCH):
        c[:, K_SCAN + n * CHUNK] = 0.0
    c[:, K_SCAN + JS] = 0.0
    return c


DENSE = ([("qkv", i) for i in range(12)] + [("c", i) for i in range(NC)] + [("gB", i) for i in range(8)]
         + [("outB", i) for i in range(8)])
GA_RING = 5
GA_OUT = ([("gA", i) for i in range(5)] + [("outA", 0), ("outA", 1), ("gA", 5), ("gA", 6), ("outA", 2), ("outA", 3),
          ("gA", 7)] + [("outA", i) for i in range(4, 8)])
DENSE += GA_OUT
DENSE += [("wo", i) for i in range(8)]
FFN_BLOCK0 = len(DENSE)
DENSE += [(("ug", "uv")[i % 2], i // 2) for i in range(2 * FT)]
DENSE += [("down", i) for i in range(8)]
BLOCK = {d: n for n, d in enumerate(DENSE)}
DOWN_PARTS = [(0, 8), (8, 7), (15, 7)]

UNITS, SEGS = [], []
for _kind, _i in DENSE:
    if _kind in ("outA", "outB"):
        if _i % 2 == 0:
            UNITS.append((_kind, _i // 2, 0))
        SEGS.append((len(UNITS) - 1, _kind, _i))
    elif _kind == "down":
        for _p in range(3):
            UNITS.append((_kind, _i, _p))
            SEGS.append((len(UNITS) - 1, _kind, _i))
    else:
        UNITS.append((_kind, _i, 0))
        SEGS.append((len(UNITS) - 1, _kind, _i))
UNIT_END = {u: max(n for n, s in enumerate(SEGS) if s[0] == u) + 1 for u in range(len(UNITS))}
BLOCK_END = {d: max(n for n, s in enumerate(SEGS) if s[1:] == d) + 1 for d in DENSE}
UNIT_OF = {}
for _n, _s in enumerate(SEGS):
    UNIT_OF.setdefault(_s[1:], []).append((_s[0], _n))
FFN_UNIT0 = UNIT_OF[("ug", 0)][0][0]
FFN_SEG0 = UNIT_OF[("ug", 0)][0][1]
DOWN_UNIT0 = UNIT_OF[("down", 0)][0][0]

WKV = [(t, g) for t in range(NT) for g in range(2)]


def levels(t):
    return range(len(LEVELS) if t < SAMPLE else len(LEVELS) - 1)


def schedule():
    s = [("params",)] + [("norm", t) for t in range(NT)]
    s += [("dense", "qkv", i) for i in range(12)]
    s += [("cache",)] + [("kvtok", t) for t in range(NT)]
    att = [("att", t, h) for t in range(NT) for h in range(BH)]
    for i in range(NC):
        s += [("dense", "c", i)] + att[:1]
        att = att[1:]
        if i % 3 == 2:
            s += att[:1]
            att = att[1:]
    s += att + [("oscale",)] + [("ofin", t) for t in range(NT)]
    s += [("shift", i) for i in range(NC)] + [("shiftout",), ("lora",)]
    s += [("knorm", c) for c in range(CT)] + [("krsqrt",)]
    for c in range(CT):
        s += [("dense", "gB", 2 * c), ("rw1", c), ("dense", "gB", 2 * c + 1), ("rw2", c)]
    s += [("init0",)]
    n = 0
    for t, g in WKV:
        if (t, g) == (SAMPLE, 0):
            s += [("init",)]
        s += [("w", st, t, g) for st in ("tok", "scores", "gv", "x0")]
        s += [("wl", l, t, g) for l in levels(t)]
        if n < 8:
            s += [("dense", "outB", n)]
            n += 1
        s += [("w", st, t, g) for st in ("wu", "ef", "chain", "q", "y")]
        if t >= SAMPLE - 1:
            s += [("final", t, g)]
    tail = [("ymean", c) for c in range(CT)] + [("yvar", c) for c in range(CT)] + [("yfin", c) for c in range(CT)]
    for k, i in GA_OUT[:5]:
        s += [("dense", k, i)] + tail[:2]
        tail = tail[2:]
    s += tail
    s += [("dense", k, i) for k, i in GA_OUT[5:]]
    for i in range(8):
        s += [("dense", "wo", i)]
        if i:
            s += [("ztok", 0, i - 1)]
    s += [("ztok", 0, 7), ("zpost", 0), ("ffn",)]
    for i in range(8):
        s += [("dense", "down", i)]
        if i:
            s += [("ztok", 1, i - 1)]
    s += [("ztok", 1, 7), ("zpost", 1)]
    return s


SCHEDULE = schedule()


def fills(step):
    k = step[0]
    if k == "params":
        return ["pv"]
    if k == "norm":
        return ["n0", "n1"]
    if k == "cache":
        return ["ck"]
    if k == "kvtok":
        return ["k", "v"]
    if k == "att":
        return ["s0", "s1", "pt", "o"]
    if k == "ofin":
        return ["o"]
    if k == "shiftout":
        return ["s"]
    if k == "knorm":
        return ["q0", "q1"]
    if k == "rw1":
        return ["w0", "w1", "a0", "a1"]
    if k == "rw2":
        return ["b0", "b1"]
    if k == "init":
        return ["s"]
    if k == "w":
        return {"tok": ["t0", "t1"], "scores": ["b0", "b1", "k0", "k1"], "gv": ["gv"], "x0": ["x"], "wu": ["wu"],
                "ef": ["e0", "e1"] if step[2] < SAMPLE else ["e0"],
                "chain": ["c0", "c1"] if step[2] < SAMPLE else ["c0"], "q": ["q"], "y": ["y"]}[step[1]]
    if k == "wl":
        return ["m", "d", "t"]
    if k == "final":
        return ["f"]
    if k in ("ymean", "yvar"):
        return ["m0", "m1"]
    if k == "yfin":
        return ["g0", "g1"]
    if k == "ztok":
        return ["z0", "z1"]
    if k == "zpost" and step[1] == 0:
        return [f"n{t}{i}" for t in range(NT) for i in range(2)]
    return []


FILL = {}
for _s in SCHEDULE:
    for _f in fills(_s):
        FILL[(_s, _f)] = len(FILL)


def encoder_kernel(nc, i_, o_):
    ctx = ExitStack()
    phase2 = ExitStack()
    region = ExitStack()

    def sb(name, shape, dt=F32, at=ctx):
        return at.enter_context(nc.sbuf_tensor(name, shape, dt))

    def sem(name):
        return ctx.enter_context(nc.semaphore(name))

    h_hi = sb("h_hi", [P, KT, TOK], F32R)
    h_lo = sb("h_lo", [P, KT, TOK], F32R)
    w_raw = sb("w_raw", [P, 2, D])
    w_hi = sb("w_hi", [P, 2, D], F32R)
    w_lo = sb("w_lo", [P, 2, D], F32R)
    gain = sb("gain", [P, D])
    pv = sb("pv", [P, PV_N])
    pvh = sb("pvh", [P, PV_N])
    ident = sb("ident", [P, P])
    ssq = sb("ssq", [P, NT])
    rms = sb("rms", [P, NT])
    rstd = sb("rstd", [P, NT])

    cst = sb("cst", [P, K_N], at=phase2)
    pv_rows = sb("pv_rows", [PV_N, P], at=phase2)
    oka = sb("oka", [P, CT], at=phase2)
    wa2 = sb("wa2", [P, AW], at=phase2)
    g2a = sb("g2a", [P, AW], at=phase2)
    g2b = sb("g2b", [P, AW], at=phase2)
    last = sb("last", [P, 2, NC], at=phase2)
    lastT = sb("lastT", [2 * NC, P], at=phase2)
    pend = sb("pend", [P, CT, NCH + 1], at=phase2)
    C = sb("C", [P, NC, J + 1], at=phase2)
    mb = sb("mb", [P, 8, TOK], at=phase2)
    o_hi = sb("o_hi", [P, BH, TOK], F32R, at=phase2)
    o_lo = sb("o_lo", [P, BH, TOK], F32R, at=phase2)

    xs = sb("xs", [P, 2, D], at=region)
    xn = sb("xn", [P, 2, D], at=region)
    region.close()
    qkv = sb("qkv", [P, 12, TOK], at=region)
    vtok = sb("vtok", [P, NT, BW], at=region)
    otok = sb("otok", [P, NT, BW], at=region)
    kout = sb("kout", [P, 2, BW], at=region)
    ck_in = sb("ck_in", [P, BW], at=region)
    ckT = sb("ckT", [P, BH, P], at=region)
    cv = sb("cv", [P, BW], at=region)
    pT = sb("pT", [P, 2, BW], at=region)
    lamv = sb("lamv", [P, 5, BD_], at=region)
    lam2 = sb("lam2", [P, 4], at=region)
    nlam = sb("nlam", [P, 1], at=region)
    amax = sb("amax", [P, 4], at=region)
    asum = sb("asum", [P, 4], at=region)
    arec = sb("arec", [P, 4], at=region)
    ossq = sb("ossq", [P, NT * BH], at=region)
    orms = sb("orms", [P, NT * BH], at=region)
    orst = sb("orst", [P, NT * BH], at=region)
    subln = sb("subln", [P, BV], at=region)
    probs = qkv[:, 8:12, :].rearrange("p a t -> p (a t)")[:, 0:4 * BW].rearrange("p (b n t) -> p b n t", b=2, n=2)
    region.close()
    AR = sb("AR", [P, CT, 2, J], at=region)
    bonus = sb("bonus", [P, CT, J], at=region)
    inner = ExitStack()
    tmp = sb("tmp", [P, 6, J], at=inner)
    inner.close()
    lt = sb("lt", [P, 4, 2 * P], at=inner)
    gt = sb("gt", [P, 4, 2 * P], at=inner)
    X = sb("X", [P, 4, P], at=inner)
    XT = sb("XT", [P, 4, P], at=inner)
    mc = sb("mc", [P, 4, 64], at=inner)
    ag = sb("ag", [P, 4, 2, 64], at=inner)
    wu = sb("wu", [P, 4, 2, 64], at=inner)
    tok = sb("tok", [P, 3, 4, 64], at=inner)
    ebd = sb("ebd", [P, 2, 2, P], at=inner)
    ff = sb("ff", [P, 2, 2, 64], at=inner)
    qT = sb("qT", [P, 2, P], at=inner)
    mt = sb("mt", [P, 2, 64], at=inner)
    mcur = sb("mcur", [P, 2, 2, 64], at=inner)
    mbd = sb("mbd", [P, 2, 3, 2, P], at=inner)
    sout = sb("sout", [P, 2, 64], at=inner)
    inner.close()
    sio = C[:, CWA, 0:4 * P].rearrange("p (c k) -> p c k", c=CT)
    mixt = sb("mixt", [P, TOK], at=inner)
    y_hi = sb("y_hi", [P, CT, TOK], F32R, at=inner)
    y_lo = sb("y_lo", [P, CT, TOK], F32R, at=inner)
    ga = sb("ga", [P, GA_RING, TOK], at=inner)
    inner.close()
    region.close()
    phase2.close()
    S = sb("S", [P, FT, 2, TOK], F32R)
    x1 = sb("x1", [P, NT, D])
    z = sb("z", [P, NT, D])
    zT = sb("zT", [P, TOK])
    gain2 = sb("gain2", [P, D])
    ftmp = z[:, :, :].rearrange("p t n -> p (t n)")
    f_t, f_s = ftmp[:, 0:TOK], ftmp[:, TOK:2 * TOK]

    dps = [ctx.enter_context(nc.psum_tensor(f"dense{i}", [P, 2, 512], F32)) for i in range(2)]
    side = [ctx.enter_context(nc.psum_tensor(f"side{i}", [P, 512], F32)) for i in range(4)]

    raw_loaded = [sem(f"raw_loaded{i}") for i in range(2)]
    hi_split, w_split = sem("hi_split"), sem("w_split")
    slot_ready = sem("slot_ready")
    seg_done = sem("seg_done")
    dense_read = [sem(f"dense_read{i}") for i in range(2)]
    filled = sem("filled")
    drained = [sem(f"drained{i}") for i in range(4)]
    vch, ach = sem("vector_chain"), sem("scalar_chain")
    stored = sem("stored")
    kout_stored = [sem(f"kout_stored{i}") for i in range(2)]
    names = """x_loaded0 x_loaded1 x_sq x_normed x_hi cst_loaded small_loaded att_loaded gain_loaded lam_prod lam_exp
        params_done smax sattn o_rms o_scaled o_hi_done last_done shifted lora_a lora_v ksq kmaxed ksqrt
        rw_g rw_p rw_gm rw_e2 rw_bo rw_done zeroed init_loaded xt_init x_upd st_bd
        y_sq y_hi_done y_done mixed mix_hi mix_done gain_used x1_loaded gain2_loaded zrms zres xrms xnorm z_hi
        f_tanh f_hi f_lo"""
    s_ = {n: sem(n) for n in names.split()}

    def bank(step, f):
        return side[FILL[(step, f)] % 4]

    def open_bank(pe, step, f):
        n = FILL[(step, f)]
        if n >= 4:
            pe.wait_ge(drained[n % 4], n // 4)
        return side[n % 4]

    def full_bank(eng, step, f):
        n = FILL[(step, f)]
        eng.wait_ge(filled, n + 1)
        return side[n % 4]

    def drain_sem(step, f):
        return drained[FILL[(step, f)] % 4]

    def landed(eng, step, f):
        n = FILL[(step, f)]
        eng.wait_ge(drained[n % 4], n // 4 + 1)

    def block_full(eng, d):
        eng.wait_ge(seg_done, BLOCK_END[d])
        return dps[BLOCK[d] % 2]

    def block_sem(d):
        return dense_read[BLOCK[d] % 2]

    def block_landed(eng, d):
        eng.wait_ge(dense_read[BLOCK[d] % 2], BLOCK[d] // 2 + 1)

    class Chain:
        def __init__(self, eng, s):
            self.eng, self.s, self.count = eng, s, {}

        def __call__(self, ins):
            self.mark(ins, self.s, "")

        def mark(self, ins, s, name):
            self.count[name] = self.count.get(name, 0) + 1
            ins.then_inc(s, 1)
            self.eng.wait_ge(s, self.count[name])

    def x_rows(t):
        return i_["x_prompt"][0, t * P:(t + 1) * P, :] if t < SAMPLE else i_["x_sample"][0, :, :]

    def y_rows(t):
        return o_["y_prompt"][0, t * P:(t + 1) * P, :] if t < SAMPLE else o_["y_sample"][0, :, :]

    w_in = i_["w_in"][0].rearrange("(k p) n -> p k n", p=P)
    w_oa = i_["w_out_a"][0].rearrange("(k p) n -> p k n", p=P)
    w_ob = i_["w_out_b"][0].rearrange("(k p) n -> p k n", p=P)
    w_o = i_["w_o"][0].rearrange("(k p) n -> p k n", p=P)
    w_fi = i_["w_ffn_in"][0].rearrange("(k p) n -> p k n", p=P)
    w_fo = i_["w_ffn_out"][0].rearrange("(k p) n -> p k n", p=P)
    COL0 = {"qkv": A_COLS, "gB": A_COLS + 3 * BW + D, "gA": A_COLS + 3 * BW}

    block = ctx.enter_context(nc.Block())

    def state_slot(t, c):
        return ((2 * t if t < SAMPLE else 9) + c) % 3

    def st_count(t, g):
        return 2 * (2 * t + g + 1) if t < SAMPLE else 4 * SAMPLE + 1 + g

    def chunks(t):
        return [(c, CHUNK) for c in range(2)] if t < SAMPLE else [(0, DEC)]

    def first(t):
        return TILES[t][0] if t < SAMPLE else JS

    N_SMALL, N_ATT = 16, 7

    @block.sync
    def _(sp):
        for u, (kind, n, part) in enumerate(UNITS):
            slot = u % 2
            if FFN_UNIT0 <= u < DOWN_UNIT0:
                if u == FFN_UNIT0:
                    with sp.Fori(0, FT) as f:
                        for k in range(2):
                            s2 = (FFN_UNIT0 + k) % 2
                            sp.wait_ge(w_split, f * 2 + (FFN_UNIT0 + k - 1))
                            sp.dma_start(w_raw[:, s2, :].rearrange("p (k n) -> p k n", k=KT),
                                         w_fi[:, :, bass.ds(f * P + k * D_FF, P)]).then_inc(raw_loaded[s2], 16)
                continue
            if u >= 2:
                sp.wait_ge(w_split, u - 1)
            dst = w_raw[:, slot, :]
            if kind in ("qkv", "gA", "gB", "c"):
                c0 = CCOL[n] if kind == "c" else COL0[kind] + n * P
                sp.dma_start(dst.rearrange("p (k n) -> p k n", k=KT), w_in[:, :, c0:c0 + P]).then_inc(raw_loaded[slot], 16)
            elif kind in ("outA", "outB"):
                w = w_oa if kind == "outA" else w_ob
                sp.dma_start(dst.rearrange("p (k n) -> p k n", k=CT), w[:, :, n * 256:(n + 1) * 256]).then_inc(
                    raw_loaded[slot], 16)
            elif kind == "wo":
                sp.dma_start(dst.rearrange("p (k n) -> p k n", k=KT), w_o[:, :, n * P:(n + 1) * P]).then_inc(
                    raw_loaded[slot], 16)
            else:
                k0, kn = DOWN_PARTS[part]
                sp.dma_start(dst[:, 0:kn * P].rearrange("p (k n) -> p k n", k=kn),
                             w_fo[:, k0:k0 + kn, n * P:(n + 1) * P]).then_inc(raw_loaded[slot], 16)

    @block.gpsimd
    def _(pool):
        def split(slot):
            nc.gpsimd.tensor_scalar(w_hi[:, slot, :], w_raw[:, slot, :], 1.0, 0.0, ALU.mult, ALU.add).then_inc(hi_split, 1)

        def split_lo(slot):
            nc.gpsimd.tensor_tensor(w_lo[:, slot, :], w_raw[:, slot, :], w_hi[:, slot, :].bitcast(F32),
                                    ALU.subtract).then_inc(w_split, 1)

        def unit(u):
            pool.wait_ge(raw_loaded[u % 2], 16 * (u // 2 + 1))
            if u >= 2:
                pool.wait_ge(seg_done, UNIT_END[u - 2])
            split(u % 2)
            pool.wait_ge(hi_split, u + 1)
            split_lo(u % 2)

        for u in range(FFN_UNIT0 + 2):
            unit(u)
        with pool.Fori(1, FT) as f:
            for k in range(2):
                u0 = FFN_UNIT0 + k
                pool.wait_ge(raw_loaded[u0 % 2], (f + (u0 // 2 + 1)) * 16)
                pool.wait_ge(seg_done, f * 2 + (FFN_SEG0 + k - 1))
                pool.sem_inc(slot_ready, 1)
                split(u0 % 2)
                pool.wait_ge(hi_split, f * 2 + (u0 + 1))
                split_lo(u0 % 2)
        for u in range(DOWN_UNIT0, len(UNITS)):
            unit(u)

    def ffn_mm(pe, three, b, u):
        for n in range(KT):
            ins = three(dps[b % 2], w_hi[:, u % 2, n * P:(n + 1) * P], w_lo[:, u % 2, n * P:(n + 1) * P],
                        h_hi[:, n, :], h_lo[:, n, :], n == 0, n == KT - 1)
        ins.then_inc(seg_done, 1)



    def wkv_pe(pe, step, transposes, close):
        t, g = step[2], step[3]
        n, j0 = TILES[t][1], first(t)
        heads = [(c, p) for c in range(2) for p in range(2)]
        if step[0] == "wl":
            lv = step[1]
            s = LEVELS[lv]
            nb = n // (2 * s)
            b = open_bank(pe, step, "m")
            landed(pe, ("w", "x0", t, g), "x")
            if lv:
                landed(pe, ("wl", lv - 1, t, g), "t")
            for h in range(4):
                rhs = X[0:n, h, 0:n].rearrange("p (b u s) -> p b u s", u=2, s=s)[:, :, 0, :]
                out = b[0:n, h * 64:h * 64 + n // 2].rearrange("p (b s) -> p b s", s=s)
                ins = pe.matmul(out, lt[0:n, h, 0:n], rhs, start=True, stop=True)
            close(ins, step, "m")
            b = open_bank(pe, step, "d")
            landed(pe, step, "m")
            for h in range(4):
                ins = pe.matmul(b[0:n, h * 64:h * 64 + n // 2], XT[0:n, h, 0:n], mc[0:n, h, 0:n // 2], start=True, stop=True)
            close(ins, step, "d")
            landed(pe, step, "d")
            transposes(step, "t", [(h * n, X[0:n, h, 0:n]) for h in range(4)])
            return
        st = step[1]
        if st == "tok":
            if (t, g) == (0, 0):
                pe.wait_ge(s_["rw_done"], CT)
            transposes(step, "t0", [((2 * q + c) * P, C[:, blk + 2 * g + c, 1 + j0:1 + j0 + n])
                                    for q, blk in enumerate((CR, CK)) for c in range(2)])
            transposes(step, "t1", [(c * P, C[:, CV + 2 * g + c, 1 + j0:1 + j0 + n]) for c in range(2)]
                       + [((2 + c) * P, AR[:, 2 * g + c, 0, j0:j0 + n]) for c in range(2)])
        elif st == "scores":
            for f, blk in (("b", CR), ("k", CK)):
                for p in range(2):
                    b = open_bank(pe, step, f"{f}{p}")
                    lo, hi = 64 * p, 64 * p + 64
                    for c in range(2):
                        ins = pe.matmul(b[0:n, c * 2 * n:(c + 1) * 2 * n].rearrange("p (u i) -> p u i", u=2),
                                        C[lo:hi, blk + 2 * g + c, 1 + j0:1 + j0 + n], AR[lo:hi, 2 * g + c, :, j0:j0 + n],
                                        start=True, stop=True)
                    close(ins, step, f"{f}{p}")
        elif st == "gv":
            b = open_bank(pe, step, "gv")
            landed(pe, ("w", "tok", t, g), "t1")
            landed(pe, ("w", "scores", t, g), "k0")
            landed(pe, ("w", "scores", t, g), "k1")
            for h in range(4):
                ins = pe.matmul(b[0:n, h * 64:(h + 1) * 64], gt[0:n, h, 0:n], tok[0:n, 2, h, :], start=True, stop=True)
            close(ins, step, "gv")
        elif st == "x0":
            pe.wait_ge(s_["xt_init"], 2 * t + g + 1)
            transposes(step, "x", [(h * n, XT[0:n, h, 0:n]) for h in range(4)])
        elif st == "wu":
            b = open_bank(pe, step, "wu")
            landed(pe, ("wl", levels(t)[-1], t, g), "t")
            landed(pe, ("w", "gv", t, g), "gv")
            for h in range(4):
                ins = pe.matmul(b[0:n, h * P:(h + 1) * P], XT[0:n, h, 0:n],
                                ag[0:n, h, :, :].rearrange("p u v -> p (u v)"), start=True, stop=True)
            close(ins, step, "wu")
        elif st == "ef":
            landed(pe, ("w", "wu", t, g), "wu")
            landed(pe, ("w", "tok", t, g), "t0")
            for ch, ln in chunks(t):
                b = open_bank(pe, step, f"e{ch}")
                r0, r1 = 64 * ch, 64 * ch + ln
                for c, p in heads:
                    h = 2 * c + p
                    out = b[64 * p:64 * p + 64, c * P:(c + 1) * P]
                    pe.matmul(out[:, 0:64], wu[r0:r1, h, 0, :], tok[r0:r1, 0, h, :], start=True, stop=True)
                    pe.matmul(out[:, 64:P], tok[r0:r1, 0, h, :], wu[r0:r1, h, 1, :], start=True, stop=False)
                    ins = pe.matmul(out[:, 64:P], tok[r0:r1, 1, h, :], tok[r0:r1, 2, h, :], start=False, stop=True)
                close(ins, step, f"e{ch}")
        elif st == "chain":
            for ch, ln in chunks(t):
                b = open_bank(pe, step, f"c{ch}")
                landed(pe, ("w", "ef", t, g), f"e{ch}")
                if t == SAMPLE:
                    landed(pe, ("init",), "s")
                elif (t, ch) == (0, 0):
                    pe.wait_ge(s_["zeroed"], 1)
                else:
                    pe.wait_ge(s_["st_bd"], st_count(t, g) - 1 if ch else st_count(t - 1, g))
                for c in range(2):
                    ins = pe.matmul(b[:, c * 64:(c + 1) * 64], ebd[:, ch, c, :], mcur[:, g, c, :], start=True, stop=True)
                close(ins, step, f"c{ch}")
        elif st == "q":
            b = open_bank(pe, step, "q")
            for p in range(2):
                landed(pe, ("w", "scores", t, g), f"b{p}")
            for c, p in heads:
                h = 2 * c + p
                ins = pe.matmul(b[64 * p:64 * p + 64, c * n:(c + 1) * n], wu[0:n, h, 0, :], lt[0:n, h, P:P + n],
                                start=True, stop=True)
            close(ins, step, "q")
        elif st == "y":
            b = open_bank(pe, step, "y")
            landed(pe, ("w", "q", t, g), "q")
            for c in range(2):
                for p in range(2):
                    h = 2 * c + p
                    out = b[64 * p:64 * p + 64, c * n:(c + 1) * n]
                    pe.matmul(out, wu[0:n, h, 1, :], lt[0:n, h, P:P + n], start=True, stop=False)
                    pe.matmul(out, tok[0:n, 2, h, :], gt[0:n, h, P:P + n], start=False, stop=True)
                for ch, ln in chunks(t):
                    if ch:
                        pe.wait_ge(s_["st_bd"], st_count(t, g) - 1)
                    ins = pe.matmul(b[:, c * n + 64 * ch:c * n + 64 * ch + ln], mbd[:, g, state_slot(t, ch), c, :],
                                    qT[:, c, 64 * ch:64 * ch + ln], start=False, stop=True, skip_group_check=True)
            close(ins, step, "y")

    @block.tensor
    def _(pe):
        count = [0]

        def close(ins, step, f):
            assert FILL[(step, f)] == count[0], (step, f)
            count[0] += 1
            ins.then_inc(filled, 1)

        def three(acc, whi, wlo, rhi, rlo, first, final):
            for n, (w, r) in enumerate(((whi, rhi), (whi, rlo), (wlo, rhi))):
                for hf in range(2):
                    ins = pe.matmul(acc[:, hf, 0:HALF], w, r[:, hf * HALF:(hf + 1) * HALF],
                                    start=first and n == 0, stop=final and n == 2)
            return ins

        def dense(kind, i):
            d = (kind, i)
            b = BLOCK[d]
            if kind in ("qkv", "c") and b == 0:
                landed(pe, ("norm", SAMPLE), "n1")
            if kind == "outB":
                landed(pe, ("ofin", SAMPLE), "o")
            if kind == "outA":
                pe.wait_ge(s_["y_done"], 2 * CT)
            if kind == "wo":
                pe.wait_ge(s_["mix_done"], 8)
            if kind == "down":
                pe.wait_ge(s_["f_lo"], FT)
            if b >= 2:
                pe.wait_ge(dense_read[b % 2], b // 2)
            acc = dps[b % 2]
            parts = UNIT_OF[d]
            for p, (u, seg) in enumerate(parts):
                pe.wait_ge(w_split, u + 1)
                if kind in ("outA", "outB"):
                    hi, lo = (y_hi, y_lo) if kind == "outA" else (o_hi, o_lo)
                    ops = [(k * 256 + (i % 2) * P, hi[:, k, :], lo[:, k, :]) for k in range(CT)]
                elif kind == "wo":
                    ops = [(k * P, S[:, k, 0, :], S[:, k, 1, :]) for k in range(KT)]
                elif kind == "down":
                    k0, kn = DOWN_PARTS[p]
                    ops = [(k * P, S[:, k0 + k, 0, :], S[:, k0 + k, 1, :]) for k in range(kn)]
                else:
                    ops = [(k * P, h_hi[:, k, :], h_lo[:, k, :]) for k in range(KT)]
                for n, (c, rh, rl) in enumerate(ops):
                    ins = three(acc, w_hi[:, u % 2, c:c + P], w_lo[:, u % 2, c:c + P], rh, rl,
                                p == 0 and n == 0, p == len(parts) - 1 and n == len(ops) - 1)
                ins.then_inc(seg_done, 1)

        def transposes(step, f, pieces):
            b = open_bank(pe, step, f)
            for c0, src in pieces:
                n, m = src.shape[0], src.shape[1]
                ins = pe.transpose(b[0:m, c0:c0 + n], src, ident[0:n, 0:n])
            close(ins, step, f)

        for step in SCHEDULE:
            k = step[0]
            if k == "dense":
                dense(*step[1:])
            elif k == "params":
                pe.wait_ge(s_["cst_loaded"], 32)
                pe.wait_ge(s_["small_loaded"], 16 * N_SMALL)
                transposes(step, "pv", [(0, pv_rows[:, :])])
            elif k == "norm":
                t = step[1]
                n = TILES[t][1]
                pe.wait_ge(s_["x_normed"], t + 1)
                for i in range(2):
                    transposes(step, f"n{i}", [(kk * n, xn[0:n, t % 2, (4 * i + kk) * P:(4 * i + kk + 1) * P])
                                               for kk in range(4)])
            elif k == "cache":
                pe.wait_ge(s_["att_loaded"], 16 * N_ATT)
                transposes(step, "ck", [(h * P, ck_in[:, h * P:(h + 1) * P]) for h in range(BH)])
            elif k == "kvtok":
                t0, n = TILES[step[1]]
                block_landed(pe, ("qkv", 11))
                if step[1] == 0:
                    block_landed(pe, ("qkv", 10))
                for f, b0 in (("k", 4), ("v", 8)):
                    transposes(step, f, [(h * P, qkv[:, b0 + h, t0:t0 + n]) for h in range(BH)])
            elif k == "att":
                _, t, h = step
                t0, n = TILES[t]
                keys = t0 + n if t < SAMPLE else PAST + DEC
                if t == SAMPLE and h == 0:
                    landed(pe, ("cache",), "ck")
                for m in range(2):
                    b = open_bank(pe, step, f"s{m}")
                    lo, hi = 64 * m, 64 * m + 64
                    q = qkv[lo:hi, h, t0:t0 + n]
                    if t < SAMPLE:
                        ins = pe.matmul(b[0:n, 0:keys], q, qkv[lo:hi, 4 + h, 0:keys], start=True, stop=True)
                    else:
                        pe.matmul(b[0:n, 0:PAST], q, ckT[lo:hi, h, :], start=True, stop=True)
                        ins = pe.matmul(b[0:n, PAST:keys], q, qkv[lo:hi, 4 + h, t0:t0 + n], start=True, stop=True)
                    close(ins, step, f"s{m}")
                pb = (t * BH + h) % 2
                pe.wait_ge(s_["sattn"], t * BH + h + 1)
                kts = [(kt * P, P) for kt in range(t + 1)] if t < SAMPLE else [(0, PAST), (PAST, DEC)]
                transposes(step, "pt", [(i * n, probs[0:n, pb, 0, c0:c0 + kn]) for i, (c0, kn) in enumerate(kts)])
                b = open_bank(pe, step, "o")
                landed(pe, step, "pt")
                if h == 0:
                    landed(pe, ("kvtok", t), "v")
                for i, (c0, kn) in enumerate(kts):
                    if t < SAMPLE:
                        v = vtok[0:P, i, h * BV:(h + 1) * BV]
                    else:
                        v = cv[:, h * BV:(h + 1) * BV] if i == 0 else vtok[0:DEC, SAMPLE, h * BV:(h + 1) * BV]
                    ins = pe.matmul(b[0:n, 0:BV], pT[0:kn, pb, i * n:(i + 1) * n], v,
                                    start=i == 0, stop=i == len(kts) - 1)
                close(ins, step, "o")
            elif k == "ofin":
                t0, n = TILES[step[1]]
                pe.wait_ge(s_["o_scaled"], step[1] + 1)
                transposes(step, "o", [(h * n, otok[0:n, step[1], h * BV:(h + 1) * BV]) for h in range(BH)])
            elif k == "shiftout":
                pe.wait_ge(s_["last_done"], 1)
                transposes(step, "s", [(0, last[:, :, :].rearrange("p g c -> p (g c)"))])
            elif k == "knorm":
                c = step[1]
                pe.wait_ge(s_["ksq"], c + 1)
                for i, (a, b_) in enumerate(((0, HALF), (HALF, J))):
                    b = open_bank(pe, step, f"q{i}")
                    close(pe.matmul(b[:, 0:b_ - a], cst[:, K_BD:K_BD + P], AR[:, c, 0, a:b_], start=True, stop=True),
                          step, f"q{i}")
            elif k == "rw1":
                c = step[1]
                if c == 0:
                    pe.wait_ge(s_["lora_a"], 1)
                for f, lo in (("w", 0), ("a", 64)):
                    for i, (a, b_) in enumerate(((0, HALF), (HALF, J))):
                        b = open_bank(pe, step, f"{f}{i}")
                        close(pe.matmul(b[:, 0:b_ - a], wa2[lo:lo + 64, c * P:(c + 1) * P],
                                        C[lo:lo + 64, CWA, 1 + a:1 + b_], start=True, stop=True), step, f"{f}{i}")
            elif k == "rw2":
                c = step[1]
                pe.wait_ge(s_["rw_bo"], c + 1)
                for i, (a, b_) in enumerate(((0, HALF), (HALF, J))):
                    b = open_bank(pe, step, f"b{i}")
                    close(pe.matmul(b[:, 0:b_ - a], cst[:, K_BD:K_BD + P], tmp[:, 5, a:b_], start=True, stop=True),
                          step, f"b{i}")
            elif k == "init":
                pe.wait_ge(s_["init_loaded"], 32)
                transposes(step, "s", [(c * P, sio[:, c, :]) for c in range(CT)])
            elif k in ("w", "wl"):
                wkv_pe(pe, step, transposes, close)
            elif k == "final":
                _, t, g = step
                pe.wait_ge(s_["st_bd"], st_count(t, g))
                slot = state_slot(t, 2 if t < SAMPLE else 1)
                transposes(step, "f", [(c * P, mbd[:, g, slot, c, :]) for c in range(2)])
            elif k in ("ymean", "yvar"):
                c = step[1]
                if k == "ymean":
                    landed(pe, ("w", "y", SAMPLE, 1), "y")
                    src = AR[:, c, 1, :]
                else:
                    pe.wait_ge(s_["y_sq"], c + 1)
                    src = AR[:, c, 0, :]
                for i, (a, b_) in enumerate(((0, HALF), (HALF, J))):
                    b = open_bank(pe, step, f"m{i}")
                    close(pe.matmul(b[:, 0:b_ - a], cst[:, K_BD:K_BD + P], src[:, a:b_], start=True, stop=True),
                          step, f"m{i}")
            elif k == "yfin":
                c = step[1]
                for i, (a, b_) in enumerate(((0, HALF), (HALF, J))):
                    b = open_bank(pe, step, f"g{i}")
                    pe.matmul(b[:, 0:b_ - a], g2a[:, c * P:(c + 1) * P], C[:, CG, 1 + a:1 + b_], start=True, stop=False)
                    close(pe.matmul(b[:, 0:b_ - a], g2b[G2P:P, c * P:(c + 1) * P], C[G2P:P, CG2, 1 + a:1 + b_],
                                    start=False, stop=True), step, f"g{i}")
            elif k == "ztok":
                _, r, i = step
                block_landed(pe, ("wo" if r == 0 else "down", i))
                transposes(step, "z0", [(t * P, zT[:, t * P:(t + 1) * P]) for t in range(4)])
                transposes(step, "z1", [(0, zT[:, SEQ:TOK])])
            elif k == "zpost" and step[1] == 0:
                for t, (t0, n) in enumerate(TILES):
                    pe.wait_ge(s_["xnorm"], t + 1)
                    for i in range(2):
                        transposes(step, f"n{t}{i}", [(kk * n, z[0:n, t, (4 * i + kk) * P:(4 * i + kk + 1) * P])
                                                      for kk in range(4)])
            elif k == "ffn":
                landed(pe, ("zpost", 0), f"n{SAMPLE}1")
                for j in (0,):
                    for kk in range(2):
                        b = FFN_BLOCK0 + kk
                        pe.wait_ge(dense_read[b % 2], b // 2)
                        pe.wait_ge(w_split, FFN_UNIT0 + kk + 1)
                        ffn_mm(pe, three, b, FFN_UNIT0 + kk)
                with pe.Fori(1, FT) as f:
                    for kk in range(2):
                        b = FFN_BLOCK0 + kk
                        pe.wait_ge(dense_read[b % 2], f + b // 2)
                        pe.wait_ge(w_split, f * 2 + (FFN_UNIT0 + kk + 1))
                        ffn_mm(pe, three, b, FFN_UNIT0 + kk)

    @block.scalar
    def _(act):
        A = Chain(act, ach)
        n_stored = [0]
        f_act = nc.scalar.activation

        def store(dst, src):
            act.dma_start(dst, src).then_inc(stored, 16)
            n_stored[0] += 1

        def drain(ins, step, f):
            ins.then_inc(drain_sem(step, f), 1)

        def halves(hi, step, f, t0, n, name, k0):
            b = full_bank(act, step, f)
            f_act(hi[:, k0:k0 + 4, t0:t0 + n], b[:, 0:4 * n].rearrange("p (k n) -> p k n", k=4), ACT.Copy).then_inc(
                s_[name], 1)

        def load_x(t):
            act.dma_start(xs[0:TILES[t][1], t % 2, :], x_rows(t)).then_inc(s_[f"x_loaded{t % 2}"], 16)

        def rows(ap2, r0, n):
            act.dma_start(pv_rows[r0:r0 + n, :], ap2).then_inc(s_["small_loaded"], 16)

        load_x(0)
        load_x(1)
        act.dma_start(gain[:, :], i_["norm_mix_pre"][0].partition_broadcast(P)).then_inc(s_["gain_loaded"], 16)
        act.dma_start(ident[:, :], i_["cst"][:, K_ID:K_ID + P]).then_inc(s_["cst_loaded"], 16)
        act.dma_start(cst[:, :], i_["cst"][:, :]).then_inc(s_["cst_loaded"], 16)
        for ap1, r0 in ((i_["state_shift"][0, 0, 0], PV_SHIFT), (i_["rwkv_mu"][0], PV_MU)):
            rows(ap1[0:14 * P].rearrange("(r c) -> r c", c=P), r0, 14)
            rows(ap1[A_COLS - P:A_COLS].rearrange("(r c) -> r c", c=P), r0 + 14, 1)
        for name, r0, n in (("rwkv_w0", PV_W0, 4), ("rwkv_a0", PV_A0, 4), ("rwkv_k_k", PV_KK, 4), ("rwkv_k_a", PV_KA, 4),
                            ("rwkv_ln_w", PV_LNW, 4), ("rwkv_ln_b", PV_LNB, 4), ("b_gate", PV_BG, 16)):
            rows(i_[name][0].rearrange("(r c) -> r c", c=P), r0, n)
        rows(i_["rwkv_r_k"][0].rearrange("(r a) c -> r (a c)", a=2), PV_RK, 4)
        act.dma_start(wa2[0:64, :], i_["rwkv_w2"][0]).then_inc(s_["small_loaded"], 16)
        act.dma_start(wa2[64:P, :], i_["rwkv_a2"][0]).then_inc(s_["small_loaded"], 16)
        act.dma_start(g2a[:, :], i_["rwkv_g2"][0, 0:P, :]).then_inc(s_["small_loaded"], 16)
        act.dma_start(g2b[G2P:P, :], i_["rwkv_g2"][0, P:GATE_LORA, :]).then_inc(s_["small_loaded"], 16)
        act.dma_start(ck_in[:, :], i_["cache_k"][0, 0].rearrange("t h n d -> t (h n d)")).then_inc(s_["att_loaded"], 16)
        act.dma_start(cv[:, :], i_["cache_v"][0, 0].rearrange("t h e -> t (h e)")).then_inc(s_["att_loaded"], 16)
        for n, name in enumerate(("diff_lq1", "diff_lk1", "diff_lq2", "diff_lk2")):
            act.dma_start(lamv[:, n, :], i_[name][0].partition_broadcast(P)).then_inc(s_["att_loaded"], 16)
        act.dma_start(subln[:, :], i_["diff_subln"][0].partition_broadcast(P)).then_inc(s_["att_loaded"], 16)

        for step in SCHEDULE:
            k = step[0]
            if k == "params":
                b = full_bank(act, step, "pv")
                A(f_act(pvh[:, :], b[:, 0:PV_N], ACT.Copy, scale=0.5))
                drain(f_act(pv[:, :], b[:, 0:PV_N], ACT.Copy), step, "pv")
            elif k == "norm":
                t = step[1]
                t0, n = TILES[t]
                act.wait_ge(s_[f"x_loaded{t % 2}"], 16 * (t // 2 + 1))
                A(f_act(xn[0:n, t % 2, :], xs[0:n, t % 2, :], ACT.Square, accum_out=ssq[0:n, t:t + 1]))
                A.mark(f_act(rms[0:n, t:t + 1], ssq[0:n, t:t + 1], ACT.Sqrt, scale=1.0 / D, bias=EPS), s_["x_sq"], "x_sq")
                for i in range(2):
                    halves(h_hi, step, f"n{i}", t0, n, "x_hi", 4 * i)
                if t + 2 < NT:
                    load_x(t + 2)
            elif k == "cache":
                act.wait_ge(s_["lam_prod"], 2)
                A.mark(f_act(lam2[:, 2:4], lam2[:, 0:2], ACT.Exp), s_["lam_exp"], "lam_exp")
                b = full_bank(act, step, "ck")
                drain(f_act(ckT[:, :, :], b[:, 0:BW].rearrange("p (h t) -> p h t", h=BH), ACT.Copy), step, "ck")
            elif k == "kvtok":
                t = step[1]
                t0, n = TILES[t]
                if t >= 2:
                    act.wait_ge(kout_stored[t % 2], 16 * (t // 2))
                b = full_bank(act, step, "k")
                drain(f_act(kout[0:n, t % 2, :], b[0:n, 0:BW], ACT.Copy), step, "k")
                landed(act, step, "k")
                kd, vd = (o_["k_prompt"], o_["v_prompt"]) if t < SAMPLE else (o_["k_sample"], o_["v_sample"])
                r0 = t0 if t < SAMPLE else 0
                act.dma_start(kd[0, 0, r0:r0 + n].rearrange("t h n d -> t (h n d)"), kout[0:n, t % 2, :]).then_inc(
                    kout_stored[t % 2], 16)
                landed(act, step, "v")
                store(vd[0, 0, r0:r0 + n].rearrange("t h e -> t (h e)"), vtok[0:n, t, :])
            elif k == "att":
                _, t, h = step
                t0, n = TILES[t]
                idx = t * BH + h
                pb = idx % 2
                keys = t0 + n if t < SAMPLE else PAST + DEC
                for m in range(2):
                    b = full_bank(act, step, f"s{m}")
                    act.wait_ge(s_["smax"], 2 * idx + m + 1)
                    drain(f_act(probs[0:n, pb, m, 0:keys], b[0:n, 0:keys], ACT.Exp, bias=amax[0:n, 2 * pb + m:2 * pb + m + 1],
                                scale=SCALE, accum_out=asum[0:n, 2 * pb + m:2 * pb + m + 1]), step, f"s{m}")
                b = full_bank(act, step, "pt")
                if t < SAMPLE:
                    drain(f_act(pT[:, pb, 0:(t + 1) * n], b[:, 0:(t + 1) * n], ACT.Copy), step, "pt")
                else:
                    f_act(pT[:, pb, 0:n], b[:, 0:n], ACT.Copy).then_inc(ach, 1)
                    A.count[""] = A.count.get("", 0) + 1
                    drain(f_act(pT[0:DEC, pb, n:2 * n], b[0:DEC, n:2 * n], ACT.Copy), step, "pt")
                b = full_bank(act, step, "o")
                A(f_act(otok[0:n, t, h * BV:(h + 1) * BV], b[0:n, 0:BV], ACT.Copy))
                drain(f_act(b[0:n, 0:BV], b[0:n, 0:BV], ACT.Square, accum_out=ossq[0:n, idx:idx + 1]), step, "o")
            elif k == "oscale":
                landed(act, ("att", SAMPLE, BH - 1), "o")
                A.mark(f_act(orms[:, 0:SAMPLE * BH], ossq[:, 0:SAMPLE * BH], ACT.Sqrt, scale=1.0 / BV, bias=EPS),
                       s_["o_rms"], "o_rms")
                A.mark(f_act(orms[0:DEC, SAMPLE * BH:], ossq[0:DEC, SAMPLE * BH:], ACT.Sqrt, scale=1.0 / BV, bias=EPS),
                       s_["o_rms"], "o_rms")
            elif k == "ofin":
                halves(o_hi, step, "o", *TILES[step[1]], "o_hi_done", 0)
            elif k == "shiftout":
                b = full_bank(act, step, "s")
                drain(f_act(lastT[:, :], b[0:2 * NC, 0:P], ACT.Copy), step, "s")
                landed(act, step, "s")
                for g, name in enumerate(("shift_prompt", "shift_sample")):
                    dst = o_[name][0, 0, 0]
                    store(dst[0:14 * P].rearrange("(r c) -> r c", c=P), lastT[g * NC:g * NC + 14, :])
                    store(dst[14 * P:A_COLS].rearrange("(r c) -> r c", c=A_COLS - 14 * P), lastT[g * NC + 14:g * NC + 15, G2P:P])
            elif k == "lora":
                act.wait_ge(s_["shifted"], NC)
                A(f_act(C[0:64, CWA, 1:1 + J], C[0:64, CWA, 1:1 + J], ACT.Tanh))
                A(f_act(C[:, CG, 1:1 + J], C[:, CG, 1:1 + J], ACT.Tanh, scale=0.5))
                A.mark(f_act(C[G2P:P, CG2, 1:1 + J], C[G2P:P, CG2, 1:1 + J], ACT.Tanh, scale=0.5), s_["lora_a"], "lora_a")
            elif k == "krsqrt":
                act.wait_ge(s_["kmaxed"], CT)
                for c in range(CT):
                    A.mark(f_act(AR[:, c, 0, :], AR[:, c, 0, :], ACT.Sqrt), s_["ksqrt"], "ksqrt")
            elif k == "rw1":
                c = step[1]
                if c:
                    act.wait_ge(s_["rw_done"], c)
                for f, s, col in (("w", 0, PV_W0), ("a", 1, PV_A0)):
                    for i, (a, b_) in enumerate(((0, HALF), (HALF, J))):
                        b = full_bank(act, step, f"{f}{i}")
                        drain(f_act(tmp[:, s, a:b_], b[:, 0:b_ - a], ACT.Tanh, scale=0.5, bias=pvh[:, col + c:col + c + 1]),
                              step, f"{f}{i}")
                act.wait_ge(s_["rw_g"], c + 1)
                A.mark(f_act(tmp[:, 3, :], tmp[:, 2, :], ACT.Exp), s_["rw_p"], "rw_p")
                act.wait_ge(s_["rw_gm"], c + 1)
                A(f_act(tmp[:, 0, :], tmp[:, 0, :], ACT.Exp))
                A.mark(f_act(tmp[:, 2, :], tmp[:, 2, :], ACT.Exp, scale=-1.0), s_["rw_e2"], "rw_e2")
            elif k == "init0":
                act.wait_ge(s_["zeroed"], 1)
                src = i_["state_wkv"][0, 0].rearrange("(c p) v k -> p v c k", p=2)
                for p in range(2):
                    act.dma_start(sio[64 * p:64 * p + 64, :, 64 * p:64 * p + 64], src[p]).then_inc(s_["init_loaded"], 16)
            elif k == "w":
                _, st, t, g = step
                n, j0 = TILES[t][1], first(t)
                if st == "tok":
                    b = full_bank(act, step, "t0")
                    drain(f_act(tok[0:n, 0:2, :, :].rearrange("p q h v -> p (q h v)"), b[0:n, 0:512], ACT.Copy), step, "t0")
                    b = full_bank(act, step, "t1")
                    A(f_act(tok[0:n, 2, :, :].rearrange("p h v -> p (h v)"), b[0:n, 0:256], ACT.Copy))
                    drain(f_act(ag[0:n, :, 0, :], b[0:n, 256:512].rearrange("p (h v) -> p h v", h=4), ACT.Copy), step, "t1")
                elif st == "gv":
                    b = full_bank(act, step, "gv")
                    drain(f_act(ag[0:n, :, 1, :], b[0:n, 0:256].rearrange("p (h v) -> p h v", h=4), ACT.Copy), step, "gv")
                elif st == "x0":
                    b = full_bank(act, step, "x")
                    drain(f_act(X[0:n, :, 0:n], b[0:n, 0:4 * n].rearrange("p (h i) -> p h i", h=4), ACT.Copy), step, "x")
                elif st == "wu":
                    b = full_bank(act, step, "wu")
                    drain(f_act(wu[0:n, :, :, :].rearrange("p h u v -> p (h u v)"), b[0:n, 0:512], ACT.Copy, scale=-1.0),
                          step, "wu")
                elif st == "y":
                    b = full_bank(act, step, "y")
                    drain(f_act(AR[:, 2 * g:2 * g + 2, 1, j0:j0 + n], b[:, 0:2 * n].rearrange("p (c i) -> p c i", c=2),
                                ACT.Copy), step, "y")
            elif k == "wl":
                t = step[2]
                n = TILES[t][1]
                b = full_bank(act, step, "t")
                drain(f_act(XT[0:n, :, 0:n], b[0:n, 0:4 * n].rearrange("p (h i) -> p h i", h=4), ACT.Copy), step, "t")
            elif k == "final":
                _, t, g = step
                b = full_bank(act, step, "f")
                act.wait_ge(stored, 16 * n_stored[0])
                bv = b[:, 0:2 * P].rearrange("p (c k) -> p c k", c=2)
                A(f_act(sout[0:64, :, :], bv[0:64, :, 0:64], ACT.Copy))
                drain(f_act(sout[64:P, :, :], bv[64:P, :, 64:P], ACT.Copy), step, "f")
                landed(act, step, "f")
                store(o_["wkv_prompt" if t < SAMPLE else "wkv_sample"][0, 0, 4 * g:4 * g + 4].rearrange(
                    "(c p) v k -> (p v) c k", p=2), sout[:, :, :])
            elif k == "yvar":
                c = step[1]
                for i, (a, b_) in enumerate(((0, HALF), (HALF, J))):
                    b = full_bank(act, step, f"m{i}")
                    drain(f_act(AR[:, c, 0, a:b_], b[:, 0:b_ - a], ACT.Sqrt, scale=1.0 / AD, bias=GN_EPS), step, f"m{i}")
            elif k == "yfin":
                c = step[1]
                landed(act, step, "g1")
                A.mark(f_act(y_hi[:, c, 0:SEQ], AR[:, c, 1, 0:SEQ], ACT.Copy), s_["y_hi_done"], "y_hi_done")
                A.mark(f_act(y_hi[:, c, SEQ:TOK], AR[:, c, 1, JS:J], ACT.Copy), s_["y_hi_done"], "y_hi_done")
            elif k == "zpost":
                r = step[1]
                last_ = ("ztok", r, 7)
                landed(act, last_, "z0")
                landed(act, last_, "z1")
                for t, (t0, n) in enumerate(TILES):
                    A(f_act(dps[0][0:n, :, :], z[0:n, t, :].rearrange("p (a b) -> p a b", a=2), ACT.Square,
                            accum_out=ssq[0:n, t:t + 1]))
                    A.mark(f_act(rms[0:n, t:t + 1], ssq[0:n, t:t + 1], ACT.Sqrt, scale=1.0 / D, bias=EPS), s_["zrms"], "zrms")
                if r == 0:
                    for t, (t0, n) in enumerate(TILES):
                        act.wait_ge(s_["zres"], t + 1)
                        A(f_act(dps[0][0:n, :, :], x1[0:n, t, :].rearrange("p (a b) -> p a b", a=2), ACT.Square,
                                accum_out=ssq[0:n, t:t + 1]))
                        A.mark(f_act(rms[0:n, t:t + 1], ssq[0:n, t:t + 1], ACT.Sqrt, scale=1.0 / D, bias=EPS),
                               s_["xrms"], "xrms")
                    act.wait_ge(s_["zres"], NT)
                    act.dma_start(gain[:, :], i_["norm_ffn_post"][0].partition_broadcast(P)).then_inc(s_["gain_loaded"], 16)
                    for t, (t0, n) in enumerate(TILES):
                        for i in range(2):
                            halves(h_hi, step, f"n{t}{i}", t0, n, "z_hi", 4 * i)
                else:
                    for t in range(NT):
                        act.wait_ge(s_["zres"], NT + t + 1)
                        store(y_rows(t), z[0:TILES[t][1], t, :])
            elif k == "ffn":
                pa, pb_ = dps[FFN_BLOCK0 % 2], dps[(FFN_BLOCK0 + 1) % 2]

                def pair(j, before):
                    act.wait_ge(seg_done, j * 2 + (FFN_SEG0 + 1))
                    if before:
                        act.wait_ge(dense_read[FFN_BLOCK0 % 2], j + FFN_BLOCK0 // 2)
                    f_act(f_t.rearrange("p (a b) -> p a b", a=2), pa[:, :, 0:HALF], ACT.Tanh, scale=0.5).then_inc(
                        s_["f_tanh"], 1)
                    act.wait_ge(dense_read[(FFN_BLOCK0 + 1) % 2], j + ((FFN_BLOCK0 + 1) // 2 + 1))
                    dst = S[:, bass.ds(j, 1), 0, :] if before else S[:, 0:1, 0, :]
                    f_act(dst, f_s.unsqueeze(1), ACT.Copy, scale=0.5).then_inc(s_["f_hi"], 1)

                pair(0, False)
                with act.Fori(1, FT) as j:
                    pair(j, True)
            elif k == "dense":
                _, kind, i = step
                d = (kind, i)
                if kind in ("outA", "outB"):
                    if kind == "outA":
                        act.wait_ge(s_["mixed"], i + 1)
                        f_act(S[:, i, 0, :], mixt[:, :], ACT.Copy, scale=0.5).then_inc(s_["mix_hi"], 1)
                    continue
                acc = block_full(act, d)
                if kind == "qkv":
                    f_act(qkv[:, i, :].rearrange("p (a b) -> p a b", a=2), acc[:, :, 0:HALF], ACT.Copy).then_inc(
                        block_sem(d), 1)
                elif kind == "c":
                    f_act(C[:, i, 1:1 + HALF], acc[:, 0, 0:HALF], ACT.Copy)
                    f_act(C[:, i, 1 + HALF:1 + SEQ], acc[:, 1, 0:SEQ - HALF], ACT.Copy)
                    f_act(C[:, i, 1 + JS:1 + J], acc[:, 1, SEQ - HALF:HALF], ACT.Copy).then_inc(block_sem(d), 1)
                elif kind in ("gA", "gB"):
                    col = PV_BG + i + (KT if kind == "gB" else 0)
                    if kind == "gA" and i >= GA_RING:
                        block_landed(act, ("outA", i - GA_RING))
                    if d == ("gA", 0):
                        act.wait_ge(stored, 16 * n_stored[0])
                        landed(act, ("w", "y", SAMPLE, 1), "y")
                    if d == ("gB", 0):
                        pass
                    dst = (mb[:, i, :] if kind == "gB" else ga[:, i % GA_RING, :]).rearrange("p (a b) -> p a b", a=2)
                    f_act(dst, acc[:, :, 0:HALF], ACT.Tanh, scale=0.5, bias=pvh[:, col:col + 1]).then_inc(block_sem(d), 1)
                elif kind in ("wo", "down"):
                    if d == ("wo", 0):
                        act.wait_ge(s_["mix_done"], 8)
                        for t in range(NT):
                            act.dma_start(x1[0:TILES[t][1], t, :], x_rows(t)).then_inc(s_["x1_loaded"], 16)
                        act.dma_start(gain[:, :], i_["norm_mix_post"][0].partition_broadcast(P)).then_inc(
                            s_["gain_loaded"], 16)
                        act.dma_start(gain2[:, :], i_["norm_ffn_pre"][0].partition_broadcast(P)).then_inc(
                            s_["gain2_loaded"], 16)
                    if i:
                        full_bank(act, ("ztok", int(kind == "down"), i - 1), "z1")
                    f_act(zT[:, :].rearrange("p (a b) -> p a b", a=2), acc[:, :, 0:HALF], ACT.Copy).then_inc(block_sem(d), 1)
        act.wait_ge(stored, 16 * n_stored[0])
        act.wait_ge(kout_stored[0], 16 * 3)
        act.wait_ge(kout_stored[1], 16 * 2)

    @block.vector
    def _(dve):
        V = Chain(dve, vch)
        vec = nc.vector

        def drain(ins, step, f):
            ins.then_inc(drain_sem(step, f), 1)
            landed(dve, step, f)

        def low(hi, lo, step, f, t0, n, name, count, k0):
            b = full_bank(dve, step, f)
            dve.wait_ge(s_[name], count)
            drain(vec.tensor_tensor(lo[:, k0:k0 + 4, t0:t0 + n], b[:, 0:4 * n].rearrange("p (k n) -> p k n", k=4),
                                    hi[:, k0:k0 + 4, t0:t0 + n].bitcast(F32), ALU.subtract), step, f)

        for step in SCHEDULE:
            k = step[0]
            if k == "norm":
                t = step[1]
                t0, n = TILES[t]
                dve.wait_ge(s_["x_sq"], t + 1)
                V(vec.reciprocal(rstd[0:n, t:t + 1], rms[0:n, t:t + 1]))
                if t == 0:
                    dve.wait_ge(s_["gain_loaded"], 16)
                V.mark(vec.scalar_tensor_tensor(out=xn[0:n, t % 2, :], in0=xs[0:n, t % 2, :], scalar=rstd[0:n, t:t + 1],
                                                in1=gain[0:n, :], op0=ALU.mult, op1=ALU.mult), s_["x_normed"], "x_normed")
                for i in range(2):
                    low(h_hi, h_lo, step, f"n{i}", t0, n, "x_hi", 2 * t + i + 1, 4 * i)
            elif k == "cache":
                dve.wait_ge(s_["att_loaded"], 16 * N_ATT)
                V(vec.tensor_scalar(subln[:, :], subln[:, :], 1.0 - LAM_INIT, None, ALU.mult))
                for m in range(2):
                    V(vec.tensor_tensor(lamv[:, 4, :], lamv[:, 2 * m, :], lamv[:, 2 * m + 1, :], ALU.mult))
                    V.mark(vec.tensor_reduce(lam2[:, m:m + 1], lamv[:, 4, :], AX.X, ALU.add), s_["lam_prod"], "lam_prod")
                dve.wait_ge(s_["lam_exp"], 1)
                V(vec.tensor_tensor(nlam[:, :], lam2[:, 3:4], lam2[:, 2:3], ALU.subtract))
                V(vec.tensor_scalar(nlam[:, :], nlam[:, :], -LAM_INIT, None, ALU.add))
            elif k == "kvtok":
                n = TILES[step[1]][1]
                b = full_bank(dve, step, "v")
                drain(vec.tensor_copy(vtok[0:n, step[1], :], b[0:n, 0:BW]), step, "v")
            elif k == "att":
                _, t, h = step
                t0, n = TILES[t]
                idx = t * BH + h
                pb = idx % 2
                keys = t0 + n if t < SAMPLE else PAST + DEC
                for m in range(2):
                    b = full_bank(dve, step, f"s{m}")
                    if t < SAMPLE:
                        V(vec.memset(b[0:CHUNK, keys - CHUNK:keys], NEG))
                    c = 2 * pb + m
                    V(vec.reduce_max(amax[0:n, c:c + 1], b[0:n, 0:keys], AX.X))
                    V.mark(vec.tensor_scalar(amax[0:n, c:c + 1], amax[0:n, c:c + 1], -SCALE, None, ALU.mult),
                           s_["smax"], "smax")
                landed(dve, step, "s0")
                landed(dve, step, "s1")
                a0, a1 = arec[0:n, 2 * pb:2 * pb + 1], arec[0:n, 2 * pb + 1:2 * pb + 2]
                V(vec.reciprocal(arec[0:n, 2 * pb:2 * pb + 2], asum[0:n, 2 * pb:2 * pb + 2]))
                V(vec.tensor_tensor(a1, a1, nlam[0:n, :], ALU.mult))
                p0, p1 = probs[0:n, pb, 0, 0:keys], probs[0:n, pb, 1, 0:keys]
                V(vec.tensor_scalar(p0, p0, a0, None, ALU.mult))
                V.mark(vec.scalar_tensor_tensor(out=p0, in0=p1, scalar=a1, in1=p0, op0=ALU.mult, op1=ALU.add),
                       s_["sattn"], "sattn")
            elif k == "oscale":
                dve.wait_ge(s_["o_rms"], 2)
                V(vec.reciprocal(orst[:, 0:SAMPLE * BH], orms[:, 0:SAMPLE * BH]))
                V(vec.reciprocal(orst[0:DEC, SAMPLE * BH:], orms[0:DEC, SAMPLE * BH:]))
            elif k == "ofin":
                t = step[1]
                t0, n = TILES[t]
                for h in range(BH):
                    o = otok[0:n, t, h * BV:(h + 1) * BV]
                    ins = vec.scalar_tensor_tensor(out=o, in0=o, scalar=orst[0:n, t * BH + h:t * BH + h + 1],
                                                   in1=subln[0:n, :], op0=ALU.mult, op1=ALU.mult)
                V.mark(ins, s_["o_scaled"], "o_scaled")
                low(o_hi, o_lo, step, "o", t0, n, "o_hi_done", t + 1, 0)
            elif k == "shift":
                i = step[1]
                if i == 0:
                    landed(dve, ("params",), "pv")
                    dve.wait_ge(stored, 16 * NT)
                    for s in range(2):
                        dve.wait_ge(kout_stored[s], 16 * (3 - s))
                block_landed(dve, ("c", i))
                V(vec.memset(C[:, i, 0:1], 0.0))
                V(vec.tensor_copy(C[:, i, JS:JS + 1], pv[:, PV_SHIFT + i:PV_SHIFT + i + 1]))
                V(vec.tensor_copy(last[:, 0, i:i + 1], C[:, i, SEQ:SEQ + 1]))
                V(vec.tensor_copy(last[:, 1, i:i + 1], C[:, i, J:J + 1]))
                V(vec.tensor_tensor(tmp[:, 0, :], C[:, i, 0:J], C[:, i, 1:1 + J], ALU.subtract))
                V.mark(vec.scalar_tensor_tensor(out=C[:, i, 1:1 + J], in0=tmp[:, 0, :], scalar=pv[:, PV_MU + i:PV_MU + i + 1],
                                                in1=C[:, i, 1:1 + J], op0=ALU.mult, op1=ALU.add), s_["shifted"], "shifted")
            elif k == "shiftout":
                V.mark(vec.tensor_scalar(oka[:, :], pv[:, PV_KA:PV_KA + CT], -1.0, 1.0, ALU.mult, ALU.add),
                       s_["last_done"], "last_done")
            elif k == "lora":
                dve.wait_ge(s_["lora_a"], 1)
                V(vec.tensor_scalar(C[:, CG, 1:1 + J], C[:, CG, 1:1 + J], 0.5, 0.5, ALU.mult, ALU.add))
                V(vec.tensor_scalar(C[G2P:P, CG2, 1:1 + J], C[G2P:P, CG2, 1:1 + J], 0.5, 0.5, ALU.mult, ALU.add))
            elif k == "knorm":
                c = step[1]
                V(vec.tensor_scalar(tmp[:, 0, :], C[:, CK + c, 1:1 + J], pv[:, PV_KK + c:PV_KK + c + 1], None, ALU.mult))
                V.mark(vec.tensor_tensor(AR[:, c, 0, :], tmp[:, 0, :], tmp[:, 0, :], ALU.mult), s_["ksq"], "ksq")
                b = full_bank(dve, step, "q0")
                full_bank(dve, step, "q1")
                drain(vec.tensor_scalar(AR[:, c, 0, 0:HALF], b[:, 0:HALF], 1e-24, None, ALU.max), step, "q0")
                b = bank(step, "q1")
                drain(vec.tensor_scalar(AR[:, c, 0, HALF:J], b[:, 0:J - HALF], 1e-24, None, ALU.max), step, "q1")
                V.mark(vec.tensor_copy(tmp[:, 1, 0:1], AR[:, c, 0, 0:1]), s_["kmaxed"], "kmaxed")
            elif k == "krsqrt":
                for c in range(CT):
                    dve.wait_ge(s_["ksqrt"], c + 1)
                    V(vec.reciprocal(AR[:, c, 0, :], AR[:, c, 0, :]))
            elif k == "rw1":
                c = step[1]
                t0, t1, t2, t3, t4, t5 = (tmp[:, n, :] for n in range(6))
                r, kx = C[:, CR + c, 1:1 + J], C[:, CK + c, 1:1 + J]

                def par(col):
                    return pv[:, col + c:col + c + 1]

                landed(dve, step, "w0")
                landed(dve, step, "w1")
                V(vec.tensor_scalar(t0, t0, -DECAY / 2, -DECAY / 2, ALU.mult, ALU.add))
                landed(dve, step, "a0")
                landed(dve, step, "a1")
                V(vec.tensor_scalar(t1, t1, 0.5, 0.5, ALU.mult, ALU.add))
                V.mark(vec.tensor_tensor_scan(t2, cst[:, K_SCAN:K_SCAN + J], t0, 0.0, ALU.mult, ALU.add), s_["rw_g"], "rw_g")
                V.mark(vec.tensor_tensor(t0, t2, t0, ALU.subtract), s_["rw_gm"], "rw_gm")
                dve.wait_ge(s_["rw_p"], c + 1)
                V(vec.tensor_copy(pend[:, c, 0:NCH], t3[:, 0:SEQ].rearrange("p (q l) -> p q l", l=CHUNK)[:, :, CHUNK - 1]))
                V(vec.tensor_copy(pend[:, c, NCH:NCH + 1], t3[:, J - 1:J]))
                V(vec.tensor_tensor(AR[:, c, 1, :], r, t3, ALU.mult))
                V(vec.tensor_scalar(t4, t1, par(PV_KA), oka[:, c:c + 1], ALU.mult, ALU.add))
                V(vec.tensor_scalar(t5, kx, par(PV_KK), None, ALU.mult))
                V(vec.tensor_tensor(kx, kx, t4, ALU.mult))
                V(vec.tensor_tensor(t4, t5, AR[:, c, 0, :], ALU.mult))
                V.mark(vec.scalar_tensor_tensor(out=t5, in0=r, scalar=par(PV_RK), in1=kx, op0=ALU.mult, op1=ALU.mult),
                       s_["rw_bo"], "rw_bo")
            elif k == "rw2":
                c = step[1]
                V(vec.tensor_tensor(t1, t4, t1, ALU.mult))
                dve.wait_ge(s_["rw_e2"], c + 1)
                V(vec.tensor_tensor(AR[:, c, 0, :], t4, t0, ALU.mult))
                V(vec.tensor_tensor(C[:, CR + c, 1:1 + J], t1, t2, ALU.mult))
                for i, (a, b_) in enumerate(((0, HALF), (HALF, J))):
                    b = full_bank(dve, step, f"b{i}")
                    drain(vec.tensor_tensor(bonus[:, c, a:b_], b[:, 0:b_ - a], C[:, CV + c, 1 + a:1 + b_], ALU.mult),
                          step, f"b{i}")
                V.mark(vec.tensor_tensor(kx, kx, t2, ALU.mult), s_["rw_done"], "rw_done")
            elif k == "init0":
                V(vec.memset(sio[:, :, :], 0.0))
                V(vec.memset(ebd[:, :, :, :], 0.0))
                V(vec.memset(mcur[:, :, :, :], 0.0))
                V.mark(vec.memset(mbd[:, :, :, :, :], 0.0), s_["zeroed"], "zeroed")
            elif k == "init":
                b = full_bank(dve, step, "s")
                bv = b[:, 0:512].rearrange("p (g c k) -> p g c k", g=2, c=2)
                for g in range(2):
                    V(vec.tensor_copy(mbd[:, g, state_slot(SAMPLE, 0), :, :], bv[:, g, :, :]))
                V(vec.tensor_copy(mcur[0:64, :, :, :], bv[0:64, :, :, 0:64]))
                drain(vec.tensor_copy(mcur[64:P, :, :, :], bv[64:P, :, :, 64:P]), step, "s")
            elif k == "w":
                _, st, t, g = step
                n, j0 = TILES[t][1], first(t)
                if st == "scores":
                    mask = cst[0:n, K_SC:K_SC + 2 * P].rearrange("p (u i) -> p u i", u=2)[:, :, 0:n]
                    for f, dst in (("b", lt), ("k", gt)):
                        for p in range(2):
                            b = full_bank(dve, step, f"{f}{p}")
                            for c in range(2):
                                o = dst[0:n, 2 * c + p, :].rearrange("p (u i) -> p u i", u=2)[:, :, 0:n]
                                ins = vec.tensor_tensor(o, b[0:n, c * 2 * n:(c + 1) * 2 * n].rearrange("p (u i) -> p u i", u=2),
                                                        mask, ALU.mult)
                                if c == 0:
                                    V(ins)
                            drain(ins, step, f"{f}{p}")
                elif st == "x0":
                    m0 = cst[0:n, K_M0:K_M0 + n].unsqueeze(1).broadcast_to([n, 4, n])
                    idb = ident[0:n, 0:n].unsqueeze(1).broadcast_to([n, 4, n])
                    xt = XT[0:n, :, 0:n]
                    V(vec.tensor_tensor(xt, lt[0:n, :, 0:n], m0, ALU.mult))
                    V.mark(vec.tensor_tensor(xt, idb, xt, ALU.subtract), s_["xt_init"], "xt_init")
                elif st == "ef":
                    for ch, ln in chunks(t):
                        b = full_bank(dve, step, f"e{ch}")
                        bv = b[:, 0:2 * P].rearrange("p (c u k) -> p c u k", c=2, u=2)
                        for p in range(2):
                            lo, hi = 64 * p, 64 * p + 64
                            i64 = cst[lo:hi, K_I64:K_I64 + 64].unsqueeze(1).broadcast_to([64, 2, 64])
                            V(vec.tensor_tensor(ebd[lo:hi, ch, :, lo:hi], bv[lo:hi, :, 0, :], i64, ALU.add))
                        drain(vec.tensor_copy(ff[:, ch, :, :], bv[:, :, 1, :]), step, f"e{ch}")
                elif st == "chain":
                    for ch, ln in chunks(t):
                        b = full_bank(dve, step, f"c{ch}")
                        q = 2 * t + ch if t < SAMPLE else NCH
                        slot = state_slot(t, ch + 1)
                        drain(vec.tensor_tensor(mt[:, :, :], b[:, 0:P].rearrange("p (c v) -> p c v", c=2), ff[:, ch, :, :],
                                                ALU.add), step, f"c{ch}")
                        pe_ = pend[:, 2 * g:2 * g + 2, q:q + 1]
                        V(vec.tensor_tensor(mcur[:, g, :, :], mt[:, :, :], pe_.broadcast_to([P, 2, 64]), ALU.mult))
                        for p in range(2):
                            lo, hi = 64 * p, 64 * p + 64
                            ins = vec.tensor_tensor(mbd[lo:hi, g, slot, :, lo:hi], mt[lo:hi, :, :],
                                                    pe_[lo:hi].broadcast_to([64, 2, 64]), ALU.mult)
                            if p == 0:
                                V(ins)
                        V.mark(ins, s_["st_bd"], "st_bd")
                elif st == "q":
                    b = full_bank(dve, step, "q")
                    drain(vec.tensor_tensor(qT[:, :, 0:n], b[:, 0:2 * n].rearrange("p (c i) -> p c i", c=2),
                                            AR[:, 2 * g:2 * g + 2, 1, j0:j0 + n], ALU.add), step, "q")
            elif k == "wl":
                _, lv, t, g = step
                n = TILES[t][1]
                s = LEVELS[lv]
                b = full_bank(dve, step, "m")
                mask = cst[0:n, K_LV + 64 * lv:K_LV + 64 * lv + n // 2].unsqueeze(1).broadcast_to([n, 4, n // 2])
                drain(vec.tensor_tensor(mc[0:n, :, 0:n // 2], b[0:n, 0:256].rearrange("p (h i) -> p h i", h=4)[:, :, 0:n // 2],
                                        mask, ALU.mult), step, "m")
                b = full_bank(dve, step, "d")
                for h in range(4):
                    xv = X[0:n, h, 0:n].rearrange("p (b u s) -> p b u s", u=2, s=s)[:, :, 0, :]
                    ins = vec.tensor_tensor(xv, xv, b[0:n, h * 64:h * 64 + n // 2].rearrange("p (b s) -> p b s", s=s),
                                            ALU.subtract)
                    if h < 3:
                        V(ins)
                drain(ins, step, "d")
            elif k == "ymean":
                c = step[1]
                for i, (a, b_) in enumerate(((0, HALF), (HALF, J))):
                    b = full_bank(dve, step, f"m{i}")
                    drain(vec.scalar_tensor_tensor(out=AR[:, c, 1, a:b_], in0=b[:, 0:b_ - a], scalar=-1.0 / AD,
                                                   in1=AR[:, c, 1, a:b_], op0=ALU.mult, op1=ALU.add), step, f"m{i}")
                V.mark(vec.tensor_tensor(AR[:, c, 0, :], AR[:, c, 1, :], AR[:, c, 1, :], ALU.mult), s_["y_sq"], "y_sq")
            elif k == "yfin":
                c = step[1]
                y = AR[:, c, 1, :]
                landed(dve, ("yvar", c), "m0")
                landed(dve, ("yvar", c), "m1")
                V(vec.reciprocal(AR[:, c, 0, :], AR[:, c, 0, :]))
                V(vec.tensor_tensor(y, y, AR[:, c, 0, :], ALU.mult))
                V(vec.tensor_scalar(y, y, pv[:, PV_LNW + c:PV_LNW + c + 1], pv[:, PV_LNB + c:PV_LNB + c + 1], ALU.mult, ALU.add))
                V(vec.tensor_tensor(y, y, bonus[:, c, :], ALU.add))
                for i, (a, b_) in enumerate(((0, HALF), (HALF, J))):
                    b = full_bank(dve, step, f"g{i}")
                    drain(vec.tensor_tensor(AR[:, c, 1, a:b_], b[:, 0:b_ - a], AR[:, c, 1, a:b_], ALU.mult), step, f"g{i}")
                for i, (a, b_, u) in enumerate(((0, SEQ, 0), (SEQ, TOK, JS))):
                    dve.wait_ge(s_["y_hi_done"], 2 * c + i + 1)
                    V.mark(vec.tensor_tensor(y_lo[:, c, a:b_], AR[:, c, 1, u:u + b_ - a], y_hi[:, c, a:b_].bitcast(F32),
                                             ALU.subtract), s_["y_done"], "y_done")
            elif k == "ztok":
                _, r, i = step
                b = full_bank(dve, step, "z0")
                drain(vec.tensor_copy(z[:, 0:4, i * P:(i + 1) * P], b[:, 0:512].rearrange("p (t n) -> p t n", t=4)), step, "z0")
                b = full_bank(dve, step, "z1")
                drain(vec.tensor_copy(z[0:DEC, SAMPLE, i * P:(i + 1) * P], b[0:DEC, 0:P]), step, "z1")
            elif k == "zpost":
                r = step[1]
                dve.wait_ge(s_["gain_loaded"], 16 * (2 + r))
                if r == 0:
                    dve.wait_ge(s_["x1_loaded"], 16 * NT)
                for t, (t0, n) in enumerate(TILES):
                    dve.wait_ge(s_["zrms"], NT * r + t + 1)
                    V(vec.reciprocal(rstd[0:n, t:t + 1], rms[0:n, t:t + 1]))
                    V(vec.scalar_tensor_tensor(out=z[0:n, t, :], in0=z[0:n, t, :], scalar=rstd[0:n, t:t + 1],
                                               in1=gain[0:n, :], op0=ALU.mult, op1=ALU.mult))
                    dst = x1 if r == 0 else z
                    V.mark(vec.tensor_tensor(dst[0:n, t, :], x1[0:n, t, :], z[0:n, t, :], ALU.add), s_["zres"], "zres")
                if r == 0:
                    dve.wait_ge(s_["gain2_loaded"], 16)
                    for t, (t0, n) in enumerate(TILES):
                        dve.wait_ge(s_["xrms"], t + 1)
                        V(vec.reciprocal(rstd[0:n, t:t + 1], rms[0:n, t:t + 1]))
                        V.mark(vec.scalar_tensor_tensor(out=z[0:n, t, :], in0=x1[0:n, t, :], scalar=rstd[0:n, t:t + 1],
                                                        in1=gain2[0:n, :], op0=ALU.mult, op1=ALU.mult), s_["xnorm"], "xnorm")
                        for i in range(2):
                            low(h_hi, h_lo, step, f"n{t}{i}", t0, n, "z_hi", 2 * t + i + 1, 4 * i)
            elif k == "ffn":
                sa, sb_ = FFN_BLOCK0 % 2, (FFN_BLOCK0 + 1) % 2
                a0, b0 = FFN_BLOCK0 // 2, (FFN_BLOCK0 + 1) // 2
                fs2 = f_s.rearrange("p (a b) -> p a b", a=2)
                ft2 = f_t.rearrange("p (a b) -> p a b", a=2)

                def pair(j, loop):
                    dve.wait_ge(s_["f_tanh"], j + 1)
                    if loop:
                        dve.wait_ge(s_["f_lo"], j)
                    vec.scalar_tensor_tensor(out=fs2, in0=ft2, scalar=1.0, in1=dps[sa][:, :, 0:HALF], op0=ALU.add,
                                             op1=ALU.mult).then_inc(dense_read[sa], 1)
                    dve.wait_ge(dense_read[sa], j + (a0 + 1))
                    dve.wait_ge(seg_done, j * 2 + (FFN_SEG0 + 2))
                    vec.tensor_tensor(fs2, fs2, dps[sb_][:, :, 0:HALF], ALU.mult).then_inc(dense_read[sb_], 1)
                    dve.wait_ge(dense_read[sb_], j + (b0 + 1))
                    dve.wait_ge(s_["f_hi"], j + 1)
                    hi = S[:, bass.ds(j, 1), 0, :] if loop else S[:, 0:1, 0, :]
                    lo = S[:, bass.ds(j, 1), 1, :] if loop else S[:, 0:1, 1, :]
                    vec.scalar_tensor_tensor(out=lo, in0=f_s.unsqueeze(1), scalar=0.5, in1=hi.bitcast(F32), op0=ALU.mult,
                                             op1=ALU.subtract).then_inc(s_["f_lo"], 1)

                pair(0, False)
                with dve.Fori(1, FT) as j:
                    pair(j, True)
            elif k == "dense":
                _, kind, i = step
                d = (kind, i)
                if kind == "outB":
                    block_landed(dve, ("gB", i))
                    acc = block_full(dve, d)
                    m2 = mb[:, i, :].rearrange("p (a b) -> p a b", a=2)
                    vec.scalar_tensor_tensor(out=m2, in0=m2, scalar=1.0, in1=acc[:, :, 0:HALF], op0=ALU.add,
                                             op1=ALU.mult).then_inc(block_sem(d), 1)
                elif kind == "outA":
                    block_landed(dve, ("gA", i))
                    acc = block_full(dve, d)
                    vec.scalar_tensor_tensor(out=mixt[:, :].rearrange("p (a b) -> p a b", a=2),
                                             in0=ga[:, i % GA_RING, :].rearrange("p (a b) -> p a b", a=2), scalar=1.0,
                                             in1=acc[:, :, 0:HALF], op0=ALU.add, op1=ALU.mult).then_inc(block_sem(d), 1)
                    block_landed(dve, d)
                    block_landed(dve, ("outB", i))
                    V.mark(vec.tensor_tensor(mixt[:, :], mixt[:, :], mb[:, i, :], ALU.add), s_["mixed"], "mixed")
                    dve.wait_ge(s_["mix_hi"], i + 1)
                    V.mark(vec.scalar_tensor_tensor(out=S[:, i, 1, :], in0=mixt[:, :], scalar=0.5,
                                                    in1=S[:, i, 0, :].bitcast(F32), op0=ALU.mult, op1=ALU.subtract),
                           s_["mix_done"], "mix_done")

    ctx.close()


_INS = ["x_prompt", "x_sample", "cache_k", "cache_v", "state_wkv", "state_shift", "norm_mix_pre", "norm_mix_post",
        "norm_ffn_pre", "norm_ffn_post", "w_in", "b_gate", "rwkv_mu", "rwkv_w0", "rwkv_w2", "rwkv_a0", "rwkv_a2",
        "rwkv_g2", "rwkv_k_k", "rwkv_k_a", "rwkv_r_k", "rwkv_ln_w", "rwkv_ln_b", "diff_lq1", "diff_lk1", "diff_lq2",
        "diff_lk2", "diff_subln", "w_out_a", "w_out_b", "w_o", "w_ffn_in", "w_ffn_out"]
_OUTS = [("y_prompt", (1, SEQ, D)), ("y_sample", (1, DEC, D)), ("k_prompt", (1, 1, SEQ, BH, 2, BD_)),
         ("v_prompt", (1, 1, SEQ, BH, BV)), ("wkv_prompt", (1, 1, AH, AD, AD)), ("shift_prompt", (1, 1, 1, A_COLS)),
         ("k_sample", (1, 1, DEC, BH, 2, BD_)), ("v_sample", (1, 1, DEC, BH, BV)), ("wkv_sample", (1, 1, AH, AD, AD)),
         ("shift_sample", (1, 1, 1, A_COLS))]


def kernel(**inputs):
    import concourse.bacc as bacc
    from concourse.bass_utils import run_bass_kernel_spmd

    nc = bacc.Bacc("TRN2", target_bir_lowering=False, num_devices=1)
    arrays, ins, outs = {}, {}, {}
    for name in _INS:
        a = np.ascontiguousarray(inputs[name])
        arrays[f"in_{name}"] = a
        ins[name] = nc.dram_tensor(f"in_{name}", a.shape, F32, kind="ExternalInput").ap()
    arrays["in_cst"] = constants()
    ins["cst"] = nc.dram_tensor("in_cst", (P, K_N), F32, kind="ExternalInput").ap()
    for name, shape in _OUTS:
        outs[name] = nc.dram_tensor(f"out_{name}", shape, F32, kind="ExternalOutput").ap()
    encoder_kernel(nc, ins, outs)
    r = run_bass_kernel_spmd(nc, [arrays], core_ids=[0])
    return tuple(r.results[0][f"out_{name}"] for name, _ in _OUTS)
```

```python
import math
from contextlib import ExitStack

import numpy as np

import concourse.bass as bass
from concourse import mybir

ALU = mybir.AluOpType
ACT = mybir.ActivationFunctionType
AX = mybir.AxisListType
F32 = mybir.dt.float32
F32R = mybir.dt.float32r

P = 128
D = 1024
KT = D // P
SEQ, DEC, PAST = 512, 32, 128
TOK = SEQ + DEC
HALF = TOK // 2
J = TOK + 1
JS = SEQ + 1
CHUNK = 64
NCH = SEQ // CHUNK
EPS = 1e-6
NEG = -1e30
AH, AD = 8, 64
AW = AH * AD
CT = AW // P
GATE_LORA = 160
A_COLS = 3 * AW + 64 + 64 + GATE_LORA
GN_EPS = 64e-5
BH, BD_, BV = 4, 64, 128
BW = BH * BV
N_IN = A_COLS + 3 * BW + 2 * D
D_FF = ((8 * D + 3 * 256 - 1) // (3 * 256)) * 256
FT = D_FF // P
LAM_INIT = 0.8 - 0.6 * math.exp(0.0)
SCALE = BD_ ** -0.5
DECAY = math.exp(-0.5)
LEVELS = [2, 4, 8, 16, 32]
TILES = [(t * P, P) for t in range(SEQ // P)] + [(SEQ, DEC)]
NT = len(TILES)
SAMPLE = NT - 1

NC = 15
CCOL = [min(P * i, A_COLS - P) for i in range(NC)]
CR, CK, CV, CWA, CG, CG2 = 0, 4, 8, 12, 13, 14
G2P = P - 32

PV_SHIFT, PV_MU, PV_W0, PV_A0, PV_KK, PV_KA, PV_RK, PV_LNW, PV_LNB, PV_BG = 0, 15, 30, 34, 38, 42, 46, 50, 54, 58
PV_N = PV_BG + 2 * KT

K_ID, K_SC = 0, P
K_M0 = K_SC + 2 * P
K_LV = K_M0 + P
K_BD = K_LV + len(LEVELS) * 64
K_I64 = K_BD + P
K_SCAN = K_I64 + 64
K_N = K_SCAN + J


def constants():
    c = np.zeros((P, K_N), np.float32)
    j, i = np.meshgrid(np.arange(P), np.arange(P), indexing="ij")
    same = j // CHUNK == i // CHUNK
    c[:, K_ID:K_ID + P] = np.eye(P)
    c[:, K_SC:K_SC + P] = (j < i) & same
    c[:, K_SC + P:K_SC + 2 * P] = (j <= i) & same
    c[:, K_M0:K_M0 + P] = (i == j + 1) & (j % 2 == 0)
    row, col = np.meshgrid(np.arange(P), np.arange(64), indexing="ij")
    for n, s in enumerate(LEVELS):
        c[:, K_LV + 64 * n:K_LV + 64 * (n + 1)] = (row // (2 * s) == col // s) & (row % (2 * s) >= s)
    c[:, K_BD:K_BD + P] = j // 64 == i // 64
    c[:, K_I64:K_I64 + 64] = row % 64 == col
    c[:, K_SCAN:K_SCAN + J] = 1.0
    for n in range(NCH):
        c[:, K_SCAN + n * CHUNK] = 0.0
    c[:, K_SCAN + JS] = 0.0
    return c


DENSE = [("qkv", i) for i in range(12)] + [("c", i) for i in range(NC)]
DENSE += [(k, i) for k in ("gB", "gA", "outB", "outA", "wo") for i in range(8)]
FFN_BLOCK0 = len(DENSE)
DENSE += [(("ug", "uv")[i % 2], i // 2) for i in range(2 * FT)]
DENSE += [("down", i) for i in range(8)]
BLOCK = {d: n for n, d in enumerate(DENSE)}
DOWN_PARTS = [(0, 8), (8, 7), (15, 7)]

UNITS, SEGS = [], []
for _kind, _i in DENSE:
    if _kind in ("outA", "outB"):
        if _i % 2 == 0:
            UNITS.append((_kind, _i // 2, 0))
        SEGS.append((len(UNITS) - 1, _kind, _i))
    elif _kind == "down":
        for _p in range(3):
            UNITS.append((_kind, _i, _p))
            SEGS.append((len(UNITS) - 1, _kind, _i))
    else:
        UNITS.append((_kind, _i, 0))
        SEGS.append((len(UNITS) - 1, _kind, _i))
UNIT_END = {u: max(n for n, s in enumerate(SEGS) if s[0] == u) + 1 for u in range(len(UNITS))}
BLOCK_END = {d: max(n for n, s in enumerate(SEGS) if s[1:] == d) + 1 for d in DENSE}
UNIT_OF = {}
for _n, _s in enumerate(SEGS):
    UNIT_OF.setdefault(_s[1:], []).append((_s[0], _n))
FFN_UNIT0 = UNIT_OF[("ug", 0)][0][0]
FFN_SEG0 = UNIT_OF[("ug", 0)][0][1]
DOWN_UNIT0 = UNIT_OF[("down", 0)][0][0]

WKV = [(t, g) for t in range(NT) for g in range(2)]


def levels(t):
    return range(len(LEVELS) if t < SAMPLE else len(LEVELS) - 1)


def schedule():
    def dense(kind, i, part=0, parts=1):
        return ("dense", kind, i, part, parts)

    def skew(n, *stages):
        return [(st, i - k) for i in range(n + len(stages) - 1) for k, st in reversed(list(enumerate(stages)))
                if 0 <= i - k < n]

    s = skew(NT, "normA", "normB") + [("params",)]
    s += [dense("qkv", i) for i in range(12)]
    s += [("cache",)] + [("kvtok", t) for t in range(NT)]
    pieces = [dense("c", i, p, 4) for i in range(NC) for p in range(4)]
    heads = [(t, h) for t in range(NT) for h in range(BH)]
    s += [("attS", *heads[0]), ("attS", *heads[1])]
    left = 0
    for i, th in enumerate(heads):
        s += pieces[:1] + [("attP", *th)] + pieces[1:2]
        if i + 2 < len(heads):
            s += [("attS", *heads[i + 2])]
        s += pieces[2:3] + [("attO", *th)]
        pieces = pieces[3:]
        while left < NC and (left + 1) * 4 <= (i + 1) * 3 - 3:
            s += [("shift", left)]
            left += 1
    s += pieces + [("oscale",)] + [("shift", i) for i in range(left, NC)]
    gates = [dense(k, i) for k in ("gB", "gA") for i in range(8)]
    s += gates[:1] + [("lora",), ("shiftout",)] + [("ofin", t) for t in range(NT)] + gates[1:2]
    gates = gates[2:]
    s += [("ksquare", c) for c in range(CT)]
    for c in range(CT):
        s += [("knorm", c)] + gates[:1]
        gates = gates[1:]
    s += [("krsqrt",)]
    for c in range(CT):
        s += gates[:1] + [("rw1", c)] + gates[1:2] + [("rw2", c)]
        gates = gates[2:]
    s += [("init0",)] + gates
    fill = [dense("outB", i, p, 2) for i in range(8) for p in range(2)]
    for t in range(NT):
        s += [("init",)] if t == SAMPLE else []
        for st in ("tok", "scores", "x0", "gv"):
            s += [("w", st, t, g) for g in range(2)]
        for lv in levels(t):
            for st in ("wm", "wd", "wt"):
                s += [(st, lv, t, g) for g in range(2)]
            s += fill[:1] if lv % 5 else []
            fill = fill[1:] if lv % 5 else fill
        for st in ("wu", "ef", "chain0", "q", "y") + (("chain1",) if t < SAMPLE else ()):
            s += [("w", st, t, g) for g in range(2)]
        if t >= SAMPLE - 1:
            s += [("final", t, g) for g in range(2)]
    assert len(fill) <= 0, len(fill)
    s += [("ymean", c) for c in range(CT)] + [("yvar", c) for c in range(CT)] + [("yfin", c) for c in range(CT)]
    s += [dense("outA", i) for i in range(8)]
    for r, kind in enumerate(("wo", "down")):
        for i in range(8):
            s += [dense(kind, i)] + ([("ztok", r, i - 1)] if i else [])
        s += [("ztok", r, 7)]
        s += skew(NT, "zA0", "zB", "zC") + [("ffn",)] if r == 0 else [("zA1", t) for t in range(NT)]
    return s


SCHEDULE = schedule()


def fills(step):
    k = step[0]
    if k == "params":
        return ["pv"]
    if k in ("normB", "zC"):
        return ["n0", "n1"]
    if k == "cache":
        return ["ck"]
    if k == "kvtok":
        return ["k", "v"]
    if k == "attS":
        return ["s0", "s1"]
    if k == "attP":
        return ["pt"]
    if k in ("ofin", "attO"):
        return ["o"]
    if k == "shiftout":
        return ["s"]
    if k == "knorm":
        return ["q0", "q1"]
    if k == "rw1":
        return ["w0", "w1", "a0", "a1"]
    if k == "rw2":
        return ["b0", "b1"]
    if k == "init":
        return ["s"]
    if k == "w":
        return {"tok": ["t0", "t1"], "scores": ["b0", "b1", "k0", "k1"], "gv": ["gv"], "x0": ["x"], "wu": ["wu"],
                "ef": ["e0", "e1"] if step[2] < SAMPLE else ["e0"], "chain0": ["c"], "chain1": ["c"],
                "q": ["q"], "y": ["y"]}[step[1]]
    if k in ("wm", "wd", "wt"):
        return [k[1]]
    if k == "final":
        return ["f"]
    if k in ("ymean", "yvar"):
        return ["m0", "m1"]
    if k == "yfin":
        return ["g0", "g1"]
    if k == "ztok":
        return ["z0", "z1"]
    return []


FILL = {}
for _s in SCHEDULE:
    for _f in fills(_s):
        FILL[(_s, _f)] = len(FILL)


def encoder_kernel(nc, i_, o_):
    ctx = ExitStack()
    phase2 = ExitStack()
    region = ExitStack()

    def sb(name, shape, dt=F32, at=ctx):
        return at.enter_context(nc.sbuf_tensor(name, shape, dt))

    def sem(name):
        return ctx.enter_context(nc.semaphore(name))

    w_raw = sb("w_raw", [P, 2, D])
    w_hi = sb("w_hi", [P, 2, D], F32R)
    w_lo = sb("w_lo", [P, 2, D], F32R)
    gain = sb("gain", [P, D])
    pv = sb("pv", [P, PV_N])
    pvh = sb("pvh", [P, PV_N])
    ident = sb("ident", [P, P])
    ssq = sb("ssq", [P, NT])
    rms = sb("rms", [P, NT])
    rstd = sb("rstd", [P, NT])

    cst = sb("cst", [P, K_N], at=phase2)
    pv_rows = sb("pv_rows", [PV_N, P], at=phase2)
    oka = sb("oka", [P, CT], at=phase2)
    wa2 = sb("wa2", [P, AW], at=phase2)
    g2a = sb("g2a", [P, AW], at=phase2)
    g2b = sb("g2b", [P, AW], at=phase2)
    last = sb("last", [P, 2, NC], at=phase2)
    lastT = sb("lastT", [2 * NC, P], at=phase2)
    pend = sb("pend", [P, CT, NCH + 1], at=phase2)
    C = sb("C", [P, NC, J + 1], at=phase2)
    dtmp = sb("dtmp", [P, J], at=phase2)
    mb = sb("mb", [P, 8, TOK], at=phase2)
    h_hi = sb("h_hi", [P, KT, TOK], F32R, at=region)
    h_lo = sb("h_lo", [P, KT, TOK], F32R, at=region)
    region.close()
    lt = sb("lt", [P, 2, 4, 2 * P], at=phase2)
    gt = sb("gt", [P, 2, 4, 2 * P], at=phase2)
    X = sb("X", [P, 2, 4, P], at=phase2)
    XT = sb("XT", [P, 2, 4, P], at=phase2)
    ag = sb("ag", [P, 2, 4, 2, 64], at=phase2)
    wu = sb("wu", [P, 2, 4, 2, 64], at=phase2)
    mc = sb("mc", [P, 2, 4, 64], at=phase2)
    o_hi = sb("o_hi", [P, BH, TOK], F32R, at=phase2)
    o_lo = sb("o_lo", [P, BH, TOK], F32R, at=phase2)

    xs = sb("xs", [P, NT, D], at=region)
    xn = sb("xn", [P, 2, D], at=region)
    region.close()
    qkv = sb("qkv", [P, 12, TOK], at=region)
    vtok = sb("vtok", [P, NT, BW], at=region)
    otok = sb("otok", [P, NT, BW], at=region)
    kout = sb("kout", [P, 2, BW], at=region)
    ck_in = sb("ck_in", [P, BW], at=region)
    ckT = sb("ckT", [P, BH, P], at=region)
    cv = sb("cv", [P, BW], at=region)
    pT = sb("pT", [P, 2, BW], at=region)
    lamv = sb("lamv", [P, 5, BD_], at=region)
    lam2 = sb("lam2", [P, 4], at=region)
    nlam = sb("nlam", [P, 1], at=region)
    amax = sb("amax", [P, 4], at=region)
    asum = sb("asum", [P, 4], at=region)
    arec = sb("arec", [P, 4], at=region)
    ossq = sb("ossq", [P, NT * BH], at=region)
    orms = sb("orms", [P, NT * BH], at=region)
    orst = sb("orst", [P, NT * BH], at=region)
    subln = sb("subln", [P, BV], at=region)
    probs = qkv[:, 8:12, :].rearrange("p a t -> p (a t)")[:, 0:4 * BW].rearrange("p (b n t) -> p b n t", b=2, n=2)
    region.close()

    AR = sb("AR", [P, CT, 2, J], at=region)
    bonus = sb("bonus", [P, CT, J], at=region)
    ga = sb("ga", [P, 8, TOK], at=region)
    inner = ExitStack()
    tmp = sb("tmp", [P, 6, J], at=inner)
    inner.close()
    tok = sb("tok", [P, 2, 3, 4, 64], at=inner)
    ebd = sb("ebd", [P, 2, 2, 2, P], at=inner)
    ff = sb("ff", [P, 2, 2, 2, 64], at=inner)
    qT = sb("qT", [P, 2, 2, P], at=inner)
    mt = sb("mt", [P, 2, 2, 64], at=inner)
    mcur = sb("mcur", [P, 2, 2, 64], at=inner)
    mbd = sb("mbd", [P, 2, 2, 2, P], at=inner)
    sout = dtmp[:, 0:2 * 64].rearrange("p (k v) -> p k v", k=2)
    sio = C[:, CWA, 0:4 * P].rearrange("p (c k) -> p c k", c=CT)
    inner.close()
    y_hi = sb("y_hi", [P, CT, TOK], F32R, at=inner)
    y_lo = sb("y_lo", [P, CT, TOK], F32R, at=inner)
    mixt = sb("mixt", [P, TOK], at=inner)
    inner.close()
    region.close()
    phase2.close()

    S = sb("S", [P, FT, 2, TOK], F32R)
    x1 = sb("x1", [P, NT, D])
    z = sb("z", [P, NT, D])
    zT = sb("zT", [P, TOK])
    gain2 = sb("gain2", [P, D])
    h2_hi = sb("h2_hi", [P, KT, TOK], F32R)
    h2_lo = sb("h2_lo", [P, KT, TOK], F32R)
    ftmp = z[:, :, :].rearrange("p t n -> p (t n)")
    f_t, f_s = ftmp[:, 0:TOK], ftmp[:, TOK:2 * TOK]

    dps = [ctx.enter_context(nc.psum_tensor(f"dense{i}", [P, 2, 512], F32)) for i in range(2)]
    side = [ctx.enter_context(nc.psum_tensor(f"side{i}", [P, 512], F32)) for i in range(4)]

    raw_loaded = [sem(f"raw_loaded{i}") for i in range(2)]
    hi_split, w_split = sem("hi_split"), sem("w_split")
    slot_ready = sem("slot_ready")
    seg_done = sem("seg_done")
    dense_read = [sem(f"dense_read{i}") for i in range(2)]
    filled = sem("filled")
    drained = [sem(f"drained{i}") for i in range(4)]
    vch, ach = sem("vector_chain"), sem("scalar_chain")
    stored = sem("stored")
    kout_stored = [sem(f"kout_stored{i}") for i in range(2)]
    names = """ident_loaded x_sq x_normed x_hi cst_loaded small_loaded att_loaded gain_loaded lam_prod lam_exp
        params_done smax sattn o_rms o_scaled o_hi_done last_done shifted lora_a kmaxed shift_set rw_w ksq ksqrt
        rw_g rw_p rw_gm rw_e2 rw_bo rw_done zeroed init_loaded xt_init x_upd st_bd
        y_sq y_hi_done y_done mixed mix_hi mix_done gain_used x1_loaded gain2_loaded zrms zres xrms xnorm z_hi
        f_tanh f_hi f_lo"""
    s_ = {n: sem(n) for n in names.split()}
    x_sems = [sem(f"x_loaded{t}") for t in range(NT)]

    def bank(step, f):
        return side[FILL[(step, f)] % 4]

    def open_bank(pe, step, f):
        n = FILL[(step, f)]
        if n >= 4:
            pe.wait_ge(drained[n % 4], n // 4)
        return side[n % 4]

    def full_bank(eng, step, f):
        n = FILL[(step, f)]
        eng.wait_ge(filled, n + 1)
        return side[n % 4]

    def drain_sem(step, f):
        return drained[FILL[(step, f)] % 4]

    def landed(eng, step, f):
        n = FILL[(step, f)]
        eng.wait_ge(drained[n % 4], n // 4 + 1)

    def block_full(eng, d):
        eng.wait_ge(seg_done, BLOCK_END[d])
        return dps[BLOCK[d] % 2]

    def block_sem(d):
        return dense_read[BLOCK[d] % 2]

    def block_landed(eng, d):
        eng.wait_ge(dense_read[BLOCK[d] % 2], BLOCK[d] // 2 + 1)

    class Chain:
        def __init__(self, eng, s):
            self.eng, self.s, self.count = eng, s, {}

        def __call__(self, ins):
            self.mark(ins, self.s, "")

        def mark(self, ins, s, name):
            self.count[name] = self.count.get(name, 0) + 1
            ins.then_inc(s, 1)
            self.eng.wait_ge(s, self.count[name])

    def x_rows(t):
        return i_["x_prompt"][0, t * P:(t + 1) * P, :] if t < SAMPLE else i_["x_sample"][0, :, :]

    def y_rows(t):
        return o_["y_prompt"][0, t * P:(t + 1) * P, :] if t < SAMPLE else o_["y_sample"][0, :, :]

    w_in = i_["w_in"][0].rearrange("(k p) n -> p k n", p=P)
    w_oa = i_["w_out_a"][0].rearrange("(k p) n -> p k n", p=P)
    w_ob = i_["w_out_b"][0].rearrange("(k p) n -> p k n", p=P)
    w_o = i_["w_o"][0].rearrange("(k p) n -> p k n", p=P)
    w_fi = i_["w_ffn_in"][0].rearrange("(k p) n -> p k n", p=P)
    w_fo = i_["w_ffn_out"][0].rearrange("(k p) n -> p k n", p=P)
    COL0 = {"qkv": A_COLS, "gB": A_COLS + 3 * BW + D, "gA": A_COLS + 3 * BW}

    block = ctx.enter_context(nc.Block())

    def st_count(t, ch, g):
        return 4 * t + 2 * ch + g + 1

    def key_tiles(t):
        return [(kt * P, P) for kt in range(t + 1)] if t < SAMPLE else [(0, PAST), (PAST, DEC)]

    def chunks(t):
        return [(c, CHUNK) for c in range(2)] if t < SAMPLE else [(0, DEC)]

    def first(t):
        return TILES[t][0] if t < SAMPLE else JS

    N_SMALL, N_ATT = 16, 7

    @block.sync
    def _(sp):
        for t in range(NT):
            sp.dma_start(xs[0:TILES[t][1], t, :], x_rows(t)).then_inc(x_sems[t], 16)
            if t == 0:
                sp.dma_start(gain[:, :], i_["norm_mix_pre"][0].partition_broadcast(P)).then_inc(s_["gain_loaded"], 16)
        for u, (kind, n, part) in enumerate(UNITS):
            slot = u % 2
            if FFN_UNIT0 <= u < DOWN_UNIT0:
                if u == FFN_UNIT0:
                    with sp.Fori(0, FT) as f:
                        for k in range(2):
                            s2 = (FFN_UNIT0 + k) % 2
                            sp.wait_ge(w_split, f * 2 + (FFN_UNIT0 + k - 1))
                            sp.dma_start(w_raw[:, s2, :].rearrange("p (k n) -> p k n", k=KT),
                                         w_fi[:, :, bass.ds(f * P + k * D_FF, P)]).then_inc(raw_loaded[s2], 16)
                continue
            if u >= 2:
                sp.wait_ge(w_split, u - 1)
            dst = w_raw[:, slot, :]
            if kind in ("qkv", "gA", "gB", "c"):
                c0 = CCOL[n] if kind == "c" else COL0[kind] + n * P
                sp.dma_start(dst.rearrange("p (k n) -> p k n", k=KT), w_in[:, :, c0:c0 + P]).then_inc(raw_loaded[slot], 16)
            elif kind in ("outA", "outB"):
                w = w_oa if kind == "outA" else w_ob
                sp.dma_start(dst.rearrange("p (k n) -> p k n", k=CT), w[:, :, n * 256:(n + 1) * 256]).then_inc(
                    raw_loaded[slot], 16)
            elif kind == "wo":
                sp.dma_start(dst.rearrange("p (k n) -> p k n", k=KT), w_o[:, :, n * P:(n + 1) * P]).then_inc(
                    raw_loaded[slot], 16)
            else:
                k0, kn = DOWN_PARTS[part]
                sp.dma_start(dst[:, 0:kn * P].rearrange("p (k n) -> p k n", k=kn),
                             w_fo[:, k0:k0 + kn, n * P:(n + 1) * P]).then_inc(raw_loaded[slot], 16)

    @block.gpsimd
    def _(pool):
        def split(slot):
            nc.gpsimd.tensor_scalar(w_hi[:, slot, :], w_raw[:, slot, :], 1.0, 0.0, ALU.mult, ALU.add).then_inc(hi_split, 1)

        def split_lo(slot):
            nc.gpsimd.tensor_tensor(w_lo[:, slot, :], w_raw[:, slot, :], w_hi[:, slot, :].bitcast(F32),
                                    ALU.subtract).then_inc(w_split, 1)

        def unit(u):
            pool.wait_ge(raw_loaded[u % 2], 16 * (u // 2 + 1))
            if u >= 2:
                pool.wait_ge(seg_done, UNIT_END[u - 2])
            split(u % 2)
            pool.wait_ge(hi_split, u + 1)
            split_lo(u % 2)

        for u in range(FFN_UNIT0 + 2):
            unit(u)
        with pool.Fori(1, FT) as f:
            for k in range(2):
                u0 = FFN_UNIT0 + k
                pool.wait_ge(raw_loaded[u0 % 2], (f + (u0 // 2 + 1)) * 16)
                pool.wait_ge(seg_done, f * 2 + (FFN_SEG0 + k - 1))
                pool.sem_inc(slot_ready, 1)
                split(u0 % 2)
                pool.wait_ge(hi_split, f * 2 + (u0 + 1))
                split_lo(u0 % 2)
        for u in range(DOWN_UNIT0, len(UNITS)):
            unit(u)

    def ffn_mm(pe, three, b, u):
        for n in range(KT):
            ins = three(dps[b % 2], w_hi[:, u % 2, n * P:(n + 1) * P], w_lo[:, u % 2, n * P:(n + 1) * P],
                        h2_hi[:, n, :], h2_lo[:, n, :], n == 0, n == KT - 1)
        ins.then_inc(seg_done, 1)



    def wkv_pe(pe, step, transposes, close):
        t, g = step[2], step[3]
        n, j0 = TILES[t][1], first(t)
        heads = [(c, p) for c in range(2) for p in range(2)]
        if step[0] in ("wm", "wd", "wt"):
            lv = step[1]
            s = LEVELS[lv]
        if step[0] == "wm":
            b = open_bank(pe, step, "m")
            landed(pe, ("w", "x0", t, g), "x")
            if lv:
                landed(pe, ("wd", lv - 1, t, g), "d")
            for h in range(4):
                rhs = X[0:n, g, h, 0:n].rearrange("p (b u s) -> p b u s", u=2, s=s)[:, :, 0, :]
                out = b[0:n, h * 64:h * 64 + n // 2].rearrange("p (b s) -> p b s", s=s)
                ins = pe.matmul(out, lt[0:n, g, h, 0:n], rhs, start=True, stop=True)
            close(ins, step, "m")
            return
        if step[0] == "wd":
            b = open_bank(pe, step, "d")
            landed(pe, ("wm", lv, t, g), "m")
            if lv:
                landed(pe, ("wt", lv - 1, t, g), "t")
            for h in range(4):
                ins = pe.matmul(b[0:n, h * 64:h * 64 + n // 2], XT[0:n, g, h, 0:n], mc[0:n, g, h, 0:n // 2],
                                start=True, stop=True)
            close(ins, step, "d")
            return
        if step[0] == "wt":
            landed(pe, ("wd", lv, t, g), "d")
            transposes(step, "t", [(h * n, X[0:n, g, h, 0:n]) for h in range(4)])
            return
        st = step[1]
        if st == "tok":
            if (t, g) == (0, 0):
                pe.wait_ge(s_["rw_done"], CT)
            transposes(step, "t0", [((2 * q + c) * P, C[:, blk + 2 * g + c, 1 + j0:1 + j0 + n])
                                    for q, blk in enumerate((CR, CK)) for c in range(2)])
            transposes(step, "t1", [(c * P, C[:, CV + 2 * g + c, 1 + j0:1 + j0 + n]) for c in range(2)]
                       + [((2 + c) * P, AR[:, 2 * g + c, 0, j0:j0 + n]) for c in range(2)])
        elif st == "scores":
            for f, blk in (("b", CR), ("k", CK)):
                for p in range(2):
                    b = open_bank(pe, step, f"{f}{p}")
                    lo, hi = 64 * p, 64 * p + 64
                    for c in range(2):
                        ins = pe.matmul(b[0:n, c * 2 * n:(c + 1) * 2 * n].rearrange("p (u i) -> p u i", u=2),
                                        C[lo:hi, blk + 2 * g + c, 1 + j0:1 + j0 + n], AR[lo:hi, 2 * g + c, :, j0:j0 + n],
                                        start=True, stop=True)
                    close(ins, step, f"{f}{p}")
        elif st == "gv":
            b = open_bank(pe, step, "gv")
            landed(pe, ("w", "tok", t, g), "t1")
            landed(pe, ("w", "scores", t, g), "k0")
            landed(pe, ("w", "scores", t, g), "k1")
            for h in range(4):
                ins = pe.matmul(b[0:n, h * 64:(h + 1) * 64], gt[0:n, g, h, 0:n], tok[0:n, g, 2, h, :], start=True, stop=True)
            close(ins, step, "gv")
        elif st == "x0":
            pe.wait_ge(s_["xt_init"], 2 * t + g + 1)
            transposes(step, "x", [(h * n, XT[0:n, g, h, 0:n]) for h in range(4)])
        elif st == "wu":
            b = open_bank(pe, step, "wu")
            landed(pe, ("wt", levels(t)[-1], t, g), "t")
            landed(pe, ("w", "gv", t, g), "gv")
            for h in range(4):
                ins = pe.matmul(b[0:n, h * P:(h + 1) * P], XT[0:n, g, h, 0:n],
                                ag[0:n, g, h, :, :].rearrange("p u v -> p (u v)"), start=True, stop=True)
            close(ins, step, "wu")
        elif st == "ef":
            landed(pe, ("w", "wu", t, g), "wu")
            landed(pe, ("w", "tok", t, g), "t0")
            for ch, ln in chunks(t):
                b = open_bank(pe, step, f"e{ch}")
                r0, r1 = 64 * ch, 64 * ch + ln
                for c, p in heads:
                    h = 2 * c + p
                    out = b[64 * p:64 * p + 64, c * P:(c + 1) * P]
                    pe.matmul(out[:, 0:64], wu[r0:r1, g, h, 0, :], tok[r0:r1, g, 0, h, :], start=True, stop=True)
                    pe.matmul(out[:, 64:P], tok[r0:r1, g, 0, h, :], wu[r0:r1, g, h, 1, :], start=True, stop=False)
                    ins = pe.matmul(out[:, 64:P], tok[r0:r1, g, 1, h, :], tok[r0:r1, g, 2, h, :], start=False, stop=True)
                close(ins, step, f"e{ch}")
        elif st in ("chain0", "chain1"):
            ch = int(st[-1])
            b = open_bank(pe, step, "c")
            landed(pe, ("w", "ef", t, g), f"e{ch}")
            if t == SAMPLE:
                landed(pe, ("init",), "s")
            elif (t, ch) == (0, 0):
                pe.wait_ge(s_["zeroed"], 1)
            else:
                pe.wait_ge(s_["st_bd"], st_count(t - 1 + ch, 1 - ch, g))
            for c in range(2):
                ins = pe.matmul(b[:, c * 64:(c + 1) * 64], ebd[:, g, ch, c, :], mcur[:, g, c, :], start=True, stop=True)
            close(ins, step, "c")
        elif st == "q":
            b = open_bank(pe, step, "q")
            for p in range(2):
                landed(pe, ("w", "scores", t, g), f"b{p}")
            for c, p in heads:
                h = 2 * c + p
                ins = pe.matmul(b[64 * p:64 * p + 64, c * n:(c + 1) * n], wu[0:n, g, h, 0, :], lt[0:n, g, h, P:P + n],
                                start=True, stop=True)
            close(ins, step, "q")
        elif st == "y":
            b = open_bank(pe, step, "y")
            landed(pe, ("w", "q", t, g), "q")
            for c in range(2):
                for p in range(2):
                    h = 2 * c + p
                    out = b[64 * p:64 * p + 64, c * n:(c + 1) * n]
                    pe.matmul(out, wu[0:n, g, h, 1, :], lt[0:n, g, h, P:P + n], start=True, stop=False)
                    pe.matmul(out, tok[0:n, g, 2, h, :], gt[0:n, g, h, P:P + n], start=False, stop=True)
                for ch, ln in chunks(t):
                    if ch:
                        pe.wait_ge(s_["st_bd"], st_count(t, 0, g))
                    ins = pe.matmul(b[:, c * n + 64 * ch:c * n + 64 * ch + ln], mbd[:, g, ch, c, :],
                                    qT[:, g, c, 64 * ch:64 * ch + ln], start=False, stop=True, skip_group_check=True)
            close(ins, step, "y")

    @block.tensor
    def _(pe):
        count = [0]

        def close(ins, step, f):
            assert FILL[(step, f)] == count[0], (step, f)
            count[0] += 1
            ins.then_inc(filled, 1)

        def three(acc, whi, wlo, rhi, rlo, first, final):
            for n, (w, r) in enumerate(((whi, rhi), (whi, rlo), (wlo, rhi))):
                for hf in range(2):
                    ins = pe.matmul(acc[:, hf, 0:HALF], w, r[:, hf * HALF:(hf + 1) * HALF],
                                    start=first and n == 0, stop=final and n == 2)
            return ins

        def dense(kind, i, part, nparts):
            d = (kind, i)
            b = BLOCK[d]
            if kind in ("qkv", "c") and b == 0:
                landed(pe, ("normB", SAMPLE), "n1")
            if kind == "outB":
                landed(pe, ("ofin", SAMPLE), "o")
            if kind == "outA":
                pe.wait_ge(s_["y_done"], 2 * CT)
            if kind == "wo":
                pe.wait_ge(s_["mix_done"], 8)
            if kind == "down":
                pe.wait_ge(s_["f_lo"], FT)
            if b >= 2 and part == 0:
                pe.wait_ge(dense_read[b % 2], b // 2)
            acc = dps[b % 2]
            parts = UNIT_OF[d]
            for p, (u, seg) in enumerate(parts):
                pe.wait_ge(w_split, u + 1)
                if kind in ("outA", "outB"):
                    hi, lo = (y_hi, y_lo) if kind == "outA" else (o_hi, o_lo)
                    ops = [(k * 256 + (i % 2) * P, hi[:, k, :], lo[:, k, :]) for k in range(CT)]
                elif kind == "wo":
                    ops = [(k * P, S[:, k, 0, :], S[:, k, 1, :]) for k in range(KT)]
                elif kind == "down":
                    k0, kn = DOWN_PARTS[p]
                    ops = [(k * P, S[:, k0 + k, 0, :], S[:, k0 + k, 1, :]) for k in range(kn)]
                else:
                    ops = [(k * P, h_hi[:, k, :], h_lo[:, k, :]) for k in range(KT)]
                here = range(len(ops) * part // nparts, len(ops) * (part + 1) // nparts)
                for n in here:
                    c, rh, rl = ops[n]
                    ins = three(acc, w_hi[:, u % 2, c:c + P], w_lo[:, u % 2, c:c + P], rh, rl,
                                p == 0 and n == 0, p == len(parts) - 1 and n == len(ops) - 1)
                if part == nparts - 1:
                    ins.then_inc(seg_done, 1)

        def transposes(step, f, pieces):
            b = open_bank(pe, step, f)
            for c0, src in pieces:
                n, m = src.shape[0], src.shape[1]
                ins = pe.transpose(b[0:m, c0:c0 + n], src, ident[0:n, 0:n])
            close(ins, step, f)

        pe.wait_ge(s_["ident_loaded"], 16)
        for step in SCHEDULE:
            k = step[0]
            if k == "dense":
                dense(*step[1:])
            elif k == "params":
                pe.wait_ge(s_["cst_loaded"], 16)
                pe.wait_ge(s_["small_loaded"], 16 * N_SMALL)
                transposes(step, "pv", [(0, pv_rows[:, :])])
            elif k == "normB":
                t = step[1]
                n = TILES[t][1]
                pe.wait_ge(s_["x_normed"], t + 1)
                for i in range(2):
                    transposes(step, f"n{i}", [(kk * n, xn[0:n, t % 2, (4 * i + kk) * P:(4 * i + kk + 1) * P])
                                               for kk in range(4)])
            elif k == "cache":
                pe.wait_ge(s_["att_loaded"], 16 * N_ATT)
                transposes(step, "ck", [(h * P, ck_in[:, h * P:(h + 1) * P]) for h in range(BH)])
            elif k == "kvtok":
                t0, n = TILES[step[1]]
                block_landed(pe, ("qkv", 11))
                if step[1] == 0:
                    block_landed(pe, ("qkv", 10))
                for f, b0 in (("k", 4), ("v", 8)):
                    transposes(step, f, [(h * P, qkv[:, b0 + h, t0:t0 + n]) for h in range(BH)])
            elif k == "attS":
                _, t, h = step
                t0, n = TILES[t]
                keys = t0 + n if t < SAMPLE else PAST + DEC
                if t == SAMPLE and h == 0:
                    landed(pe, ("cache",), "ck")
                for m in range(2):
                    b = open_bank(pe, step, f"s{m}")
                    lo, hi = 64 * m, 64 * m + 64
                    q = qkv[lo:hi, h, t0:t0 + n]
                    if t < SAMPLE:
                        ins = pe.matmul(b[0:n, 0:keys], q, qkv[lo:hi, 4 + h, 0:keys], start=True, stop=True)
                    else:
                        pe.matmul(b[0:n, 0:PAST], q, ckT[lo:hi, h, :], start=True, stop=True)
                        ins = pe.matmul(b[0:n, PAST:keys], q, qkv[lo:hi, 4 + h, t0:t0 + n], start=True, stop=True)
                    close(ins, step, f"s{m}")
            elif k == "attP":
                _, t, h = step
                n = TILES[t][1]
                pb = (t * BH + h) % 2
                pe.wait_ge(s_["sattn"], t * BH + h + 1)
                transposes(step, "pt", [(i * n, probs[0:n, pb, 0, c0:c0 + kn]) for i, (c0, kn) in enumerate(key_tiles(t))])
            elif k == "attO":
                _, t, h = step
                n = TILES[t][1]
                pb = (t * BH + h) % 2
                b = open_bank(pe, step, "o")
                landed(pe, ("attP", t, h), "pt")
                if h == 0:
                    landed(pe, ("kvtok", t), "v")
                kts = key_tiles(t)
                for i, (c0, kn) in enumerate(kts):
                    if t < SAMPLE:
                        v = vtok[0:P, i, h * BV:(h + 1) * BV]
                    else:
                        v = cv[:, h * BV:(h + 1) * BV] if i == 0 else vtok[0:DEC, SAMPLE, h * BV:(h + 1) * BV]
                    ins = pe.matmul(b[0:n, 0:BV], pT[0:kn, pb, i * n:(i + 1) * n], v,
                                    start=i == 0, stop=i == len(kts) - 1)
                close(ins, step, "o")
            elif k == "ofin":
                t0, n = TILES[step[1]]
                pe.wait_ge(s_["o_scaled"], step[1] + 1)
                transposes(step, "o", [(h * n, otok[0:n, step[1], h * BV:(h + 1) * BV]) for h in range(BH)])
            elif k == "shiftout":
                pe.wait_ge(s_["last_done"], 1)
                transposes(step, "s", [(0, last[:, :, :].rearrange("p g c -> p (g c)"))])
            elif k == "knorm":
                c = step[1]
                pe.wait_ge(s_["ksq"], c + 1)
                for i, (a, b_) in enumerate(((0, HALF), (HALF, J))):
                    b = open_bank(pe, step, f"q{i}")
                    close(pe.matmul(b[:, 0:b_ - a], cst[:, K_BD:K_BD + P], AR[:, c, 0, a:b_], start=True, stop=True),
                          step, f"q{i}")
            elif k == "rw1":
                c = step[1]
                if c == 0:
                    pe.wait_ge(s_["lora_a"], 1)
                for f, lo in (("w", 0), ("a", 64)):
                    for i, (a, b_) in enumerate(((0, HALF), (HALF, J))):
                        b = open_bank(pe, step, f"{f}{i}")
                        close(pe.matmul(b[:, 0:b_ - a], wa2[lo:lo + 64, c * P:(c + 1) * P],
                                        C[lo:lo + 64, CWA, 1 + a:1 + b_], start=True, stop=True), step, f"{f}{i}")
            elif k == "rw2":
                c = step[1]
                pe.wait_ge(s_["rw_bo"], c + 1)
                for i, (a, b_) in enumerate(((0, HALF), (HALF, J))):
                    b = open_bank(pe, step, f"b{i}")
                    close(pe.matmul(b[:, 0:b_ - a], cst[:, K_BD:K_BD + P], tmp[:, 5, a:b_], start=True, stop=True),
                          step, f"b{i}")
            elif k == "init":
                pe.wait_ge(s_["init_loaded"], 32)
                transposes(step, "s", [(c * P, sio[:, c, :]) for c in range(CT)])
            elif k in ("w", "wm", "wd", "wt"):
                wkv_pe(pe, step, transposes, close)
            elif k == "final":
                _, t, g = step
                pe.wait_ge(s_["st_bd"], st_count(t, len(chunks(t)) - 1, g))
                transposes(step, "f", [(c * P, mbd[:, g, len(chunks(t)) % 2, c, :]) for c in range(2)])
            elif k in ("ymean", "yvar"):
                c = step[1]
                if k == "ymean":
                    landed(pe, ("w", "y", SAMPLE, c // 2), "y")
                    src = AR[:, c, 1, :]
                else:
                    pe.wait_ge(s_["y_sq"], c + 1)
                    src = AR[:, c, 0, :]
                for i, (a, b_) in enumerate(((0, HALF), (HALF, J))):
                    b = open_bank(pe, step, f"m{i}")
                    close(pe.matmul(b[:, 0:b_ - a], cst[:, K_BD:K_BD + P], src[:, a:b_], start=True, stop=True),
                          step, f"m{i}")
            elif k == "yfin":
                c = step[1]
                for i, (a, b_) in enumerate(((0, HALF), (HALF, J))):
                    b = open_bank(pe, step, f"g{i}")
                    pe.matmul(b[:, 0:b_ - a], g2a[:, c * P:(c + 1) * P], C[:, CG, 1 + a:1 + b_], start=True, stop=False)
                    close(pe.matmul(b[:, 0:b_ - a], g2b[G2P:P, c * P:(c + 1) * P], C[G2P:P, CG2, 1 + a:1 + b_],
                                    start=False, stop=True), step, f"g{i}")
            elif k == "ztok":
                _, r, i = step
                block_landed(pe, ("wo" if r == 0 else "down", i))
                transposes(step, "z0", [(t * P, zT[:, t * P:(t + 1) * P]) for t in range(4)])
                transposes(step, "z1", [(0, zT[:, SEQ:TOK])])
            elif k == "zC":
                t, n = step[1], TILES[step[1]][1]
                pe.wait_ge(s_["xnorm"], t + 1)
                for i in range(2):
                    transposes(step, f"n{i}", [(kk * n, z[0:n, t, (4 * i + kk) * P:(4 * i + kk + 1) * P])
                                               for kk in range(4)])
            elif k == "ffn":
                landed(pe, ("zC", SAMPLE), "n1")
                for j in (0,):
                    for kk in range(2):
                        b = FFN_BLOCK0 + kk
                        pe.wait_ge(dense_read[b % 2], b // 2)
                        pe.wait_ge(w_split, FFN_UNIT0 + kk + 1)
                        ffn_mm(pe, three, b, FFN_UNIT0 + kk)
                with pe.Fori(1, FT) as f:
                    for kk in range(2):
                        b = FFN_BLOCK0 + kk
                        pe.wait_ge(dense_read[b % 2], f + b // 2)
                        pe.wait_ge(w_split, f * 2 + (FFN_UNIT0 + kk + 1))
                        ffn_mm(pe, three, b, FFN_UNIT0 + kk)

    @block.scalar
    def _(act):
        A = Chain(act, ach)
        n_stored = [0]
        f_act = nc.scalar.activation

        def store(dst, src):
            act.dma_start(dst, src).then_inc(stored, 16)
            n_stored[0] += 1

        def drain(ins, step, f):
            ins.then_inc(drain_sem(step, f), 1)

        def halves(hi, step, f, t0, n, name, k0):
            b = full_bank(act, step, f)
            f_act(hi[:, k0:k0 + 4, t0:t0 + n], b[:, 0:4 * n].rearrange("p (k n) -> p k n", k=4), ACT.Copy).then_inc(
                s_[name], 1)

        def rows(ap2, r0, n):
            act.dma_start(pv_rows[r0:r0 + n, :], ap2).then_inc(s_["small_loaded"], 16)

        act.dma_start(ident[:, :], i_["cst"][:, K_ID:K_ID + P]).then_inc(s_["ident_loaded"], 16)

        def load_parameters():
            act.dma_start(cst[:, :], i_["cst"][:, :]).then_inc(s_["cst_loaded"], 16)
            for ap1, r0 in ((i_["state_shift"][0, 0, 0], PV_SHIFT), (i_["rwkv_mu"][0], PV_MU)):
                rows(ap1[0:14 * P].rearrange("(r c) -> r c", c=P), r0, 14)
                rows(ap1[A_COLS - P:A_COLS].rearrange("(r c) -> r c", c=P), r0 + 14, 1)
            for name, r0, n in (("rwkv_w0", PV_W0, 4), ("rwkv_a0", PV_A0, 4), ("rwkv_k_k", PV_KK, 4), ("rwkv_k_a", PV_KA, 4),
                                ("rwkv_ln_w", PV_LNW, 4), ("rwkv_ln_b", PV_LNB, 4), ("b_gate", PV_BG, 16)):
                rows(i_[name][0].rearrange("(r c) -> r c", c=P), r0, n)
            rows(i_["rwkv_r_k"][0].rearrange("(r a) c -> r (a c)", a=2), PV_RK, 4)
            act.dma_start(wa2[0:64, :], i_["rwkv_w2"][0]).then_inc(s_["small_loaded"], 16)
            act.dma_start(wa2[64:P, :], i_["rwkv_a2"][0]).then_inc(s_["small_loaded"], 16)
            act.dma_start(g2a[:, :], i_["rwkv_g2"][0, 0:P, :]).then_inc(s_["small_loaded"], 16)
            act.dma_start(g2b[G2P:P, :], i_["rwkv_g2"][0, P:GATE_LORA, :]).then_inc(s_["small_loaded"], 16)
            act.dma_start(ck_in[:, :], i_["cache_k"][0, 0].rearrange("t h n d -> t (h n d)")).then_inc(s_["att_loaded"], 16)
            act.dma_start(cv[:, :], i_["cache_v"][0, 0].rearrange("t h e -> t (h e)")).then_inc(s_["att_loaded"], 16)
            for n, name in enumerate(("diff_lq1", "diff_lk1", "diff_lq2", "diff_lk2")):
                act.dma_start(lamv[:, n, :], i_[name][0].partition_broadcast(P)).then_inc(s_["att_loaded"], 16)
            act.dma_start(subln[:, :], i_["diff_subln"][0].partition_broadcast(P)).then_inc(s_["att_loaded"], 16)

        for step in SCHEDULE:
            k = step[0]
            if k == "params":
                b = full_bank(act, step, "pv")
                A(f_act(pvh[:, :], b[:, 0:PV_N], ACT.Copy, scale=0.5))
                drain(f_act(pv[:, :], b[:, 0:PV_N], ACT.Copy), step, "pv")
            elif k == "normA":
                t = step[1]
                t0, n = TILES[t]
                act.wait_ge(x_sems[t], 16)
                A(f_act(dps[0][0:n, :, :], xs[0:n, t, :].rearrange("p (a b) -> p a b", a=2), ACT.Square,
                        accum_out=ssq[0:n, t:t + 1]))
                A.mark(f_act(rms[0:n, t:t + 1], ssq[0:n, t:t + 1], ACT.Sqrt, scale=1.0 / D, bias=EPS), s_["x_sq"], "x_sq")
                if t == 1:
                    load_parameters()
            elif k == "normB":
                for i in range(2):
                    halves(h_hi, step, f"n{i}", *TILES[step[1]], "x_hi", 4 * i)
            elif k == "cache":
                act.wait_ge(s_["lam_prod"], 2)
                A.mark(f_act(lam2[:, 2:4], lam2[:, 0:2], ACT.Exp), s_["lam_exp"], "lam_exp")
                b = full_bank(act, step, "ck")
                drain(f_act(ckT[:, :, :], b[:, 0:BW].rearrange("p (h t) -> p h t", h=BH), ACT.Copy), step, "ck")
            elif k == "kvtok":
                t = step[1]
                t0, n = TILES[t]
                if t >= 2:
                    act.wait_ge(kout_stored[t % 2], 16 * (t // 2))
                b = full_bank(act, step, "k")
                drain(f_act(kout[0:n, t % 2, :], b[0:n, 0:BW], ACT.Copy), step, "k")
                landed(act, step, "k")
                kd, vd = (o_["k_prompt"], o_["v_prompt"]) if t < SAMPLE else (o_["k_sample"], o_["v_sample"])
                r0 = t0 if t < SAMPLE else 0
                act.dma_start(kd[0, 0, r0:r0 + n].rearrange("t h n d -> t (h n d)"), kout[0:n, t % 2, :]).then_inc(
                    kout_stored[t % 2], 16)
                landed(act, step, "v")
                store(vd[0, 0, r0:r0 + n].rearrange("t h e -> t (h e)"), vtok[0:n, t, :])
            elif k == "attS":
                _, t, h = step
                t0, n = TILES[t]
                idx = t * BH + h
                pb = idx % 2
                keys = t0 + n if t < SAMPLE else PAST + DEC
                for m in range(2):
                    b = full_bank(act, step, f"s{m}")
                    act.wait_ge(s_["smax"], 2 * idx + m + 1)
                    drain(f_act(probs[0:n, pb, m, 0:keys], b[0:n, 0:keys], ACT.Exp, bias=amax[0:n, 2 * pb + m:2 * pb + m + 1],
                                scale=SCALE, accum_out=asum[0:n, 2 * pb + m:2 * pb + m + 1]), step, f"s{m}")
            elif k == "attP":
                _, t, h = step
                n = TILES[t][1]
                pb = (t * BH + h) % 2
                b = full_bank(act, step, "pt")
                if t < SAMPLE:
                    drain(f_act(pT[:, pb, 0:(t + 1) * n], b[:, 0:(t + 1) * n], ACT.Copy), step, "pt")
                else:
                    f_act(pT[:, pb, 0:n], b[:, 0:n], ACT.Copy).then_inc(ach, 1)
                    A.count[""] = A.count.get("", 0) + 1
                    drain(f_act(pT[0:DEC, pb, n:2 * n], b[0:DEC, n:2 * n], ACT.Copy), step, "pt")
            elif k == "attO":
                _, t, h = step
                n, idx = TILES[t][1], t * BH + h
                b = full_bank(act, step, "o")
                A(f_act(otok[0:n, t, h * BV:(h + 1) * BV], b[0:n, 0:BV], ACT.Copy))
                drain(f_act(b[0:n, 0:BV], b[0:n, 0:BV], ACT.Square, accum_out=ossq[0:n, idx:idx + 1]), step, "o")
            elif k == "oscale":
                landed(act, ("attO", SAMPLE, BH - 1), "o")
                A.mark(f_act(orms[:, 0:SAMPLE * BH], ossq[:, 0:SAMPLE * BH], ACT.Sqrt, scale=1.0 / BV, bias=EPS),
                       s_["o_rms"], "o_rms")
                A.mark(f_act(orms[0:DEC, SAMPLE * BH:], ossq[0:DEC, SAMPLE * BH:], ACT.Sqrt, scale=1.0 / BV, bias=EPS),
                       s_["o_rms"], "o_rms")
            elif k == "ofin":
                halves(o_hi, step, "o", *TILES[step[1]], "o_hi_done", 0)
            elif k == "shiftout":
                b = full_bank(act, step, "s")
                drain(f_act(lastT[:, :], b[0:2 * NC, 0:P], ACT.Copy), step, "s")
                landed(act, step, "s")
                for g, name in enumerate(("shift_prompt", "shift_sample")):
                    dst = o_[name][0, 0, 0]
                    store(dst[0:14 * P].rearrange("(r c) -> r c", c=P), lastT[g * NC:g * NC + 14, :])
                    store(dst[14 * P:A_COLS].rearrange("(r c) -> r c", c=A_COLS - 14 * P), lastT[g * NC + 14:g * NC + 15, G2P:P])
            elif k == "lora":
                act.wait_ge(s_["shifted"], NC)
                A(f_act(C[0:64, CWA, 1:1 + J], C[0:64, CWA, 1:1 + J], ACT.Tanh))
                A(f_act(C[:, CG, 1:1 + J], C[:, CG, 1:1 + J], ACT.Tanh, scale=0.5))
                A.mark(f_act(C[G2P:P, CG2, 1:1 + J], C[G2P:P, CG2, 1:1 + J], ACT.Tanh, scale=0.5), s_["lora_a"], "lora_a")
            elif k == "ksquare":
                c = step[1]
                act.wait_ge(s_["shifted"], NC)
                if c == 0:
                    landed(act, ("ofin", SAMPLE), "o")
                    act.wait_ge(stored, 16 * n_stored[0])
                    for m in range(2):
                        act.wait_ge(kout_stored[m], 16 * (3 - m))
                A.mark(f_act(AR[:, c, 0, :], C[:, CK + c, 1:1 + J], ACT.Square, scale=pv[:, PV_KK + c:PV_KK + c + 1]),
                       s_["ksq"], "ksq")
            elif k == "krsqrt":
                act.wait_ge(s_["kmaxed"], 1)
                for c in range(CT):
                    A.mark(f_act(AR[:, c, 0, :], AR[:, c, 0, :], ACT.Sqrt), s_["ksqrt"], "ksqrt")
            elif k == "rw1":
                c = step[1]
                if c:
                    act.wait_ge(s_["rw_done"], c)
                for f, sl, col in (("w", 0, PV_W0), ("a", 1, PV_A0)):
                    for i, (a, b_) in enumerate(((0, HALF), (HALF, J))):
                        b = full_bank(act, step, f"{f}{i}")
                        drain(f_act(tmp[:, sl, a:b_], b[:, 0:b_ - a], ACT.Tanh, scale=0.5,
                                    bias=pvh[:, col + c:col + c + 1]), step, f"{f}{i}")
                        landed(act, step, f"{f}{i}")
                A(f_act(tmp[:, 0, :], tmp[:, 0, :], ACT.Copy, scale=-DECAY / 2, bias=-DECAY / 2))
                A(f_act(tmp[:, 1, :], tmp[:, 1, :], ACT.Copy, scale=0.5, bias=0.5))
                A(f_act(tmp[:, 4, :], tmp[:, 1, :], ACT.Identity, scale=pv[:, PV_KA + c:PV_KA + c + 1],
                        bias=oka[:, c:c + 1]))
                A.mark(f_act(tmp[:, 5, :], C[:, CK + c, 1:1 + J], ACT.Copy, scale=pv[:, PV_KK + c:PV_KK + c + 1]),
                       s_["rw_w"], "rw_w")
                act.wait_ge(s_["rw_g"], c + 1)
                A.mark(f_act(tmp[:, 3, :], tmp[:, 2, :], ACT.Exp), s_["rw_p"], "rw_p")
                act.wait_ge(s_["rw_gm"], c + 1)
                A(f_act(tmp[:, 0, :], tmp[:, 0, :], ACT.Exp))
                A.mark(f_act(tmp[:, 2, :], tmp[:, 2, :], ACT.Exp, scale=-1.0), s_["rw_e2"], "rw_e2")
            elif k == "init0":
                act.wait_ge(s_["zeroed"], 1)
                src = i_["state_wkv"][0, 0].rearrange("(c p) v k -> p v c k", p=2)
                for p in range(2):
                    act.dma_start(sio[64 * p:64 * p + 64, :, 64 * p:64 * p + 64], src[p]).then_inc(s_["init_loaded"], 16)
            elif k == "w":
                _, st, t, g = step
                n, j0 = TILES[t][1], first(t)
                if st == "tok":
                    b = full_bank(act, step, "t0")
                    drain(f_act(tok[0:n, g, 0:2, :, :].rearrange("p q h v -> p (q h v)"), b[0:n, 0:512], ACT.Copy), step, "t0")
                    b = full_bank(act, step, "t1")
                    A(f_act(tok[0:n, g, 2, :, :].rearrange("p h v -> p (h v)"), b[0:n, 0:256], ACT.Copy))
                    drain(f_act(ag[0:n, g, :, 0, :], b[0:n, 256:512].rearrange("p (h v) -> p h v", h=4), ACT.Copy), step, "t1")
                elif st == "gv":
                    b = full_bank(act, step, "gv")
                    drain(f_act(ag[0:n, g, :, 1, :], b[0:n, 0:256].rearrange("p (h v) -> p h v", h=4), ACT.Copy), step, "gv")
                elif st == "x0":
                    b = full_bank(act, step, "x")
                    drain(f_act(X[0:n, g, :, 0:n], b[0:n, 0:4 * n].rearrange("p (h i) -> p h i", h=4), ACT.Copy), step, "x")
                elif st == "wu":
                    b = full_bank(act, step, "wu")
                    drain(f_act(wu[0:n, g, :, :, :].rearrange("p h u v -> p (h u v)"), b[0:n, 0:512], ACT.Copy, scale=-1.0),
                          step, "wu")
                elif st == "y":
                    b = full_bank(act, step, "y")
                    drain(f_act(AR[:, 2 * g:2 * g + 2, 1, j0:j0 + n], b[:, 0:2 * n].rearrange("p (c i) -> p c i", c=2),
                                ACT.Copy), step, "y")
            elif k == "wt":
                t, g = step[2], step[3]
                n = TILES[t][1]
                b = full_bank(act, step, "t")
                drain(f_act(XT[0:n, g, :, 0:n], b[0:n, 0:4 * n].rearrange("p (h i) -> p h i", h=4), ACT.Copy), step, "t")
            elif k == "final":
                _, t, g = step
                b = full_bank(act, step, "f")
                act.wait_ge(stored, 16 * n_stored[0])
                bv = b[:, 0:2 * P].rearrange("p (c k) -> p c k", c=2)
                A(f_act(sout[0:64, :, :], bv[0:64, :, 0:64], ACT.Copy))
                drain(f_act(sout[64:P, :, :], bv[64:P, :, 64:P], ACT.Copy), step, "f")
                landed(act, step, "f")
                store(o_["wkv_prompt" if t < SAMPLE else "wkv_sample"][0, 0, 4 * g:4 * g + 4].rearrange(
                    "(c p) v k -> (p v) c k", p=2), sout[:, :, :])
            elif k == "yvar":
                c = step[1]
                for i, (a, b_) in enumerate(((0, HALF), (HALF, J))):
                    b = full_bank(act, step, f"m{i}")
                    drain(f_act(AR[:, c, 0, a:b_], b[:, 0:b_ - a], ACT.Sqrt, scale=1.0 / AD, bias=GN_EPS), step, f"m{i}")
            elif k == "yfin":
                c = step[1]
                landed(act, step, "g1")
                if c == 0:
                    act.wait_ge(stored, 16 * n_stored[0])
                A.mark(f_act(y_hi[:, c, 0:SEQ], AR[:, c, 1, 0:SEQ], ACT.Copy), s_["y_hi_done"], "y_hi_done")
                A.mark(f_act(y_hi[:, c, SEQ:TOK], AR[:, c, 1, JS:J], ACT.Copy), s_["y_hi_done"], "y_hi_done")
            elif k in ("zA0", "zA1"):
                r, t = int(k[-1]), step[1]
                n = TILES[t][1]
                landed(act, ("ztok", r, 7), "z0")
                landed(act, ("ztok", r, 7), "z1")
                A(f_act(dps[0][0:n, :, :], z[0:n, t, :].rearrange("p (a b) -> p a b", a=2), ACT.Square,
                        accum_out=ssq[0:n, t:t + 1]))
                A.mark(f_act(rms[0:n, t:t + 1], ssq[0:n, t:t + 1], ACT.Sqrt, scale=1.0 / D, bias=EPS), s_["zrms"], "zrms")
                if r:
                    for u in [t - 1] * (t > 0) + [t] * (t == SAMPLE):
                        act.wait_ge(s_["zres"], NT + u + 1)
                        store(y_rows(u), z[0:TILES[u][1], u, :])
            elif k == "zB":
                t = step[1]
                n = TILES[t][1]
                act.wait_ge(s_["zres"], t + 1)
                A(f_act(dps[0][0:n, :, :], x1[0:n, t, :].rearrange("p (a b) -> p a b", a=2), ACT.Square,
                        accum_out=ssq[0:n, t:t + 1]))
                A.mark(f_act(rms[0:n, t:t + 1], ssq[0:n, t:t + 1], ACT.Sqrt, scale=1.0 / D, bias=EPS), s_["xrms"], "xrms")
                if t == SAMPLE:
                    act.dma_start(gain[:, :], i_["norm_ffn_post"][0].partition_broadcast(P)).then_inc(s_["gain_loaded"], 16)
            elif k == "zC":
                for i in range(2):
                    halves(h2_hi, step, f"n{i}", *TILES[step[1]], "z_hi", 4 * i)
            elif k == "ffn":
                pa, pb_ = dps[FFN_BLOCK0 % 2], dps[(FFN_BLOCK0 + 1) % 2]

                def pair(j, before):
                    act.wait_ge(seg_done, j * 2 + (FFN_SEG0 + 1))
                    if before:
                        act.wait_ge(dense_read[FFN_BLOCK0 % 2], j + FFN_BLOCK0 // 2)
                    f_act(f_t.rearrange("p (a b) -> p a b", a=2), pa[:, :, 0:HALF], ACT.Tanh, scale=0.5).then_inc(
                        s_["f_tanh"], 1)
                    act.wait_ge(dense_read[(FFN_BLOCK0 + 1) % 2], j + ((FFN_BLOCK0 + 1) // 2 + 1))
                    dst = S[:, bass.ds(j, 1), 0, :] if before else S[:, 0:1, 0, :]
                    f_act(dst, f_s.unsqueeze(1), ACT.Copy, scale=0.5).then_inc(s_["f_hi"], 1)

                pair(0, False)
                with act.Fori(1, FT) as j:
                    pair(j, True)
            elif k == "dense":
                _, kind, i, part, parts = step
                d = (kind, i)
                if part < parts - 1:
                    continue
                if kind in ("outA", "outB"):
                    if kind == "outA":
                        act.wait_ge(s_["mixed"], i + 1)
                        f_act(S[:, i, 0, :], mixt[:, :], ACT.Copy, scale=0.5).then_inc(s_["mix_hi"], 1)
                    continue
                acc = block_full(act, d)
                if kind == "qkv":
                    f_act(qkv[:, i, :].rearrange("p (a b) -> p a b", a=2), acc[:, :, 0:HALF], ACT.Copy).then_inc(
                        block_sem(d), 1)
                elif kind == "c":
                    f_act(C[:, i, 1:1 + HALF], acc[:, 0, 0:HALF], ACT.Copy)
                    f_act(C[:, i, 1 + HALF:1 + SEQ], acc[:, 1, 0:SEQ - HALF], ACT.Copy)
                    f_act(C[:, i, 1 + JS:1 + J], acc[:, 1, SEQ - HALF:HALF], ACT.Copy).then_inc(block_sem(d), 1)
                elif kind in ("gA", "gB"):
                    col = PV_BG + i + (KT if kind == "gB" else 0)
                    dst = (mb if kind == "gB" else ga)[:, i, :].rearrange("p (a b) -> p a b", a=2)
                    f_act(dst, acc[:, :, 0:HALF], ACT.Tanh, scale=0.5, bias=pvh[:, col:col + 1]).then_inc(block_sem(d), 1)
                elif kind in ("wo", "down"):
                    if d == ("wo", 0):
                        act.wait_ge(s_["mix_done"], 8)
                        for t in range(NT):
                            act.dma_start(x1[0:TILES[t][1], t, :], x_rows(t)).then_inc(s_["x1_loaded"], 16)
                        act.dma_start(gain[:, :], i_["norm_mix_post"][0].partition_broadcast(P)).then_inc(
                            s_["gain_loaded"], 16)
                        act.dma_start(gain2[:, :], i_["norm_ffn_pre"][0].partition_broadcast(P)).then_inc(
                            s_["gain2_loaded"], 16)
                    if i:
                        full_bank(act, ("ztok", int(kind == "down"), i - 1), "z1")
                    f_act(zT[:, :].rearrange("p (a b) -> p a b", a=2), acc[:, :, 0:HALF], ACT.Copy).then_inc(block_sem(d), 1)
        act.wait_ge(stored, 16 * n_stored[0])
        act.wait_ge(kout_stored[0], 16 * 3)
        act.wait_ge(kout_stored[1], 16 * 2)

    @block.vector
    def _(dve):
        V = Chain(dve, vch)
        vec = nc.vector

        def drain(ins, step, f):
            ins.then_inc(drain_sem(step, f), 1)
            landed(dve, step, f)

        def low(hi, lo, step, f, t0, n, name, count, k0):
            b = full_bank(dve, step, f)
            dve.wait_ge(s_[name], count)
            drain(vec.tensor_tensor(lo[:, k0:k0 + 4, t0:t0 + n], b[:, 0:4 * n].rearrange("p (k n) -> p k n", k=4),
                                    hi[:, k0:k0 + 4, t0:t0 + n].bitcast(F32), ALU.subtract), step, f)

        for step in SCHEDULE:
            k = step[0]
            if k == "params":
                landed(dve, step, "pv")
                V(vec.memset(C[:, :, 0:1], 0.0))
                V.mark(vec.tensor_copy(C[:, :, JS:JS + 1], pv[:, PV_SHIFT:PV_SHIFT + NC].unsqueeze(2)),
                       s_["shift_set"], "shift_set")
            elif k == "normA":
                t = step[1]
                t0, n = TILES[t]
                dve.wait_ge(s_["x_sq"], t + 1)
                V(vec.reciprocal(rstd[0:n, t:t + 1], rms[0:n, t:t + 1]))
                if t == 0:
                    dve.wait_ge(s_["gain_loaded"], 16)
                if t >= 2:
                    full_bank(dve, ("normB", t - 2), "n1")
                V.mark(vec.scalar_tensor_tensor(out=xn[0:n, t % 2, :], in0=xs[0:n, t, :], scalar=rstd[0:n, t:t + 1],
                                                in1=gain[0:n, :], op0=ALU.mult, op1=ALU.mult), s_["x_normed"], "x_normed")
            elif k == "normB":
                t = step[1]
                for i in range(2):
                    low(h_hi, h_lo, step, f"n{i}", *TILES[t], "x_hi", 2 * t + i + 1, 4 * i)
            elif k == "cache":
                dve.wait_ge(s_["att_loaded"], 16 * N_ATT)
                V(vec.tensor_scalar(subln[:, :], subln[:, :], 1.0 - LAM_INIT, None, ALU.mult))
                for m in range(2):
                    V(vec.tensor_tensor(lamv[:, 4, :], lamv[:, 2 * m, :], lamv[:, 2 * m + 1, :], ALU.mult))
                    V.mark(vec.tensor_reduce(lam2[:, m:m + 1], lamv[:, 4, :], AX.X, ALU.add), s_["lam_prod"], "lam_prod")
                dve.wait_ge(s_["lam_exp"], 1)
                V(vec.tensor_tensor(nlam[:, :], lam2[:, 3:4], lam2[:, 2:3], ALU.subtract))
                V(vec.tensor_scalar(nlam[:, :], nlam[:, :], -LAM_INIT, None, ALU.add))
            elif k == "kvtok":
                n = TILES[step[1]][1]
                b = full_bank(dve, step, "v")
                drain(vec.tensor_copy(vtok[0:n, step[1], :], b[0:n, 0:BW]), step, "v")
            elif k == "attS":
                _, t, h = step
                t0, n = TILES[t]
                idx = t * BH + h
                pb = idx % 2
                keys = t0 + n if t < SAMPLE else PAST + DEC
                if idx >= 2:
                    landed(dve, ("attP", *divmod(idx - 2, BH)), "pt")
                for m in range(2):
                    b = full_bank(dve, step, f"s{m}")
                    if t < SAMPLE:
                        V(vec.memset(b[0:CHUNK, keys - CHUNK:keys], NEG))
                    c = 2 * pb + m
                    V(vec.reduce_max(amax[0:n, c:c + 1], b[0:n, 0:keys], AX.X))
                    V.mark(vec.tensor_scalar(amax[0:n, c:c + 1], amax[0:n, c:c + 1], -SCALE, None, ALU.mult),
                           s_["smax"], "smax")
            elif k == "attP":
                _, t, h = step
                t0, n = TILES[t]
                pb = (t * BH + h) % 2
                keys = t0 + n if t < SAMPLE else PAST + DEC
                landed(dve, ("attS", t, h), "s0")
                landed(dve, ("attS", t, h), "s1")
                a0, a1 = arec[0:n, 2 * pb:2 * pb + 1], arec[0:n, 2 * pb + 1:2 * pb + 2]
                V(vec.reciprocal(arec[0:n, 2 * pb:2 * pb + 2], asum[0:n, 2 * pb:2 * pb + 2]))
                V(vec.tensor_tensor(a1, a1, nlam[0:n, :], ALU.mult))
                p0, p1 = probs[0:n, pb, 0, 0:keys], probs[0:n, pb, 1, 0:keys]
                V(vec.tensor_scalar(p0, p0, a0, None, ALU.mult))
                V.mark(vec.scalar_tensor_tensor(out=p0, in0=p1, scalar=a1, in1=p0, op0=ALU.mult, op1=ALU.add),
                       s_["sattn"], "sattn")
            elif k == "oscale":
                dve.wait_ge(s_["o_rms"], 2)
                V(vec.reciprocal(orst[:, 0:SAMPLE * BH], orms[:, 0:SAMPLE * BH]))
                V(vec.reciprocal(orst[0:DEC, SAMPLE * BH:], orms[0:DEC, SAMPLE * BH:]))
            elif k == "ofin":
                t = step[1]
                t0, n = TILES[t]
                for h in range(BH):
                    o = otok[0:n, t, h * BV:(h + 1) * BV]
                    ins = vec.scalar_tensor_tensor(out=o, in0=o, scalar=orst[0:n, t * BH + h:t * BH + h + 1],
                                                   in1=subln[0:n, :], op0=ALU.mult, op1=ALU.mult)
                V.mark(ins, s_["o_scaled"], "o_scaled")
                low(o_hi, o_lo, step, "o", t0, n, "o_hi_done", t + 1, 0)
            elif k == "shift":
                i = step[1]
                block_landed(dve, ("c", i))
                V(vec.tensor_copy(last[:, :, i], C[:, i, SEQ:J + 1:J - SEQ]))
                V(vec.tensor_tensor(dtmp[:, :], C[:, i, 0:J], C[:, i, 1:1 + J], ALU.subtract))
                V.mark(vec.scalar_tensor_tensor(out=C[:, i, 1:1 + J], in0=dtmp[:, :], scalar=pv[:, PV_MU + i:PV_MU + i + 1],
                                                in1=C[:, i, 1:1 + J], op0=ALU.mult, op1=ALU.add), s_["shifted"], "shifted")
            elif k == "shiftout":
                V.mark(vec.tensor_scalar(oka[:, :], pv[:, PV_KA:PV_KA + CT], -1.0, 1.0, ALU.mult, ALU.add),
                       s_["last_done"], "last_done")
            elif k == "lora":
                dve.wait_ge(s_["lora_a"], 1)
                V(vec.tensor_scalar(C[:, CG, 1:1 + J], C[:, CG, 1:1 + J], 0.5, 0.5, ALU.mult, ALU.add))
                V(vec.tensor_scalar(C[G2P:P, CG2, 1:1 + J], C[G2P:P, CG2, 1:1 + J], 0.5, 0.5, ALU.mult, ALU.add))
            elif k == "knorm":
                c = step[1]
                for i, (a, b_) in enumerate(((0, HALF), (HALF, J))):
                    b = full_bank(dve, step, f"q{i}")
                    if i == 0:
                        full_bank(dve, step, "q1")
                    drain(vec.tensor_scalar(AR[:, c, 0, a:b_], b[:, 0:b_ - a], 1e-24, None, ALU.max), step, f"q{i}")
            elif k == "krsqrt":
                V.mark(vec.memset(dtmp[:, 0:1], 0.0), s_["kmaxed"], "kmaxed")
                for c in range(CT):
                    dve.wait_ge(s_["ksqrt"], c + 1)
                    V(vec.reciprocal(AR[:, c, 0, :], AR[:, c, 0, :]))
            elif k == "rw1":
                c = step[1]
                t0, t1, t2, t3, t4, t5 = (tmp[:, n, :] for n in range(6))
                r, kx = C[:, CR + c, 1:1 + J], C[:, CK + c, 1:1 + J]
                dve.wait_ge(s_["rw_w"], c + 1)
                V.mark(vec.tensor_tensor_scan(t2, cst[:, K_SCAN:K_SCAN + J], t0, 0.0, ALU.mult, ALU.add), s_["rw_g"], "rw_g")
                V.mark(vec.tensor_tensor(t0, t2, t0, ALU.subtract), s_["rw_gm"], "rw_gm")
                V(vec.tensor_tensor(kx, kx, t4, ALU.mult))
                V(vec.tensor_tensor(t4, t5, AR[:, c, 0, :], ALU.mult))
                V.mark(vec.scalar_tensor_tensor(out=t5, in0=r, scalar=pv[:, PV_RK + c:PV_RK + c + 1], in1=kx, op0=ALU.mult,
                                                op1=ALU.mult), s_["rw_bo"], "rw_bo")
                dve.wait_ge(s_["rw_p"], c + 1)
                V(vec.tensor_copy(pend[:, c, 0:NCH], t3[:, 0:SEQ].rearrange("p (q l) -> p q l", l=CHUNK)[:, :, CHUNK - 1]))
                V(vec.tensor_copy(pend[:, c, NCH:NCH + 1], t3[:, J - 1:J]))
                V(vec.tensor_tensor(AR[:, c, 1, :], r, t3, ALU.mult))
            elif k == "rw2":
                c = step[1]
                V(vec.tensor_tensor(t1, t4, t1, ALU.mult))
                dve.wait_ge(s_["rw_e2"], c + 1)
                V(vec.tensor_tensor(AR[:, c, 0, :], t4, t0, ALU.mult))
                V(vec.tensor_tensor(C[:, CR + c, 1:1 + J], t1, t2, ALU.mult))
                for i, (a, b_) in enumerate(((0, HALF), (HALF, J))):
                    b = full_bank(dve, step, f"b{i}")
                    drain(vec.tensor_tensor(bonus[:, c, a:b_], b[:, 0:b_ - a], C[:, CV + c, 1 + a:1 + b_], ALU.mult),
                          step, f"b{i}")
                V.mark(vec.tensor_tensor(kx, kx, t2, ALU.mult), s_["rw_done"], "rw_done")
            elif k == "init0":
                V(vec.memset(sio[:, :, :], 0.0))
                V(vec.memset(ebd[:, :, :, :], 0.0))
                V(vec.memset(mcur[:, :, :, :], 0.0))
                V.mark(vec.memset(mbd[:, :, :, :, :], 0.0), s_["zeroed"], "zeroed")
            elif k == "init":
                b = full_bank(dve, step, "s")
                bv = b[:, 0:512].rearrange("p (g c k) -> p g c k", g=2, c=2)
                for g in range(2):
                    V(vec.tensor_copy(mbd[:, g, 0, :, :], bv[:, g, :, :]))
                V(vec.tensor_copy(mcur[0:64, :, :, :], bv[0:64, :, :, 0:64]))
                drain(vec.tensor_copy(mcur[64:P, :, :, :], bv[64:P, :, :, 64:P]), step, "s")
            elif k == "w":
                _, st, t, g = step
                n, j0 = TILES[t][1], first(t)
                if st == "scores":
                    mask = cst[0:n, K_SC:K_SC + 2 * P].rearrange("p (u i) -> p u i", u=2)[:, :, 0:n]
                    mask = mask.unsqueeze(1).broadcast_to([n, 2, 2, n])
                    for f, dst in (("b", lt), ("k", gt)):
                        for p in range(2):
                            b = full_bank(dve, step, f"{f}{p}")
                            o = dst[0:n, g, p::2, :].rearrange("p c (u i) -> p c u i", u=2)[:, :, :, 0:n]
                            drain(vec.tensor_tensor(o, b[0:n, 0:4 * n].rearrange("p (c u i) -> p c u i", c=2, u=2), mask,
                                                    ALU.mult), step, f"{f}{p}")
                elif st == "x0":
                    m0 = cst[0:n, K_M0:K_M0 + n].unsqueeze(1).broadcast_to([n, 4, n])
                    idb = ident[0:n, 0:n].unsqueeze(1).broadcast_to([n, 4, n])
                    xt = XT[0:n, g, :, 0:n]
                    V(vec.tensor_tensor(xt, lt[0:n, g, :, 0:n], m0, ALU.mult))
                    V.mark(vec.tensor_tensor(xt, idb, xt, ALU.subtract), s_["xt_init"], "xt_init")
                elif st == "ef":
                    for ch, ln in chunks(t):
                        b = full_bank(dve, step, f"e{ch}")
                        bv = b[:, 0:2 * P].rearrange("p (c u k) -> p c u k", c=2, u=2)
                        for p in range(2):
                            lo, hi = 64 * p, 64 * p + 64
                            i64 = cst[lo:hi, K_I64:K_I64 + 64].unsqueeze(1).broadcast_to([64, 2, 64])
                            V(vec.tensor_tensor(ebd[lo:hi, g, ch, :, lo:hi], bv[lo:hi, :, 0, :], i64, ALU.add))
                        drain(vec.tensor_copy(ff[:, g, ch, :, :], bv[:, :, 1, :]), step, f"e{ch}")
                elif st in ("chain0", "chain1"):
                    ch = int(st[-1])
                    b = full_bank(dve, step, "c")
                    q = 2 * t + ch if t < SAMPLE else NCH
                    drain(vec.tensor_tensor(mt[:, g, :, :], b[:, 0:P].rearrange("p (c v) -> p c v", c=2), ff[:, g, ch, :, :],
                                            ALU.add), step, "c")
                    pe_ = pend[:, 2 * g:2 * g + 2, q:q + 1]
                    for p in range(2):
                        lo, hi = 64 * p, 64 * p + 64
                        vec.tensor_tensor(mbd[lo:hi, g, 1 - ch, :, lo:hi], mt[lo:hi, g, :, :],
                                          pe_[lo:hi].broadcast_to([64, 2, 64]), ALU.mult)
                    V.mark(vec.tensor_tensor(mcur[:, g, :, :], mt[:, g, :, :], pe_.broadcast_to([P, 2, 64]), ALU.mult),
                           s_["st_bd"], "st_bd")
                elif st == "q":
                    b = full_bank(dve, step, "q")
                    drain(vec.tensor_tensor(qT[:, g, :, 0:n], b[:, 0:2 * n].rearrange("p (c i) -> p c i", c=2),
                                            AR[:, 2 * g:2 * g + 2, 1, j0:j0 + n], ALU.add), step, "q")
            elif k == "wm":
                _, lv, t, g = step
                n = TILES[t][1]
                b = full_bank(dve, step, "m")
                mask = cst[0:n, K_LV + 64 * lv:K_LV + 64 * lv + n // 2].unsqueeze(1).broadcast_to([n, 4, n // 2])
                drain(vec.tensor_tensor(mc[0:n, g, :, 0:n // 2], b[0:n, 0:256].rearrange("p (h i) -> p h i", h=4)[:, :, 0:n // 2],
                                        mask, ALU.mult), step, "m")
            elif k == "wd":
                _, lv, t, g = step
                n = TILES[t][1]
                s = LEVELS[lv]
                b = full_bank(dve, step, "d")
                xv = X[0:n, g, :, 0:n].rearrange("p h (b u s) -> p h b u s", u=2, s=s)[:, :, :, 0, :]
                bv = b[0:n, 0:256].rearrange("p (h i) -> p h i", h=4)[:, :, 0:n // 2].rearrange("p h (b s) -> p h b s", s=s)
                drain(vec.tensor_tensor(xv, xv, bv, ALU.subtract), step, "d")
            elif k == "ymean":
                c = step[1]
                for i, (a, b_) in enumerate(((0, HALF), (HALF, J))):
                    b = full_bank(dve, step, f"m{i}")
                    drain(vec.scalar_tensor_tensor(out=AR[:, c, 1, a:b_], in0=b[:, 0:b_ - a], scalar=-1.0 / AD,
                                                   in1=AR[:, c, 1, a:b_], op0=ALU.mult, op1=ALU.add), step, f"m{i}")
                V.mark(vec.tensor_tensor(AR[:, c, 0, :], AR[:, c, 1, :], AR[:, c, 1, :], ALU.mult), s_["y_sq"], "y_sq")
            elif k == "yfin":
                c = step[1]
                y = AR[:, c, 1, :]
                landed(dve, ("yvar", c), "m0")
                landed(dve, ("yvar", c), "m1")
                V(vec.reciprocal(AR[:, c, 0, :], AR[:, c, 0, :]))
                V(vec.tensor_tensor(y, y, AR[:, c, 0, :], ALU.mult))
                V(vec.tensor_scalar(y, y, pv[:, PV_LNW + c:PV_LNW + c + 1], pv[:, PV_LNB + c:PV_LNB + c + 1], ALU.mult, ALU.add))
                V(vec.tensor_tensor(y, y, bonus[:, c, :], ALU.add))
                for i, (a, b_) in enumerate(((0, HALF), (HALF, J))):
                    b = full_bank(dve, step, f"g{i}")
                    drain(vec.tensor_tensor(AR[:, c, 1, a:b_], b[:, 0:b_ - a], AR[:, c, 1, a:b_], ALU.mult), step, f"g{i}")
                for i, (a, b_, u) in enumerate(((0, SEQ, 0), (SEQ, TOK, JS))):
                    dve.wait_ge(s_["y_hi_done"], 2 * c + i + 1)
                    V.mark(vec.tensor_tensor(y_lo[:, c, a:b_], AR[:, c, 1, u:u + b_ - a], y_hi[:, c, a:b_].bitcast(F32),
                                             ALU.subtract), s_["y_done"], "y_done")
            elif k == "ztok":
                _, r, i = step
                b = full_bank(dve, step, "z0")
                drain(vec.tensor_copy(z[:, 0:4, i * P:(i + 1) * P], b[:, 0:512].rearrange("p (t n) -> p t n", t=4)), step, "z0")
                b = full_bank(dve, step, "z1")
                drain(vec.tensor_copy(z[0:DEC, SAMPLE, i * P:(i + 1) * P], b[0:DEC, 0:P]), step, "z1")
            elif k in ("zA0", "zA1"):
                r, t = int(k[-1]), step[1]
                n = TILES[t][1]
                if t == 0:
                    dve.wait_ge(s_["gain_loaded"], 16 * (2 + r))
                    dve.wait_ge(s_["x1_loaded"], 16 * NT)
                dve.wait_ge(s_["zrms"], NT * r + t + 1)
                V(vec.reciprocal(rstd[0:n, t:t + 1], rms[0:n, t:t + 1]))
                V(vec.scalar_tensor_tensor(out=z[0:n, t, :], in0=z[0:n, t, :], scalar=rstd[0:n, t:t + 1],
                                           in1=gain[0:n, :], op0=ALU.mult, op1=ALU.mult))
                dst = x1 if r == 0 else z
                V.mark(vec.tensor_tensor(dst[0:n, t, :], x1[0:n, t, :], z[0:n, t, :], ALU.add), s_["zres"], "zres")
            elif k == "zB":
                t = step[1]
                n = TILES[t][1]
                if t == 0:
                    dve.wait_ge(s_["gain2_loaded"], 16)
                dve.wait_ge(s_["xrms"], t + 1)
                V(vec.reciprocal(rstd[0:n, t:t + 1], rms[0:n, t:t + 1]))
                V.mark(vec.scalar_tensor_tensor(out=z[0:n, t, :], in0=x1[0:n, t, :], scalar=rstd[0:n, t:t + 1],
                                                in1=gain2[0:n, :], op0=ALU.mult, op1=ALU.mult), s_["xnorm"], "xnorm")
            elif k == "zC":
                t = step[1]
                for i in range(2):
                    low(h2_hi, h2_lo, step, f"n{i}", *TILES[t], "z_hi", 2 * t + i + 1, 4 * i)
            elif k == "ffn":
                sa, sb_ = FFN_BLOCK0 % 2, (FFN_BLOCK0 + 1) % 2
                a0, b0 = FFN_BLOCK0 // 2, (FFN_BLOCK0 + 1) // 2
                fs2 = f_s.rearrange("p (a b) -> p a b", a=2)
                ft2 = f_t.rearrange("p (a b) -> p a b", a=2)

                def pair(j, loop):
                    dve.wait_ge(s_["f_tanh"], j + 1)
                    if loop:
                        dve.wait_ge(s_["f_lo"], j)
                    vec.scalar_tensor_tensor(out=fs2, in0=ft2, scalar=1.0, in1=dps[sa][:, :, 0:HALF], op0=ALU.add,
                                             op1=ALU.mult).then_inc(dense_read[sa], 1)
                    dve.wait_ge(dense_read[sa], j + (a0 + 1))
                    dve.wait_ge(seg_done, j * 2 + (FFN_SEG0 + 2))
                    vec.tensor_tensor(fs2, fs2, dps[sb_][:, :, 0:HALF], ALU.mult).then_inc(dense_read[sb_], 1)
                    dve.wait_ge(dense_read[sb_], j + (b0 + 1))
                    dve.wait_ge(s_["f_hi"], j + 1)
                    hi = S[:, bass.ds(j, 1), 0, :] if loop else S[:, 0:1, 0, :]
                    lo = S[:, bass.ds(j, 1), 1, :] if loop else S[:, 0:1, 1, :]
                    vec.scalar_tensor_tensor(out=lo, in0=f_s.unsqueeze(1), scalar=0.5, in1=hi.bitcast(F32), op0=ALU.mult,
                                             op1=ALU.subtract).then_inc(s_["f_lo"], 1)

                pair(0, False)
                with dve.Fori(1, FT) as j:
                    pair(j, True)
            elif k == "dense":
                _, kind, i, part, parts = step
                d = (kind, i)
                if part < parts - 1:
                    continue
                if kind == "outB":
                    block_landed(dve, ("gB", i))
                    acc = block_full(dve, d)
                    m2 = mb[:, i, :].rearrange("p (a b) -> p a b", a=2)
                    vec.scalar_tensor_tensor(out=m2, in0=m2, scalar=1.0, in1=acc[:, :, 0:HALF], op0=ALU.add,
                                             op1=ALU.mult).then_inc(block_sem(d), 1)
                elif kind == "outA":
                    block_landed(dve, ("gA", i))
                    acc = block_full(dve, d)
                    vec.scalar_tensor_tensor(out=mixt[:, :].rearrange("p (a b) -> p a b", a=2),
                                             in0=ga[:, i, :].rearrange("p (a b) -> p a b", a=2), scalar=1.0,
                                             in1=acc[:, :, 0:HALF], op0=ALU.add, op1=ALU.mult).then_inc(block_sem(d), 1)
                    block_landed(dve, d)
                    block_landed(dve, ("outB", i))
                    V.mark(vec.tensor_tensor(mixt[:, :], mixt[:, :], mb[:, i, :], ALU.add), s_["mixed"], "mixed")
                    dve.wait_ge(s_["mix_hi"], i + 1)
                    V.mark(vec.scalar_tensor_tensor(out=S[:, i, 1, :], in0=mixt[:, :], scalar=0.5,
                                                    in1=S[:, i, 0, :].bitcast(F32), op0=ALU.mult, op1=ALU.subtract),
                           s_["mix_done"], "mix_done")

    ctx.close()


_INS = ["x_prompt", "x_sample", "cache_k", "cache_v", "state_wkv", "state_shift", "norm_mix_pre", "norm_mix_post",
        "norm_ffn_pre", "norm_ffn_post", "w_in", "b_gate", "rwkv_mu", "rwkv_w0", "rwkv_w2", "rwkv_a0", "rwkv_a2",
        "rwkv_g2", "rwkv_k_k", "rwkv_k_a", "rwkv_r_k", "rwkv_ln_w", "rwkv_ln_b", "diff_lq1", "diff_lk1", "diff_lq2",
        "diff_lk2", "diff_subln", "w_out_a", "w_out_b", "w_o", "w_ffn_in", "w_ffn_out"]
_OUTS = [("y_prompt", (1, SEQ, D)), ("y_sample", (1, DEC, D)), ("k_prompt", (1, 1, SEQ, BH, 2, BD_)),
         ("v_prompt", (1, 1, SEQ, BH, BV)), ("wkv_prompt", (1, 1, AH, AD, AD)), ("shift_prompt", (1, 1, 1, A_COLS)),
         ("k_sample", (1, 1, DEC, BH, 2, BD_)), ("v_sample", (1, 1, DEC, BH, BV)), ("wkv_sample", (1, 1, AH, AD, AD)),
         ("shift_sample", (1, 1, 1, A_COLS))]


def kernel(**inputs):
    import concourse.bacc as bacc
    from concourse.bass_utils import run_bass_kernel_spmd

    nc = bacc.Bacc("TRN2", target_bir_lowering=False, num_devices=1)
    arrays, ins, outs = {}, {}, {}
    for name in _INS:
        a = np.ascontiguousarray(inputs[name])
        arrays[f"in_{name}"] = a
        ins[name] = nc.dram_tensor(f"in_{name}", a.shape, F32, kind="ExternalInput").ap()
    arrays["in_cst"] = constants()
    ins["cst"] = nc.dram_tensor("in_cst", (P, K_N), F32, kind="ExternalInput").ap()
    for name, shape in _OUTS:
        outs[name] = nc.dram_tensor(f"out_{name}", shape, F32, kind="ExternalOutput").ap()
    encoder_kernel(nc, ins, outs)
    r = run_bass_kernel_spmd(nc, [arrays], core_ids=[0])
    return tuple(r.results[0][f"out_{name}"] for name, _ in _OUTS)
```

```python
import math
from contextlib import ExitStack

import numpy as np

import concourse.bass as bass
from concourse import mybir

ALU = mybir.AluOpType
ACT = mybir.ActivationFunctionType
AX = mybir.AxisListType
F32 = mybir.dt.float32
F32R = mybir.dt.float32r

P = 128
D = 1024
KT = D // P
SEQ, DEC, PAST = 512, 32, 128
TOK = SEQ + DEC
HALF = TOK // 2
J = TOK + 1
JS = SEQ + 1
CHUNK = 64
NCH = SEQ // CHUNK
EPS = 1e-6
NEG = -1e30
AH, AD = 8, 64
AW = AH * AD
CT = AW // P
GATE_LORA = 160
A_COLS = 3 * AW + 64 + 64 + GATE_LORA
GN_EPS = 64e-5
BH, BD_, BV = 4, 64, 128
BW = BH * BV
N_IN = A_COLS + 3 * BW + 2 * D
D_FF = ((8 * D + 3 * 256 - 1) // (3 * 256)) * 256
FT = D_FF // P
LAM_INIT = 0.8 - 0.6 * math.exp(0.0)
SCALE = BD_ ** -0.5
DECAY = math.exp(-0.5)
LEVELS = [2, 4, 8, 16, 32]
TILES = [(t * P, P) for t in range(SEQ // P)] + [(SEQ, DEC)]
NT = len(TILES)
SAMPLE = NT - 1

NC = 15
CCOL = [min(P * i, A_COLS - P) for i in range(NC)]
CR, CK, CV, CWA, CG, CG2 = 0, 4, 8, 12, 13, 14
G2P = P - 32

PV_SHIFT, PV_MU, PV_W0, PV_A0, PV_KK, PV_KA, PV_RK, PV_LNW, PV_LNB, PV_BG = 0, 15, 30, 34, 38, 42, 46, 50, 54, 58
PV_N = PV_BG + 2 * KT

K_ID, K_SC = 0, P
K_M0 = K_SC + 2 * P
K_LV = K_M0 + P
K_BD = K_LV + len(LEVELS) * 64
K_I64 = K_BD + P
K_SCAN = K_I64 + 64
K_N = K_SCAN + J


def constants():
    c = np.zeros((P, K_N), np.float32)
    j, i = np.meshgrid(np.arange(P), np.arange(P), indexing="ij")
    same = j // CHUNK == i // CHUNK
    c[:, K_ID:K_ID + P] = np.eye(P)
    c[:, K_SC:K_SC + P] = (j < i) & same
    c[:, K_SC + P:K_SC + 2 * P] = (j <= i) & same
    c[:, K_M0:K_M0 + P] = (i == j + 1) & (j % 2 == 0)
    row, col = np.meshgrid(np.arange(P), np.arange(64), indexing="ij")
    for n, s in enumerate(LEVELS):
        c[:, K_LV + 64 * n:K_LV + 64 * (n + 1)] = (row // (2 * s) == col // s) & (row % (2 * s) >= s)
    c[:, K_BD:K_BD + P] = j // 64 == i // 64
    c[:, K_I64:K_I64 + 64] = row % 64 == col
    c[:, K_SCAN:K_SCAN + J] = 1.0
    for n in range(NCH):
        c[:, K_SCAN + n * CHUNK] = 0.0
    c[:, K_SCAN + JS] = 0.0
    return c


DENSE = [("qkv", i) for i in range(12)] + [("c", i) for i in range(NC)]
DENSE += [(k, i) for k in ("gB", "gA", "outB", "outA", "wo") for i in range(8)]
FFN_BLOCK0 = len(DENSE)
DENSE += [(("ug", "uv")[i % 2], i // 2) for i in range(2 * FT)]
DENSE += [("down", i) for i in range(8)]
BLOCK = {d: n for n, d in enumerate(DENSE)}
DOWN_PARTS = [(0, 8), (8, 7), (15, 7)]

UNITS, SEGS = [], []
for _kind, _i in DENSE:
    if _kind in ("outA", "outB"):
        if _i % 2 == 0:
            UNITS.append((_kind, _i // 2, 0))
        SEGS.append((len(UNITS) - 1, _kind, _i))
    elif _kind == "down":
        for _p in range(3):
            UNITS.append((_kind, _i, _p))
            SEGS.append((len(UNITS) - 1, _kind, _i))
    else:
        UNITS.append((_kind, _i, 0))
        SEGS.append((len(UNITS) - 1, _kind, _i))
UNIT_END = {u: max(n for n, s in enumerate(SEGS) if s[0] == u) + 1 for u in range(len(UNITS))}
BLOCK_END = {d: max(n for n, s in enumerate(SEGS) if s[1:] == d) + 1 for d in DENSE}
UNIT_OF = {}
for _n, _s in enumerate(SEGS):
    UNIT_OF.setdefault(_s[1:], []).append((_s[0], _n))
FFN_UNIT0 = UNIT_OF[("ug", 0)][0][0]
FFN_SEG0 = UNIT_OF[("ug", 0)][0][1]
DOWN_UNIT0 = UNIT_OF[("down", 0)][0][0]

WKV = [(t, g) for t in range(NT) for g in range(2)]


BY_TOKENS = -2


def levels(t):
    return range(len(LEVELS) if t < SAMPLE else len(LEVELS) - 1)


def schedule():
    def dense(kind, i, part=0, parts=1):
        return ("dense", kind, i, part, parts)

    def skew(n, *stages):
        return [(st, i - k) for i in range(n + len(stages) - 1) for k, st in enumerate(stages) if 0 <= i - k < n]

    def first_pair(steps, blocks):
        halves = [("dense", *d, hf, BY_TOKENS) for hf in range(2) for d in blocks]
        return steps[:-2] + halves[:1] + steps[-2:-1] + halves[1:2] + steps[-1:] + halves[2:]

    s = first_pair(skew(NT, "normA", "normB"), [("qkv", 0), ("qkv", 1)]) + [("params",)]
    s += [dense("qkv", i) for i in range(2, 9)]
    s += [("ktok", 0), ("ktok", 1), dense("qkv", 9), ("ktok", 2), ("ktok", 3), dense("qkv", 10), ("ktok", 4), ("cache",)]
    pieces = [dense("c", i, p, 4) for i in range(NC) for p in range(4)]
    heads = [(t, h) for t in range(NT) for h in range(BH)]
    s += [dense("qkv", 11)] + [("vtok", t) for t in range(NT)]
    s += [("attS", *heads[0]), ("attC", *heads[0]), ("attS", *heads[1])]
    left = 0
    for i, th in enumerate(heads):
        s += pieces[:1] + [("attP", *th)] + pieces[1:2]
        if i + 2 < len(heads):
            s += [("attC", *heads[i + 1]), ("attS", *heads[i + 2])]
        elif i + 1 < len(heads):
            s += [("attC", *heads[i + 1])]
        s += pieces[2:3] + [("attO", *th)]
        pieces = pieces[3:]
        while left < NC and (left + 1) * 4 <= (i + 1) * 3 - 3:
            s += [("shift", left)]
            left += 1
    s += pieces + [("oscale",)] + [("shift", i) for i in range(left, NC)]
    gates = [dense(k, i) for k in ("gB", "gA") for i in range(8)]
    quarters = [dense("gB", 2, p, 4) for p in range(4)]
    s += gates[:1] + [("lora",)] + gates[1:2]
    for st in skew(NT, "oA", "ofin"):
        s += [st]
        if st[0] == "ofin":
            s += quarters[:1]
            quarters = quarters[1:]
    s += [("ksquare", c) for c in range(CT)] + gates[3:4] + [("shiftout",)]
    gates = gates[4:]
    s += [("knorm", 0), ("knorm", 1)] + gates[:1] + [("knorm", 2), ("knorm", 3)] + gates[1:3]
    s += [("krsqrt",), ("rwA", 0)] + gates[3:4] + [("rwA", 1), ("rwB", 0)] + gates[4:6] + [("rw2", 0)]
    gates = gates[6:]
    for c in range(1, CT):
        s += gates[:1] + ([("rwA", c + 1)] if c + 1 < CT else []) + [("rwB", c)] + gates[1:2] + [("rw2", c)]
        gates = gates[2:]
    fill = [dense("outB", i, p, 2) for i in range(8) for p in range(2)]

    def filler(n):
        out, fill[:n] = fill[:n], []
        return out

    for t in range(NT):
        s += [("init",)] if t == SAMPLE else []
        if t == 0:
            s += filler(1) + [("w", st, t, g) for g in range(2) for st in ("tok", "sb", "sk")]
        else:
            s += [("w", st, t, g) for st in ("tok", "sb", "sk") for g in range(2)]
        s += [("ymean", t - 1, g) for g in range(2)] if t else []
        s += filler(1 if t in (0, SAMPLE) else 0)
        for st in ("x0", "gv"):
            s += [("w", st, t, g) for g in range(2)]
        s += [("yvar", t - 1, g) for g in range(2)] if t else []
        for lv in levels(t):
            for st in ("wm", "wd", "wt"):
                s += [(st, lv, t, g) for g in range(2)]
            s += [("yfin", t - 1, lv - 1)] if t and lv in (1, 2) else []
            s += [("init0",)] if (t, lv) == (0, 1) else []
            s += filler(1) if t == SAMPLE else []
        for st in ("wu", "ef", "chain0", "q", "ya"):
            s += [("w", st, t, g) for g in range(2)]
        s += filler(1)
        for st in ("yb",) + (("chain1",) if t < SAMPLE else ()):
            s += [("w", st, t, g) for g in range(2)]
        if t >= SAMPLE - 1:
            s += [("final", t, g) for g in range(2)]
    for st in ("ymean", "yvar", "yfin"):
        s += [(st, SAMPLE, g) for g in range(2)]
        s += filler(1)
    s += [("ysplit", c) for c in range(CT)] + filler(len(fill))
    s += [dense("outA", i) for i in range(8)]
    for r, kind in enumerate(("wo", "down")):
        for i in range(8):
            s += [dense(kind, i)] + ([("ztok", r, i - 1)] if i else [])
        s += [("ztok", r, 7), ("zS", r)]
        s += first_pair(skew(NT, "zA0", "zB", "zC"), [("ug", 0), ("uv", 0)]) + [("ffn",)] if r == 0 else [("zA1", t) for t in range(NT)]
    return s


SCHEDULE = schedule()


def fills(step):
    k = step[0]
    if k == "params":
        return ["pv"]
    if k in ("normB", "zC"):
        return ["n0", "n1"]
    if k == "cache":
        return ["ck"]
    if k in ("ktok", "vtok"):
        return [k[0]]
    if k == "attS":
        return ["s0", "s1"]
    if k == "attP":
        return ["pt"]
    if k in ("ofin", "attO"):
        return ["o"]
    if k == "shiftout":
        return ["s"]
    if k == "knorm":
        return ["q0", "q1"]
    if k == "rwA":
        return ["w0", "w1", "a0", "a1"]
    if k == "rw2":
        return ["b0", "b1"]
    if k == "init":
        return ["s"]
    if k == "w":
        return {"tok": ["t0", "t1"], "sb": ["b0", "b1"], "sk": ["k0", "k1"], "ya": [], "gv": ["gv"], "x0": ["x"], "wu": ["wu"],
                "ef": ["e0", "e1"] if step[2] < SAMPLE else ["e0"], "chain0": ["c"], "chain1": ["c"],
                "q": ["q"], "yb": ["y"]}[step[1]]
    if k in ("wm", "wd", "wt"):
        return [k[1]]
    if k == "final":
        return ["f"]
    if k in ("ymean", "yvar"):
        return ["m"]
    if k == "yfin":
        return ["g"]
    if k == "ztok":
        return ["z0", "z1"]
    return []


FILL = {}
for _s in SCHEDULE:
    for _f in fills(_s):
        FILL[(_s, _f)] = len(FILL)


def encoder_kernel(nc, i_, o_):
    ctx = ExitStack()
    phase2 = ExitStack()
    region = ExitStack()

    def sb(name, shape, dt=F32, at=ctx):
        return at.enter_context(nc.sbuf_tensor(name, shape, dt))

    def sem(name):
        return ctx.enter_context(nc.semaphore(name))

    w_raw = sb("w_raw", [P, 2, D])
    w_hi = sb("w_hi", [P, 2, D], F32R)
    w_lo = sb("w_lo", [P, 2, D], F32R)
    gain = sb("gain", [P, D])
    pv = sb("pv", [P, PV_N])
    pvh = sb("pvh", [P, PV_N])
    ident = sb("ident", [P, P])
    ssq = sb("ssq", [P, NT])
    rms = sb("rms", [P, NT])
    rstd = sb("rstd", [P, NT])
    zsq = sb("zsq", [P, NT, KT])

    cst = sb("cst", [P, K_N], at=phase2)
    pv_rows = sb("pv_rows", [PV_N, P], at=phase2)
    oka = sb("oka", [P, CT], at=phase2)
    wa2 = sb("wa2", [P, AW], at=phase2)
    g2a = sb("g2a", [P, AW], at=phase2)
    g2b = sb("g2b", [P, AW], at=phase2)
    last = sb("last", [P, 2, NC], at=phase2)
    lastT = sb("lastT", [2 * NC, P], at=phase2)
    pend = sb("pend", [P, CT, NCH + 1], at=phase2)
    C = sb("C", [P, NC, J + 1], at=phase2)
    dtmp = sb("dtmp", [P, J], at=phase2)
    mb = sb("mb", [P, 8, TOK], at=phase2)
    h_hi = sb("h_hi", [P, KT, TOK], F32R, at=region)
    h_lo = sb("h_lo", [P, KT, TOK], F32R, at=region)
    region.close()
    lt = sb("lt", [P, 2, 4, 2 * P], at=phase2)
    gt = sb("gt", [P, 2, 4, 2 * P], at=phase2)
    X = sb("X", [P, 2, 4, P], at=phase2)
    XT = sb("XT", [P, 2, 4, P], at=phase2)
    ag = sb("ag", [P, 2, 4, 2, 64], at=phase2)
    wu = sb("wu", [P, 2, 4, 2, 64], at=phase2)
    mc = sb("mc", [P, 2, 4, 64], at=phase2)
    o_hi = sb("o_hi", [P, BH, TOK], F32R, at=phase2)
    o_lo = sb("o_lo", [P, BH, TOK], F32R, at=phase2)

    xs = sb("xs", [P, NT, D], at=region)
    xn = sb("xn", [P, 2, D], at=region)
    region.close()
    qkv = sb("qkv", [P, 12, TOK], at=region)
    vtok = sb("vtok", [P, NT, BW], at=region)
    otok = sb("otok", [P, NT, BW], at=region)
    kout = sb("kout", [P, 2, BW], at=region)
    ck_in = sb("ck_in", [P, BW], at=region)
    ckT = sb("ckT", [P, BH, P], at=region)
    cv = sb("cv", [P, BW], at=region)
    pT = sb("pT", [P, 2, BW], at=region)
    lamv = sb("lamv", [P, 5, BD_], at=region)
    lam2 = sb("lam2", [P, 4], at=region)
    nlam = sb("nlam", [P, 1], at=region)
    amax = sb("amax", [P, 4], at=region)
    asum = sb("asum", [P, 4], at=region)
    arec = sb("arec", [P, 4], at=region)
    ossq = sb("ossq", [P, NT * BH], at=region)
    orms = sb("orms", [P, NT * BH], at=region)
    orst = sb("orst", [P, NT * BH], at=region)
    subln = sb("subln", [P, BV], at=region)
    probs = qkv[:, 8:12, :].rearrange("p a t -> p (a t)")[:, 0:4 * BW].rearrange("p (b n t) -> p b n t", b=2, n=2)
    region.close()

    AR = sb("AR", [P, CT, 2, J], at=region)
    bonus = sb("bonus", [P, CT, J], at=region)
    ga = sb("ga", [P, 8, TOK], at=region)
    inner = ExitStack()
    tmp = sb("tmp", [P, 9, J], at=inner)
    inner.close()
    tok = sb("tok", [P, 2, 3, 4, 64], at=inner)
    ebd = sb("ebd", [P, 2, 2, 2, P], at=inner)
    ff = sb("ff", [P, 2, 2, 2, 64], at=inner)
    qT = sb("qT", [P, 2, 2, P], at=inner)
    mt = sb("mt", [P, 2, 2, 64], at=inner)
    mcur = sb("mcur", [P, 2, 2, 64], at=inner)
    mbd = sb("mbd", [P, 2, 2, 2, P], at=inner)
    sout = dtmp[:, 0:2 * 64].rearrange("p (k v) -> p k v", k=2)
    sio = C[:, CWA, 0:4 * P].rearrange("p (c k) -> p c k", c=CT)
    inner.close()
    y_hi = sb("y_hi", [P, CT, TOK], F32R, at=inner)
    y_lo = sb("y_lo", [P, CT, TOK], F32R, at=inner)
    inner.close()
    region.close()
    phase2.close()

    S = sb("S", [P, FT, 2, TOK], F32R)
    x1 = sb("x1", [P, NT, D])
    z = sb("z", [P, NT, D])
    zT = sb("zT", [P, TOK])
    gain2 = sb("gain2", [P, D])
    h2_hi = sb("h2_hi", [P, KT, TOK], F32R)
    h2_lo = sb("h2_lo", [P, KT, TOK], F32R)
    ftmp = z[:, :, :].rearrange("p t n -> p (t n)")
    f_t, f_s = ftmp[:, 0:TOK], ftmp[:, TOK:2 * TOK]

    dps = [ctx.enter_context(nc.psum_tensor(f"dense{i}", [P, 2, 512], F32)) for i in range(2)]
    side = [ctx.enter_context(nc.psum_tensor(f"side{i}", [P, 512], F32)) for i in range(4)]

    raw_loaded = [sem(f"raw_loaded{i}") for i in range(2)]
    hi_split, w_split = sem("hi_split"), sem("w_split")
    slot_ready = sem("slot_ready")
    seg_done = sem("seg_done")
    dense_read = [sem(f"dense_read{i}") for i in range(2)]
    filled = sem("filled")
    drained = [sem(f"drained{i}") for i in range(4)]
    vch, ach = sem("vector_chain"), sem("scalar_chain")
    stored = sem("stored")
    kout_stored = [sem(f"kout_stored{i}") for i in range(2)]
    names = """ident_loaded x_sq x_normed x_hi cst_loaded small_loaded att_loaded gain_loaded lam_prod lam_exp
        smax sattn o_rms o_scaled o_hi_done last_done shifted lora_a kinv shift_set rw_w rw_kk ksq ksqrt
        rw_g rw_p rw_gm rw_e2 rw_bo rw_done zeroed init_loaded xt_init st_bd y_sq y_hi_done y_done mixed
        mix_hi mix_done x1_loaded gain2_loaded z_sq z_sum zrms zres xrms xnorm z_hi f_tanh f_hi f_lo"""
    s_ = {n: sem(n) for n in names.split()}
    x_sems = [sem(f"x_loaded{t}") for t in range(NT)]

    def bank(step, f):
        return side[FILL[(step, f)] % 4]

    def open_bank(pe, step, f):
        n = FILL[(step, f)]
        if n >= 4:
            pe.wait_ge(drained[n % 4], n // 4)
        return side[n % 4]

    def full_bank(eng, step, f):
        n = FILL[(step, f)]
        eng.wait_ge(filled, n + 1)
        return side[n % 4]

    def drain_sem(step, f):
        return drained[FILL[(step, f)] % 4]

    def landed(eng, step, f):
        n = FILL[(step, f)]
        eng.wait_ge(drained[n % 4], n // 4 + 1)

    def block_full(eng, d):
        eng.wait_ge(seg_done, BLOCK_END[d])
        return dps[BLOCK[d] % 2]

    def block_sem(d):
        return dense_read[BLOCK[d] % 2]

    def block_landed(eng, d):
        eng.wait_ge(dense_read[BLOCK[d] % 2], BLOCK[d] // 2 + 1)

    class Chain:
        def __init__(self, eng, s):
            self.eng, self.s, self.count = eng, s, {}

        def __call__(self, ins):
            self.mark(ins, self.s, "")

        def mark(self, ins, s, name):
            self.count[name] = self.count.get(name, 0) + 1
            ins.then_inc(s, 1)
            self.eng.wait_ge(s, self.count[name])

    def x_rows(t):
        return i_["x_prompt"][0, t * P:(t + 1) * P, :] if t < SAMPLE else i_["x_sample"][0, :, :]

    def y_rows(t):
        return o_["y_prompt"][0, t * P:(t + 1) * P, :] if t < SAMPLE else o_["y_sample"][0, :, :]

    w_in = i_["w_in"][0].rearrange("(k p) n -> p k n", p=P)
    w_oa = i_["w_out_a"][0].rearrange("(k p) n -> p k n", p=P)
    w_ob = i_["w_out_b"][0].rearrange("(k p) n -> p k n", p=P)
    w_o = i_["w_o"][0].rearrange("(k p) n -> p k n", p=P)
    w_fi = i_["w_ffn_in"][0].rearrange("(k p) n -> p k n", p=P)
    w_fo = i_["w_ffn_out"][0].rearrange("(k p) n -> p k n", p=P)
    COL0 = {"qkv": A_COLS, "gB": A_COLS + 3 * BW + D, "gA": A_COLS + 3 * BW}

    block = ctx.enter_context(nc.Block())

    def st_count(t, ch, g):
        return 4 * t + 2 * ch + g + 1

    def key_tiles(t):
        return [(kt * P, P) for kt in range(t + 1)] if t < SAMPLE else [(0, PAST), (PAST, DEC)]

    def chunks(t):
        return [(c, CHUNK) for c in range(2)] if t < SAMPLE else [(0, DEC)]

    def first(t):
        return TILES[t][0] if t < SAMPLE else JS

    N_SMALL, N_ATT = 16, 7

    @block.sync
    def _(sp):
        def rows(ap2, r0, n):
            sp.dma_start(pv_rows[r0:r0 + n, :], ap2).then_inc(s_["small_loaded"], 16)

        def load_parameters():
            sp.dma_start(cst[:, :], i_["cst"][:, :]).then_inc(s_["cst_loaded"], 16)
            for ap1, r0 in ((i_["state_shift"][0, 0, 0], PV_SHIFT), (i_["rwkv_mu"][0], PV_MU)):
                rows(ap1[0:14 * P].rearrange("(r c) -> r c", c=P), r0, 14)
                rows(ap1[A_COLS - P:A_COLS].rearrange("(r c) -> r c", c=P), r0 + 14, 1)
            for name, r0, n in (("rwkv_w0", PV_W0, 4), ("rwkv_a0", PV_A0, 4), ("rwkv_k_k", PV_KK, 4), ("rwkv_k_a", PV_KA, 4),
                                ("rwkv_ln_w", PV_LNW, 4), ("rwkv_ln_b", PV_LNB, 4), ("b_gate", PV_BG, 16)):
                rows(i_[name][0].rearrange("(r c) -> r c", c=P), r0, n)
            rows(i_["rwkv_r_k"][0].rearrange("(r a) c -> r (a c)", a=2), PV_RK, 4)
            sp.dma_start(wa2[0:64, :], i_["rwkv_w2"][0]).then_inc(s_["small_loaded"], 16)
            sp.dma_start(wa2[64:P, :], i_["rwkv_a2"][0]).then_inc(s_["small_loaded"], 16)
            sp.dma_start(g2a[:, :], i_["rwkv_g2"][0, 0:P, :]).then_inc(s_["small_loaded"], 16)
            sp.dma_start(g2b[G2P:P, :], i_["rwkv_g2"][0, P:GATE_LORA, :]).then_inc(s_["small_loaded"], 16)
            sp.dma_start(ck_in[:, :], i_["cache_k"][0, 0].rearrange("t h n d -> t (h n d)")).then_inc(s_["att_loaded"], 16)
            sp.dma_start(cv[:, :], i_["cache_v"][0, 0].rearrange("t h e -> t (h e)")).then_inc(s_["att_loaded"], 16)
            for n, name in enumerate(("diff_lq1", "diff_lk1", "diff_lq2", "diff_lk2")):
                sp.dma_start(lamv[:, n, :], i_[name][0].partition_broadcast(P)).then_inc(s_["att_loaded"], 16)
            sp.dma_start(subln[:, :], i_["diff_subln"][0].partition_broadcast(P)).then_inc(s_["att_loaded"], 16)

        for t in range(NT):
            sp.dma_start(xs[0:TILES[t][1], t, :], x_rows(t)).then_inc(x_sems[t], 16)
            if t == 0:
                sp.dma_start(gain[:, :], i_["norm_mix_pre"][0].partition_broadcast(P)).then_inc(s_["gain_loaded"], 16)
        for u, (kind, n, part) in enumerate(UNITS):
            if u == 2:
                load_parameters()
            slot = u % 2
            if FFN_UNIT0 <= u < DOWN_UNIT0:
                if u == FFN_UNIT0:
                    with sp.Fori(0, FT) as f:
                        for k in range(2):
                            s2 = (FFN_UNIT0 + k) % 2
                            sp.wait_ge(w_split, f * 2 + (FFN_UNIT0 + k - 1))
                            sp.dma_start(w_raw[:, s2, :].rearrange("p (k n) -> p k n", k=KT),
                                         w_fi[:, :, bass.ds(f * P + k * D_FF, P)]).then_inc(raw_loaded[s2], 16)
                continue
            if u >= 2:
                sp.wait_ge(w_split, u - 1)
            dst = w_raw[:, slot, :]
            if kind in ("qkv", "gA", "gB", "c"):
                c0 = CCOL[n] if kind == "c" else COL0[kind] + n * P
                sp.dma_start(dst.rearrange("p (k n) -> p k n", k=KT), w_in[:, :, c0:c0 + P]).then_inc(raw_loaded[slot], 16)
            elif kind in ("outA", "outB"):
                w = w_oa if kind == "outA" else w_ob
                sp.dma_start(dst.rearrange("p (k n) -> p k n", k=CT), w[:, :, n * 256:(n + 1) * 256]).then_inc(
                    raw_loaded[slot], 16)
            elif kind == "wo":
                sp.dma_start(dst.rearrange("p (k n) -> p k n", k=KT), w_o[:, :, n * P:(n + 1) * P]).then_inc(
                    raw_loaded[slot], 16)
            else:
                k0, kn = DOWN_PARTS[part]
                sp.dma_start(dst[:, 0:kn * P].rearrange("p (k n) -> p k n", k=kn),
                             w_fo[:, k0:k0 + kn, n * P:(n + 1) * P]).then_inc(raw_loaded[slot], 16)

    @block.gpsimd
    def _(pool):
        def split(slot):
            nc.gpsimd.tensor_scalar(w_hi[:, slot, :], w_raw[:, slot, :], 1.0, 0.0, ALU.mult, ALU.add).then_inc(hi_split, 1)

        def split_lo(slot):
            nc.gpsimd.tensor_tensor(w_lo[:, slot, :], w_raw[:, slot, :], w_hi[:, slot, :].bitcast(F32),
                                    ALU.subtract).then_inc(w_split, 1)

        def unit(u):
            pool.wait_ge(raw_loaded[u % 2], 16 * (u // 2 + 1))
            if u >= 2:
                pool.wait_ge(seg_done, UNIT_END[u - 2])
            split(u % 2)
            pool.wait_ge(hi_split, u + 1)
            split_lo(u % 2)

        for u in range(FFN_UNIT0 + 2):
            unit(u)
        with pool.Fori(1, FT) as f:
            for k in range(2):
                u0 = FFN_UNIT0 + k
                pool.wait_ge(raw_loaded[u0 % 2], (f + (u0 // 2 + 1)) * 16)
                pool.wait_ge(seg_done, f * 2 + (FFN_SEG0 + k - 1))
                pool.sem_inc(slot_ready, 1)
                split(u0 % 2)
                pool.wait_ge(hi_split, f * 2 + (u0 + 1))
                split_lo(u0 % 2)
        for u in range(DOWN_UNIT0, len(UNITS)):
            unit(u)

    def ffn_mm(pe, three, b, u):
        for n in range(KT):
            ins = three(dps[b % 2], w_hi[:, u % 2, n * P:(n + 1) * P], w_lo[:, u % 2, n * P:(n + 1) * P],
                        h2_hi[:, n, :], h2_lo[:, n, :], n == 0, n == KT - 1)
        ins.then_inc(seg_done, 1)

    def wkv_pe(pe, step, transposes, close):
        t, g = step[2], step[3]
        n, j0 = TILES[t][1], first(t)
        heads = [(c, p) for c in range(2) for p in range(2)]
        if step[0] in ("wm", "wd", "wt"):
            lv = step[1]
            s = LEVELS[lv]
        if step[0] == "wm":
            b = open_bank(pe, step, "m")
            landed(pe, ("w", "x0", t, g), "x")
            if lv:
                landed(pe, ("wd", lv - 1, t, g), "d")
            for h in range(4):
                rhs = X[0:n, g, h, 0:n].rearrange("p (b u s) -> p b u s", u=2, s=s)[:, :, 0, :]
                out = b[0:n, h * 64:h * 64 + n // 2].rearrange("p (b s) -> p b s", s=s)
                ins = pe.matmul(out, lt[0:n, g, h, 0:n], rhs, start=True, stop=True)
            close(ins, step, "m")
            return
        if step[0] == "wd":
            b = open_bank(pe, step, "d")
            landed(pe, ("wm", lv, t, g), "m")
            if lv:
                landed(pe, ("wt", lv - 1, t, g), "t")
            for h in range(4):
                ins = pe.matmul(b[0:n, h * 64:h * 64 + n // 2], XT[0:n, g, h, 0:n], mc[0:n, g, h, 0:n // 2],
                                start=True, stop=True)
            close(ins, step, "d")
            return
        if step[0] == "wt":
            landed(pe, ("wd", lv, t, g), "d")
            transposes(step, "t", [(h * n, X[0:n, g, h, 0:n]) for h in range(4)])
            return
        st = step[1]
        if st == "tok":
            if t == 0:
                pe.wait_ge(s_["rw_done"], 3 + g)
            transposes(step, "t0", [((2 * q + c) * P, C[:, blk + 2 * g + c, 1 + j0:1 + j0 + n])
                                    for q, blk in enumerate((CR, CK)) for c in range(2)])
            transposes(step, "t1", [(c * P, C[:, CV + 2 * g + c, 1 + j0:1 + j0 + n]) for c in range(2)]
                       + [((2 + c) * P, AR[:, 2 * g + c, 0, j0:j0 + n]) for c in range(2)])
        elif st in ("sb", "sk"):
            f, blk = ("b", CR) if st == "sb" else ("k", CK)
            for p in range(2):
                b = open_bank(pe, step, f"{f}{p}")
                lo, hi = 64 * p, 64 * p + 64
                for c in range(2):
                    ins = pe.matmul(b[0:n, c * 2 * n:(c + 1) * 2 * n].rearrange("p (u i) -> p u i", u=2),
                                    C[lo:hi, blk + 2 * g + c, 1 + j0:1 + j0 + n], AR[lo:hi, 2 * g + c, :, j0:j0 + n],
                                    start=True, stop=True)
                close(ins, step, f"{f}{p}")
        elif st == "gv":
            b = open_bank(pe, step, "gv")
            landed(pe, ("w", "tok", t, g), "t1")
            landed(pe, ("w", "sk", t, g), "k0")
            landed(pe, ("w", "sk", t, g), "k1")
            for h in range(4):
                ins = pe.matmul(b[0:n, h * 64:(h + 1) * 64], gt[0:n, g, h, 0:n], tok[0:n, g, 2, h, :], start=True, stop=True)
            close(ins, step, "gv")
        elif st == "x0":
            pe.wait_ge(s_["xt_init"], 2 * t + g + 1)
            transposes(step, "x", [(h * n, XT[0:n, g, h, 0:n]) for h in range(4)])
        elif st == "wu":
            b = open_bank(pe, step, "wu")
            landed(pe, ("wt", levels(t)[-1], t, g), "t")
            landed(pe, ("w", "gv", t, g), "gv")
            for h in range(4):
                ins = pe.matmul(b[0:n, h * P:(h + 1) * P], XT[0:n, g, h, 0:n],
                                ag[0:n, g, h, :, :].rearrange("p u v -> p (u v)"), start=True, stop=True)
            close(ins, step, "wu")
        elif st == "ef":
            landed(pe, ("w", "wu", t, g), "wu")
            landed(pe, ("w", "tok", t, g), "t0")
            for ch, ln in chunks(t):
                b = open_bank(pe, step, f"e{ch}")
                r0, r1 = 64 * ch, 64 * ch + ln
                for c, p in heads:
                    h = 2 * c + p
                    out = b[64 * p:64 * p + 64, c * P:(c + 1) * P]
                    pe.matmul(out[:, 0:64], wu[r0:r1, g, h, 0, :], tok[r0:r1, g, 0, h, :], start=True, stop=True)
                    pe.matmul(out[:, 64:P], tok[r0:r1, g, 0, h, :], wu[r0:r1, g, h, 1, :], start=True, stop=False)
                    ins = pe.matmul(out[:, 64:P], tok[r0:r1, g, 1, h, :], tok[r0:r1, g, 2, h, :], start=False, stop=True)
                close(ins, step, f"e{ch}")
        elif st in ("chain0", "chain1"):
            ch = int(st[-1])
            b = open_bank(pe, step, "c")
            landed(pe, ("w", "ef", t, g), f"e{ch}")
            if t == SAMPLE:
                landed(pe, ("init",), "s")
            elif (t, ch) == (0, 0):
                pe.wait_ge(s_["zeroed"], 1)
            else:
                pe.wait_ge(s_["st_bd"], st_count(t - 1 + ch, 1 - ch, g))
            for c in range(2):
                ins = pe.matmul(b[:, c * 64:(c + 1) * 64], ebd[:, g, ch, c, :], mcur[:, g, c, :], start=True, stop=True)
            close(ins, step, "c")
        elif st == "q":
            b = open_bank(pe, step, "q")
            for p in range(2):
                landed(pe, ("w", "sb", t, g), f"b{p}")
            for c, p in heads:
                h = 2 * c + p
                ins = pe.matmul(b[64 * p:64 * p + 64, c * n:(c + 1) * n], wu[0:n, g, h, 0, :], lt[0:n, g, h, P:P + n],
                                start=True, stop=True)
            close(ins, step, "q")
        elif st == "ya":
            b = open_bank(pe, ("w", "yb", t, g), "y")
            for c, p in heads:
                h = 2 * c + p
                out = b[64 * p:64 * p + 64, c * n:(c + 1) * n]
                pe.matmul(out, wu[0:n, g, h, 1, :], lt[0:n, g, h, P:P + n], start=c == 0, stop=False,
                          skip_group_check=c > 0)
                pe.matmul(out, tok[0:n, g, 2, h, :], gt[0:n, g, h, P:P + n], start=False, stop=True,
                          skip_group_check=c > 0)
        elif st == "yb":
            b = bank(step, "y")
            landed(pe, ("w", "q", t, g), "q")
            for ch, ln in chunks(t):
                if ch:
                    pe.wait_ge(s_["st_bd"], st_count(t, 0, g))
                for c in range(2):
                    ins = pe.matmul(b[:, c * n + 64 * ch:c * n + 64 * ch + ln], mbd[:, g, ch, c, :],
                                    qT[:, g, c, 64 * ch:64 * ch + ln], start=False, stop=True, skip_group_check=True)
            close(ins, step, "y")

    @block.tensor
    def _(pe):
        count = [0]

        def close(ins, step, f):
            assert FILL[(step, f)] == count[0], (step, f)
            count[0] += 1
            ins.then_inc(filled, 1)

        def three(acc, whi, wlo, rhi, rlo, first, final, halves=(0, 1)):
            for n, (w, r) in enumerate(((whi, rhi), (whi, rlo), (wlo, rhi))):
                for hf in halves:
                    ins = pe.matmul(acc[:, hf, 0:HALF], w, r[:, hf * HALF:(hf + 1) * HALF],
                                    start=first and n == 0, stop=final and n == 2)
            return ins

        def dense(kind, i, part, parts_):
            d = (kind, i)
            b = BLOCK[d]
            if parts_ == BY_TOKENS:
                landed(pe, ("normB" if kind == "qkv" else "zC", (2, SAMPLE)[part]), "n1")
                pe.wait_ge(s_["x_sq" if kind == "qkv" else "xrms"], NT)
            if kind == "outB":
                landed(pe, ("ofin", SAMPLE), "o")
            if b >= 2 and part == 0:
                pe.wait_ge(dense_read[b % 2], b // 2)
            acc = dps[b % 2]
            parts = UNIT_OF[d]
            for p, (u, seg) in enumerate(parts):
                pe.wait_ge(w_split, u + 1)
                if kind in ("outA", "outB"):
                    hi, lo = (y_hi, y_lo) if kind == "outA" else (o_hi, o_lo)
                    ops = [(k * 256 + (i % 2) * P, hi[:, k, :], lo[:, k, :]) for k in range(CT)]
                elif kind == "wo":
                    ops = [(k * P, S[:, k, 0, :], S[:, k, 1, :]) for k in range(KT)]
                elif kind == "down":
                    k0, kn = DOWN_PARTS[p]
                    ops = [(k * P, S[:, k0 + k, 0, :], S[:, k0 + k, 1, :]) for k in range(kn)]
                else:
                    hi, lo = (h2_hi, h2_lo) if kind in ("ug", "uv") else (h_hi, h_lo)
                    ops = [(k * P, hi[:, k, :], lo[:, k, :]) for k in range(KT)]
                here = range(len(ops) * part // parts_, len(ops) * (part + 1) // parts_) if parts_ > 0 else range(len(ops))
                for n in here:
                    if kind == "outA" and i == 0:
                        pe.wait_ge(s_["y_done"], 2 * (n + 1))
                    if kind == "wo" and i == 0:
                        pe.wait_ge(s_["mix_done"], n + 1)
                    if kind == "down" and i == 0:
                        pe.wait_ge(s_["f_lo"], DOWN_PARTS[p][0] + n + 1)
                    c, rh, rl = ops[n]
                    ins = three(acc, w_hi[:, u % 2, c:c + P], w_lo[:, u % 2, c:c + P], rh, rl,
                                p == 0 and n == 0, p == len(parts) - 1 and n == len(ops) - 1,
                                (0, 1) if parts_ > 0 else (part,))
                if part == abs(parts_) - 1:
                    ins.then_inc(seg_done, 1)

        def transposes(step, f, pieces):
            b = open_bank(pe, step, f)
            for c0, src in pieces:
                n, m = src.shape[0], src.shape[1]
                ins = pe.transpose(b[0:m, c0:c0 + n], src, ident[0:n, 0:n])
            close(ins, step, f)

        pe.wait_ge(s_["ident_loaded"], 16)
        for step in SCHEDULE:
            k = step[0]
            if k == "dense":
                dense(*step[1:])
            elif k == "params":
                pe.wait_ge(s_["cst_loaded"], 16)
                pe.wait_ge(s_["small_loaded"], 16 * N_SMALL)
                transposes(step, "pv", [(0, pv_rows[:, :])])
            elif k == "normB":
                t = step[1]
                n = TILES[t][1]
                pe.wait_ge(s_["x_normed"], t + 1)
                for i in range(2):
                    transposes(step, f"n{i}", [(kk * n, xn[0:n, t % 2, (4 * i + kk) * P:(4 * i + kk + 1) * P])
                                               for kk in range(4)])
            elif k == "cache":
                pe.wait_ge(s_["att_loaded"], 16 * N_ATT)
                transposes(step, "ck", [(h * P, ck_in[:, h * P:(h + 1) * P]) for h in range(BH)])
            elif k in ("ktok", "vtok"):
                t0, n = TILES[step[1]]
                b0 = 4 if k == "ktok" else 8
                block_landed(pe, ("qkv", b0 + 2))
                block_landed(pe, ("qkv", b0 + 3))
                transposes(step, k[0], [(h * P, qkv[:, b0 + h, t0:t0 + n]) for h in range(BH)])
            elif k == "attS":
                _, t, h = step
                t0, n = TILES[t]
                keys = t0 + n if t < SAMPLE else PAST + DEC
                if (t, h) == (0, 0):
                    block_landed(pe, ("qkv", 7))
                if t == SAMPLE and h == 0:
                    landed(pe, ("cache",), "ck")
                for m in range(2):
                    b = open_bank(pe, step, f"s{m}")
                    lo, hi = 64 * m, 64 * m + 64
                    q = qkv[lo:hi, h, t0:t0 + n]
                    if t < SAMPLE:
                        ins = pe.matmul(b[0:n, 0:keys], q, qkv[lo:hi, 4 + h, 0:keys], start=True, stop=True)
                    else:
                        pe.matmul(b[0:n, 0:PAST], q, ckT[lo:hi, h, :], start=True, stop=True)
                        ins = pe.matmul(b[0:n, PAST:keys], q, qkv[lo:hi, 4 + h, t0:t0 + n], start=True, stop=True)
                    close(ins, step, f"s{m}")
            elif k == "attP":
                _, t, h = step
                n = TILES[t][1]
                pb = (t * BH + h) % 2
                pe.wait_ge(s_["sattn"], t * BH + h + 1)
                transposes(step, "pt", [(i * n, probs[0:n, pb, 0, c0:c0 + kn]) for i, (c0, kn) in enumerate(key_tiles(t))])
            elif k == "attO":
                _, t, h = step
                n = TILES[t][1]
                pb = (t * BH + h) % 2
                b = open_bank(pe, step, "o")
                landed(pe, ("attP", t, h), "pt")
                if h == 0:
                    landed(pe, ("vtok", t), "v")
                kts = key_tiles(t)
                for i, (c0, kn) in enumerate(kts):
                    if t < SAMPLE:
                        v = vtok[0:P, i, h * BV:(h + 1) * BV]
                    else:
                        v = cv[:, h * BV:(h + 1) * BV] if i == 0 else vtok[0:DEC, SAMPLE, h * BV:(h + 1) * BV]
                    ins = pe.matmul(b[0:n, 0:BV], pT[0:kn, pb, i * n:(i + 1) * n], v,
                                    start=i == 0, stop=i == len(kts) - 1)
                close(ins, step, "o")
            elif k == "ofin":
                t0, n = TILES[step[1]]
                pe.wait_ge(s_["o_scaled"], step[1] + 1)
                transposes(step, "o", [(h * n, otok[0:n, step[1], h * BV:(h + 1) * BV]) for h in range(BH)])
            elif k == "shiftout":
                pe.wait_ge(s_["last_done"], 1)
                transposes(step, "s", [(0, last[:, :, :].rearrange("p g c -> p (g c)"))])
            elif k == "knorm":
                c = step[1]
                pe.wait_ge(s_["ksq"], c + 1)
                for i, (a, b_) in enumerate(((0, HALF), (HALF, J))):
                    b = open_bank(pe, step, f"q{i}")
                    close(pe.matmul(b[:, 0:b_ - a], cst[:, K_BD:K_BD + P], AR[:, c, 0, a:b_], start=True, stop=True),
                          step, f"q{i}")
            elif k == "rwA":
                c = step[1]
                if c == 0:
                    pe.wait_ge(s_["lora_a"], 1)
                for f, lo in (("w", 0), ("a", 64)):
                    for i, (a, b_) in enumerate(((0, HALF), (HALF, J))):
                        b = open_bank(pe, step, f"{f}{i}")
                        close(pe.matmul(b[:, 0:b_ - a], wa2[lo:lo + 64, c * P:(c + 1) * P],
                                        C[lo:lo + 64, CWA, 1 + a:1 + b_], start=True, stop=True), step, f"{f}{i}")
            elif k == "rw2":
                c = step[1]
                pe.wait_ge(s_["rw_bo"], c + 1)
                for i, (a, b_) in enumerate(((0, HALF), (HALF, J))):
                    b = open_bank(pe, step, f"b{i}")
                    close(pe.matmul(b[:, 0:b_ - a], cst[:, K_BD:K_BD + P], tmp[:, 8, a:b_], start=True, stop=True),
                          step, f"b{i}")
            elif k == "init":
                pe.wait_ge(s_["init_loaded"], 32)
                transposes(step, "s", [(c * P, sio[:, c, :]) for c in range(CT)])
            elif k in ("w", "wm", "wd", "wt"):
                wkv_pe(pe, step, transposes, close)
            elif k == "final":
                _, t, g = step
                pe.wait_ge(s_["st_bd"], st_count(t, len(chunks(t)) - 1, g))
                transposes(step, "f", [(c * P, mbd[:, g, len(chunks(t)) % 2, c, :]) for c in range(2)])
            elif k in ("ymean", "yvar"):
                _, t, g = step
                n, j0 = TILES[t][1], first(t)
                if k == "ymean":
                    landed(pe, ("w", "yb", t, g), "y")
                else:
                    pe.wait_ge(s_["y_sq"], 2 * t + g + 1)
                b = open_bank(pe, step, "m")
                close(pe.matmul(b[:, 0:2 * n].rearrange("p (c i) -> p c i", c=2), cst[:, K_BD:K_BD + P],
                                AR[:, 2 * g:2 * g + 2, int(k == "ymean"), j0:j0 + n], start=True, stop=True), step, "m")
            elif k == "yfin":
                _, t, g = step
                n, j0 = TILES[t][1], first(t)
                b = open_bank(pe, step, "g")
                for c in range(2):
                    o0 = (2 * g + c) * P
                    pe.matmul(b[:, c * n:(c + 1) * n], g2a[:, o0:o0 + P], C[:, CG, 1 + j0:1 + j0 + n], start=True, stop=False)
                    ins = pe.matmul(b[:, c * n:(c + 1) * n], g2b[G2P:P, o0:o0 + P], C[G2P:P, CG2, 1 + j0:1 + j0 + n],
                                    start=False, stop=True)
                close(ins, step, "g")
            elif k == "ztok":
                _, r, i = step
                block_landed(pe, ("wo" if r == 0 else "down", i))
                transposes(step, "z0", [(t * P, zT[:, t * P:(t + 1) * P]) for t in range(4)])
                transposes(step, "z1", [(0, zT[:, SEQ:TOK])])
            elif k == "zC":
                t, n = step[1], TILES[step[1]][1]
                pe.wait_ge(s_["xnorm"], t + 1)
                for i in range(2):
                    transposes(step, f"n{i}", [(kk * n, z[0:n, t, (4 * i + kk) * P:(4 * i + kk + 1) * P])
                                               for kk in range(4)])
            elif k == "ffn":
                with pe.Fori(1, FT) as f:
                    for kk in range(2):
                        b = FFN_BLOCK0 + kk
                        pe.wait_ge(dense_read[b % 2], f + b // 2)
                        pe.wait_ge(w_split, f * 2 + (FFN_UNIT0 + kk + 1))
                        ffn_mm(pe, three, b, FFN_UNIT0 + kk)

    @block.scalar
    def _(act):
        A = Chain(act, ach)
        n_stored = [0]
        f_act = nc.scalar.activation

        def store(dst, src):
            act.dma_start(dst, src).then_inc(stored, 16)
            n_stored[0] += 1

        def drain(ins, step, f):
            ins.then_inc(drain_sem(step, f), 1)

        def halves(hi, step, f, t0, n, name, k0):
            b = full_bank(act, step, f)
            f_act(hi[:, k0:k0 + 4, t0:t0 + n], b[:, 0:4 * n].rearrange("p (k n) -> p k n", k=4), ACT.Copy).then_inc(
                s_[name], 1)

        act.dma_start(ident[:, :], i_["cst"][:, K_ID:K_ID + P]).then_inc(s_["ident_loaded"], 16)
        for step in SCHEDULE:
            k = step[0]
            if k == "params":
                b = full_bank(act, step, "pv")
                A(f_act(pvh[:, :], b[:, 0:PV_N], ACT.Copy, scale=0.5))
                drain(f_act(pv[:, :], b[:, 0:PV_N], ACT.Copy), step, "pv")
            elif k == "normA":
                t = step[1]
                t0, n = TILES[t]
                act.wait_ge(x_sems[t], 16)
                A(f_act(dps[0][0:n, :, :], xs[0:n, t, :].rearrange("p (a b) -> p a b", a=2), ACT.Square,
                        accum_out=ssq[0:n, t:t + 1]))
                A.mark(f_act(rms[0:n, t:t + 1], ssq[0:n, t:t + 1], ACT.Sqrt, scale=1.0 / D, bias=EPS), s_["x_sq"], "x_sq")
            elif k == "normB":
                for i in range(2):
                    halves(h_hi, step, f"n{i}", *TILES[step[1]], "x_hi", 4 * i)
            elif k == "cache":
                act.wait_ge(s_["lam_prod"], 2)
                A.mark(f_act(lam2[:, 2:4], lam2[:, 0:2], ACT.Exp), s_["lam_exp"], "lam_exp")
                b = full_bank(act, step, "ck")
                drain(f_act(ckT[:, :, :], b[:, 0:BW].rearrange("p (h t) -> p h t", h=BH), ACT.Copy), step, "ck")
            elif k == "ktok":
                t = step[1]
                t0, n = TILES[t]
                if t >= 2:
                    act.wait_ge(kout_stored[t % 2], 16 * (t // 2))
                b = full_bank(act, step, "k")
                drain(f_act(kout[0:n, t % 2, :], b[0:n, 0:BW], ACT.Copy), step, "k")
                landed(act, step, "k")
                kd, r0 = (o_["k_prompt"], t0) if t < SAMPLE else (o_["k_sample"], 0)
                act.dma_start(kd[0, 0, r0:r0 + n].rearrange("t h n d -> t (h n d)"), kout[0:n, t % 2, :]).then_inc(
                    kout_stored[t % 2], 16)
            elif k == "vtok":
                t = step[1]
                t0, n = TILES[t]
                landed(act, step, "v")
                vd, r0 = (o_["v_prompt"], t0) if t < SAMPLE else (o_["v_sample"], 0)
                store(vd[0, 0, r0:r0 + n].rearrange("t h e -> t (h e)"), vtok[0:n, t, :])
            elif k == "attS":
                _, t, h = step
                t0, n = TILES[t]
                idx = t * BH + h
                pb = idx % 2
                keys = t0 + n if t < SAMPLE else PAST + DEC
                for m in range(2):
                    b = full_bank(act, step, f"s{m}")
                    act.wait_ge(s_["smax"], 2 * idx + m + 1)
                    drain(f_act(probs[0:n, pb, m, 0:keys], b[0:n, 0:keys], ACT.Exp, bias=amax[0:n, 2 * pb + m:2 * pb + m + 1],
                                scale=SCALE, accum_out=asum[0:n, 2 * pb + m:2 * pb + m + 1]), step, f"s{m}")
            elif k == "attP":
                _, t, h = step
                n = TILES[t][1]
                pb = (t * BH + h) % 2
                b = full_bank(act, step, "pt")
                if t < SAMPLE:
                    drain(f_act(pT[:, pb, 0:(t + 1) * n], b[:, 0:(t + 1) * n], ACT.Copy), step, "pt")
                else:
                    f_act(pT[:, pb, 0:n], b[:, 0:n], ACT.Copy).then_inc(ach, 1)
                    A.count[""] = A.count.get("", 0) + 1
                    drain(f_act(pT[0:DEC, pb, n:2 * n], b[0:DEC, n:2 * n], ACT.Copy), step, "pt")
            elif k == "attO":
                _, t, h = step
                n, idx = TILES[t][1], t * BH + h
                b = full_bank(act, step, "o")
                A(f_act(otok[0:n, t, h * BV:(h + 1) * BV], b[0:n, 0:BV], ACT.Copy))
                drain(f_act(b[0:n, 0:BV], b[0:n, 0:BV], ACT.Square, accum_out=ossq[0:n, idx:idx + 1]), step, "o")
            elif k == "oscale":
                landed(act, ("attO", SAMPLE, BH - 1), "o")
                A.mark(f_act(orms[:, 0:SAMPLE * BH], ossq[:, 0:SAMPLE * BH], ACT.Sqrt, scale=1.0 / BV, bias=EPS),
                       s_["o_rms"], "o_rms")
                A.mark(f_act(orms[0:DEC, SAMPLE * BH:], ossq[0:DEC, SAMPLE * BH:], ACT.Sqrt, scale=1.0 / BV, bias=EPS),
                       s_["o_rms"], "o_rms")
            elif k == "ofin":
                halves(o_hi, step, "o", *TILES[step[1]], "o_hi_done", 0)
            elif k == "shiftout":
                b = full_bank(act, step, "s")
                drain(f_act(lastT[:, :], b[0:2 * NC, 0:P], ACT.Copy), step, "s")
                landed(act, step, "s")
                for g, name in enumerate(("shift_prompt", "shift_sample")):
                    dst = o_[name][0, 0, 0]
                    store(dst[0:14 * P].rearrange("(r c) -> r c", c=P), lastT[g * NC:g * NC + 14, :])
                    store(dst[14 * P:A_COLS].rearrange("(r c) -> r c", c=A_COLS - 14 * P), lastT[g * NC + 14:g * NC + 15, G2P:P])
            elif k == "lora":
                act.wait_ge(s_["shifted"], NC)
                A(f_act(C[0:64, CWA, 1:1 + J], C[0:64, CWA, 1:1 + J], ACT.Tanh))
                A(f_act(C[:, CG, 1:1 + J], C[:, CG, 1:1 + J], ACT.Tanh, scale=0.5))
                A.mark(f_act(C[G2P:P, CG2, 1:1 + J], C[G2P:P, CG2, 1:1 + J], ACT.Tanh, scale=0.5), s_["lora_a"], "lora_a")
            elif k == "ksquare":
                c = step[1]
                act.wait_ge(s_["shifted"], NC)
                if c == 0:
                    landed(act, ("ofin", SAMPLE), "o")
                    act.wait_ge(stored, 16 * n_stored[0])
                    for m in range(2):
                        act.wait_ge(kout_stored[m], 16 * (3 - m))
                A.mark(f_act(AR[:, c, 0, :], C[:, CK + c, 1:1 + J], ACT.Square, scale=pv[:, PV_KK + c:PV_KK + c + 1]),
                       s_["ksq"], "ksq")
            elif k == "krsqrt":
                act.wait_ge(s_["kinv"], CT)
                for c in range(CT):
                    A.mark(f_act(AR[:, c, 0, :], AR[:, c, 0, :], ACT.Sqrt), s_["ksqrt"], "ksqrt")
            elif k == "rwA":
                c = step[1]
                if c >= 2:
                    act.wait_ge(s_["rw_done"], c - 1)
                t0, t1, t4 = (tmp[:, sl + 3 * (c % 2), :] for sl in range(3))
                for f, t, col in (("w", t0, PV_W0), ("a", t1, PV_A0)):
                    for i, (a, b_) in enumerate(((0, HALF), (HALF, J))):
                        b = full_bank(act, step, f"{f}{i}")
                        drain(f_act(t[:, a:b_], b[:, 0:b_ - a], ACT.Tanh, scale=0.5,
                                    bias=pvh[:, col + c:col + c + 1]), step, f"{f}{i}")
                        landed(act, step, f"{f}{i}")
                A(f_act(t0, t0, ACT.Copy, scale=-DECAY / 2, bias=-DECAY / 2))
                A(f_act(t1, t1, ACT.Copy, scale=0.5, bias=0.5))
                A.mark(f_act(t4, t1, ACT.Identity, scale=pv[:, PV_KA + c:PV_KA + c + 1], bias=oka[:, c:c + 1]),
                       s_["rw_w"], "rw_w")
            elif k == "rwB":
                c = step[1]
                t0, t2, t3, t5 = (tmp[:, sl, :] for sl in (3 * (c % 2), 6, 7, 8))
                if c:
                    act.wait_ge(s_["rw_done"], c)
                A.mark(f_act(t5, C[:, CK + c, 1:1 + J], ACT.Copy, scale=pv[:, PV_KK + c:PV_KK + c + 1]), s_["rw_kk"], "rw_kk")
                act.wait_ge(s_["rw_g"], c + 1)
                A.mark(f_act(t3, t2, ACT.Exp), s_["rw_p"], "rw_p")
                act.wait_ge(s_["rw_gm"], c + 1)
                A(f_act(t0, t0, ACT.Exp))
                A.mark(f_act(t2, t2, ACT.Exp, scale=-1.0), s_["rw_e2"], "rw_e2")
            elif k == "init0":
                act.wait_ge(s_["zeroed"], 1)
                src = i_["state_wkv"][0, 0].rearrange("(c p) v k -> p v c k", p=2)
                for p in range(2):
                    act.dma_start(sio[64 * p:64 * p + 64, :, 64 * p:64 * p + 64], src[p]).then_inc(s_["init_loaded"], 16)
            elif k == "w":
                _, st, t, g = step
                n, j0 = TILES[t][1], first(t)
                if st == "tok":
                    b = full_bank(act, step, "t0")
                    drain(f_act(tok[0:n, g, 0:2, :, :].rearrange("p q h v -> p (q h v)"), b[0:n, 0:512], ACT.Copy), step, "t0")
                    b = full_bank(act, step, "t1")
                    A(f_act(tok[0:n, g, 2, :, :].rearrange("p h v -> p (h v)"), b[0:n, 0:256], ACT.Copy))
                    drain(f_act(ag[0:n, g, :, 0, :], b[0:n, 256:512].rearrange("p (h v) -> p h v", h=4), ACT.Copy), step, "t1")
                elif st == "gv":
                    b = full_bank(act, step, "gv")
                    drain(f_act(ag[0:n, g, :, 1, :], b[0:n, 0:256].rearrange("p (h v) -> p h v", h=4), ACT.Copy), step, "gv")
                elif st == "x0":
                    b = full_bank(act, step, "x")
                    drain(f_act(X[0:n, g, :, 0:n], b[0:n, 0:4 * n].rearrange("p (h i) -> p h i", h=4), ACT.Copy), step, "x")
                elif st == "wu":
                    b = full_bank(act, step, "wu")
                    drain(f_act(wu[0:n, g, :, :, :].rearrange("p h u v -> p (h u v)"), b[0:n, 0:512], ACT.Copy, scale=-1.0),
                          step, "wu")
                elif st == "yb":
                    b = full_bank(act, step, "y")
                    drain(f_act(AR[:, 2 * g:2 * g + 2, 1, j0:j0 + n], b[:, 0:2 * n].rearrange("p (c i) -> p c i", c=2),
                                ACT.Copy), step, "y")
            elif k == "wt":
                t, g = step[2], step[3]
                n = TILES[t][1]
                b = full_bank(act, step, "t")
                drain(f_act(XT[0:n, g, :, 0:n], b[0:n, 0:4 * n].rearrange("p (h i) -> p h i", h=4), ACT.Copy), step, "t")
            elif k == "final":
                _, t, g = step
                b = full_bank(act, step, "f")
                act.wait_ge(stored, 16 * n_stored[0])
                bv = b[:, 0:2 * P].rearrange("p (c k) -> p c k", c=2)
                A(f_act(sout[0:64, :, :], bv[0:64, :, 0:64], ACT.Copy))
                drain(f_act(sout[64:P, :, :], bv[64:P, :, 64:P], ACT.Copy), step, "f")
                landed(act, step, "f")
                store(o_["wkv_prompt" if t < SAMPLE else "wkv_sample"][0, 0, 4 * g:4 * g + 4].rearrange(
                    "(c p) v k -> (p v) c k", p=2), sout[:, :, :])
            elif k == "ymean":
                _, t, g = step
                n, j0 = TILES[t][1], first(t)
                landed(act, step, "m")
                A.mark(f_act(AR[:, 2 * g:2 * g + 2, 0, j0:j0 + n], AR[:, 2 * g:2 * g + 2, 1, j0:j0 + n], ACT.Square),
                       s_["y_sq"], "y_sq")
            elif k == "yvar":
                _, t, g = step
                n, j0 = TILES[t][1], first(t)
                b = full_bank(act, step, "m")
                drain(f_act(AR[:, 2 * g:2 * g + 2, 0, j0:j0 + n], b[:, 0:2 * n].rearrange("p (c i) -> p c i", c=2), ACT.Sqrt,
                            scale=1.0 / AD, bias=GN_EPS), step, "m")
            elif k == "ysplit":
                c = step[1]
                landed(act, ("yfin", SAMPLE, c // 2), "g")
                A.mark(f_act(y_hi[:, c, 0:SEQ], AR[:, c, 1, 0:SEQ], ACT.Copy), s_["y_hi_done"], "y_hi_done")
                A.mark(f_act(y_hi[:, c, SEQ:TOK], AR[:, c, 1, JS:J], ACT.Copy), s_["y_hi_done"], "y_hi_done")
            elif k == "ztok":
                _, r, i = step
                if (r, i) == (1, 0):
                    A(f_act(rms[:, 0:1], rms[:, 0:1], ACT.Sqrt))
                b = full_bank(act, step, "z0")
                for t in range(SAMPLE):
                    ins = f_act(h2_lo[:, t, 0:P], b[:, t * P:(t + 1) * P], ACT.Square, accum_out=zsq[:, t, i:i + 1])
                A.mark(ins, s_["z_sq"], "z_sq")
                b = full_bank(act, step, "z1")
                A.mark(f_act(h2_lo[0:DEC, SAMPLE, 0:P], b[0:DEC, 0:P], ACT.Square, accum_out=zsq[0:DEC, SAMPLE, i:i + 1]),
                       s_["z_sq"], "z_sq")
            elif k == "zS":
                r = step[1]
                for i, (n, a, b_) in enumerate(((P, 0, SAMPLE), (DEC, SAMPLE, NT))):
                    act.wait_ge(s_["z_sum"], 2 * r + i + 1)
                    A.mark(f_act(rms[0:n, a:b_], ssq[0:n, a:b_], ACT.Sqrt, scale=1.0 / D, bias=EPS), s_["zrms"], "zrms")
            elif k == "zA1":
                t = step[1]
                act.wait_ge(s_["zres"], NT + t + 1)
                store(y_rows(t), z[0:TILES[t][1], t, :])
            elif k == "zB":
                t = step[1]
                n = TILES[t][1]
                act.wait_ge(s_["zres"], t + 1)
                A(f_act(dps[0][0:n, :, :], x1[0:n, t, :].rearrange("p (a b) -> p a b", a=2), ACT.Square,
                        accum_out=ssq[0:n, t:t + 1]))
                A.mark(f_act(rms[0:n, t:t + 1], ssq[0:n, t:t + 1], ACT.Sqrt, scale=1.0 / D, bias=EPS), s_["xrms"], "xrms")
                if t == SAMPLE:
                    act.dma_start(gain[:, :], i_["norm_ffn_post"][0].partition_broadcast(P)).then_inc(s_["gain_loaded"], 16)
            elif k == "zC":
                for i in range(2):
                    halves(h2_hi, step, f"n{i}", *TILES[step[1]], "z_hi", 4 * i)
            elif k == "ffn":
                pa, pb_ = dps[FFN_BLOCK0 % 2], dps[(FFN_BLOCK0 + 1) % 2]

                def pair(j, before):
                    act.wait_ge(seg_done, j * 2 + (FFN_SEG0 + 1))
                    if before:
                        act.wait_ge(dense_read[FFN_BLOCK0 % 2], j + FFN_BLOCK0 // 2)
                    f_act(f_t.rearrange("p (a b) -> p a b", a=2), pa[:, :, 0:HALF], ACT.Tanh, scale=0.5).then_inc(
                        s_["f_tanh"], 1)
                    act.wait_ge(dense_read[(FFN_BLOCK0 + 1) % 2], j + ((FFN_BLOCK0 + 1) // 2 + 1))
                    dst = S[:, bass.ds(j, 1), 0, :] if before else S[:, 0:1, 0, :]
                    f_act(dst, f_s.unsqueeze(1), ACT.Copy, scale=0.5).then_inc(s_["f_hi"], 1)

                pair(0, False)
                with act.Fori(1, FT) as j:
                    pair(j, True)
            elif k == "dense":
                _, kind, i, part, parts = step
                d = (kind, i)
                if part < abs(parts) - 1 or kind in ("ug", "uv"):
                    continue
                if kind in ("outA", "outB"):
                    if kind == "outA":
                        act.wait_ge(s_["mixed"], i + 1)
                        f_act(S[:, i, 0, :], mb[:, i, :], ACT.Copy, scale=0.5).then_inc(s_["mix_hi"], 1)
                    continue
                acc = block_full(act, d)
                if kind == "qkv":
                    f_act(qkv[:, i, :].rearrange("p (a b) -> p a b", a=2), acc[:, :, 0:HALF], ACT.Copy).then_inc(
                        block_sem(d), 1)
                elif kind == "c":
                    f_act(C[:, i, 1:1 + HALF], acc[:, 0, 0:HALF], ACT.Copy)
                    f_act(C[:, i, 1 + HALF:1 + SEQ], acc[:, 1, 0:SEQ - HALF], ACT.Copy)
                    f_act(C[:, i, 1 + JS:1 + J], acc[:, 1, SEQ - HALF:HALF], ACT.Copy).then_inc(block_sem(d), 1)
                elif kind in ("gA", "gB"):
                    col = PV_BG + i + (KT if kind == "gB" else 0)
                    dst = (mb if kind == "gB" else ga)[:, i, :].rearrange("p (a b) -> p a b", a=2)
                    f_act(dst, acc[:, :, 0:HALF], ACT.Tanh, scale=0.5, bias=pvh[:, col:col + 1]).then_inc(block_sem(d), 1)
                elif kind in ("wo", "down"):
                    if d == ("wo", 0):
                        act.wait_ge(s_["mix_done"], 8)
                        act.dma_start(gain[:, :], i_["norm_mix_post"][0].partition_broadcast(P)).then_inc(
                            s_["gain_loaded"], 16)
                        act.dma_start(gain2[:, :], i_["norm_ffn_pre"][0].partition_broadcast(P)).then_inc(
                            s_["gain2_loaded"], 16)
                        for t in range(NT):
                            act.dma_start(x1[0:TILES[t][1], t, :], x_rows(t)).then_inc(s_["x1_loaded"], 16)
                    if i:
                        full_bank(act, ("ztok", int(kind == "down"), i - 1), "z1")
                    f_act(zT[:, :].rearrange("p (a b) -> p a b", a=2), acc[:, :, 0:HALF], ACT.Copy).then_inc(block_sem(d), 1)
        act.wait_ge(stored, 16 * n_stored[0])
        act.wait_ge(kout_stored[0], 16 * 3)
        act.wait_ge(kout_stored[1], 16 * 2)

    @block.vector
    def _(dve):
        V = Chain(dve, vch)
        vec = nc.vector

        def drain(ins, step, f):
            ins.then_inc(drain_sem(step, f), 1)

        def rw_slots(c):
            return [tmp[:, sl, :] for sl in (3 * (c % 2), 3 * (c % 2) + 1, 3 * (c % 2) + 2, 6, 7, 8)]

        def low(hi, lo, step, f, t0, n, name, count, k0):
            b = full_bank(dve, step, f)
            dve.wait_ge(s_[name], count)
            drain(vec.tensor_tensor(lo[:, k0:k0 + 4, t0:t0 + n], b[:, 0:4 * n].rearrange("p (k n) -> p k n", k=4),
                                    hi[:, k0:k0 + 4, t0:t0 + n].bitcast(F32), ALU.subtract), step, f)

        for step in SCHEDULE:
            k = step[0]
            if k == "params":
                landed(dve, step, "pv")
                V(vec.memset(C[:, :, 0:1], 0.0))
                V.mark(vec.tensor_copy(C[:, :, JS:JS + 1], pv[:, PV_SHIFT:PV_SHIFT + NC].unsqueeze(2)),
                       s_["shift_set"], "shift_set")
            elif k == "normA":
                t = step[1]
                t0, n = TILES[t]
                dve.wait_ge(s_["x_sq"], t + 1)
                V(vec.reciprocal(rstd[0:n, t:t + 1], rms[0:n, t:t + 1]))
                if t == 0:
                    dve.wait_ge(s_["gain_loaded"], 16)
                if t >= 2:
                    full_bank(dve, ("normB", t - 2), "n1")
                V.mark(vec.scalar_tensor_tensor(out=xn[0:n, t % 2, :], in0=xs[0:n, t, :], scalar=rstd[0:n, t:t + 1],
                                                in1=gain[0:n, :], op0=ALU.mult, op1=ALU.mult), s_["x_normed"], "x_normed")
            elif k == "normB":
                t = step[1]
                for i in range(2):
                    low(h_hi, h_lo, step, f"n{i}", *TILES[t], "x_hi", 2 * t + i + 1, 4 * i)
            elif k == "cache":
                dve.wait_ge(s_["att_loaded"], 16 * N_ATT)
                V(vec.tensor_scalar(subln[:, :], subln[:, :], 1.0 - LAM_INIT, None, ALU.mult))
                for m in range(2):
                    V(vec.tensor_tensor(lamv[:, 4, :], lamv[:, 2 * m, :], lamv[:, 2 * m + 1, :], ALU.mult))
                    V.mark(vec.tensor_reduce(lam2[:, m:m + 1], lamv[:, 4, :], AX.X, ALU.add), s_["lam_prod"], "lam_prod")
                dve.wait_ge(s_["lam_exp"], 1)
                V(vec.tensor_tensor(nlam[:, :], lam2[:, 3:4], lam2[:, 2:3], ALU.subtract))
                V(vec.tensor_scalar(nlam[:, :], nlam[:, :], -LAM_INIT, None, ALU.add))
            elif k == "vtok":
                n = TILES[step[1]][1]
                b = full_bank(dve, step, "v")
                drain(vec.tensor_copy(vtok[0:n, step[1], :], b[0:n, 0:BW]), step, "v")
            elif k == "attS":
                _, t, h = step
                t0, n = TILES[t]
                idx = t * BH + h
                pb = idx % 2
                keys = t0 + n if t < SAMPLE else PAST + DEC
                if idx >= 2:
                    landed(dve, ("attP", *divmod(idx - 2, BH)), "pt")
                for m in range(2):
                    b = full_bank(dve, step, f"s{m}")
                    if t < SAMPLE:
                        V(vec.memset(b[0:CHUNK, keys - CHUNK:keys], NEG))
                    c = 2 * pb + m
                    V(vec.reduce_max(amax[0:n, c:c + 1], b[0:n, 0:keys], AX.X))
                    V.mark(vec.tensor_scalar(amax[0:n, c:c + 1], amax[0:n, c:c + 1], -SCALE, None, ALU.mult),
                           s_["smax"], "smax")
            elif k == "attC":
                _, t, h = step
                t0, n = TILES[t]
                pb = (t * BH + h) % 2
                keys = t0 + n if t < SAMPLE else PAST + DEC
                landed(dve, ("attS", t, h), "s0")
                landed(dve, ("attS", t, h), "s1")
                a0, a1 = arec[0:n, 2 * pb:2 * pb + 1], arec[0:n, 2 * pb + 1:2 * pb + 2]
                V(vec.reciprocal(arec[0:n, 2 * pb:2 * pb + 2], asum[0:n, 2 * pb:2 * pb + 2]))
                V(vec.tensor_tensor(a1, a1, nlam[0:n, :], ALU.mult))
                p0, p1 = probs[0:n, pb, 0, 0:keys], probs[0:n, pb, 1, 0:keys]
                V(vec.tensor_scalar(p0, p0, a0, None, ALU.mult))
                V.mark(vec.scalar_tensor_tensor(out=p0, in0=p1, scalar=a1, in1=p0, op0=ALU.mult, op1=ALU.add),
                       s_["sattn"], "sattn")
            elif k == "oscale":
                dve.wait_ge(s_["o_rms"], 2)
                V(vec.reciprocal(orst[:, 0:SAMPLE * BH], orms[:, 0:SAMPLE * BH]))
                V(vec.reciprocal(orst[0:DEC, SAMPLE * BH:], orms[0:DEC, SAMPLE * BH:]))
            elif k == "oA":
                t = step[1]
                n = TILES[t][1]
                for h in range(BH):
                    o = otok[0:n, t, h * BV:(h + 1) * BV]
                    ins = vec.scalar_tensor_tensor(out=o, in0=o, scalar=orst[0:n, t * BH + h:t * BH + h + 1],
                                                   in1=subln[0:n, :], op0=ALU.mult, op1=ALU.mult)
                V.mark(ins, s_["o_scaled"], "o_scaled")
            elif k == "ofin":
                t = step[1]
                t0, n = TILES[t]
                low(o_hi, o_lo, step, "o", t0, n, "o_hi_done", t + 1, 0)
            elif k == "shift":
                i = step[1]
                block_landed(dve, ("c", i))
                V(vec.tensor_copy(last[:, :, i], C[:, i, SEQ:J + 1:J - SEQ]))
                V(vec.tensor_tensor(dtmp[:, :], C[:, i, 0:J], C[:, i, 1:1 + J], ALU.subtract))
                V.mark(vec.scalar_tensor_tensor(out=C[:, i, 1:1 + J], in0=dtmp[:, :], scalar=pv[:, PV_MU + i:PV_MU + i + 1],
                                                in1=C[:, i, 1:1 + J], op0=ALU.mult, op1=ALU.add), s_["shifted"], "shifted")
            elif k == "shiftout":
                V.mark(vec.tensor_scalar(oka[:, :], pv[:, PV_KA:PV_KA + CT], -1.0, 1.0, ALU.mult, ALU.add),
                       s_["last_done"], "last_done")
            elif k == "lora":
                dve.wait_ge(s_["lora_a"], 1)
                V(vec.tensor_scalar(C[:, CG, 1:1 + J], C[:, CG, 1:1 + J], 0.5, 0.5, ALU.mult, ALU.add))
                V(vec.tensor_scalar(C[G2P:P, CG2, 1:1 + J], C[G2P:P, CG2, 1:1 + J], 0.5, 0.5, ALU.mult, ALU.add))
            elif k == "knorm":
                c = step[1]
                for i, (a, b_) in enumerate(((0, HALF), (HALF, J))):
                    b = full_bank(dve, step, f"q{i}")
                    if i == 0:
                        full_bank(dve, step, "q1")
                    drain(vec.tensor_scalar(AR[:, c, 0, a:b_], b[:, 0:b_ - a], 1e-24, None, ALU.max), step, f"q{i}")
                landed(dve, step, "q0")
                landed(dve, step, "q1")
                V.mark(vec.reciprocal(AR[:, c, 0, :], AR[:, c, 0, :]), s_["kinv"], "kinv")
            elif k == "rwB":
                c = step[1]
                t0, t1, t4, t2, t3, t5 = rw_slots(c)
                r, kx = C[:, CR + c, 1:1 + J], C[:, CK + c, 1:1 + J]
                dve.wait_ge(s_["rw_w"], c + 1)
                V.mark(vec.tensor_tensor_scan(t2, cst[:, K_SCAN:K_SCAN + J], t0, 0.0, ALU.mult, ALU.add), s_["rw_g"], "rw_g")
                V.mark(vec.tensor_tensor(t0, t2, t0, ALU.subtract), s_["rw_gm"], "rw_gm")
                dve.wait_ge(s_["rw_kk"], c + 1)
                V(vec.tensor_tensor(kx, kx, t4, ALU.mult))
                V(vec.tensor_tensor(t4, t5, AR[:, c, 0, :], ALU.mult))
                V.mark(vec.scalar_tensor_tensor(out=t5, in0=r, scalar=pv[:, PV_RK + c:PV_RK + c + 1], in1=kx, op0=ALU.mult,
                                                op1=ALU.mult), s_["rw_bo"], "rw_bo")
                dve.wait_ge(s_["rw_p"], c + 1)
                V(vec.tensor_copy(pend[:, c, 0:NCH], t3[:, 0:SEQ].rearrange("p (q l) -> p q l", l=CHUNK)[:, :, CHUNK - 1]))
                V(vec.tensor_copy(pend[:, c, NCH:NCH + 1], t3[:, J - 1:J]))
                V(vec.tensor_tensor(AR[:, c, 1, :], r, t3, ALU.mult))
            elif k == "rw2":
                c = step[1]
                t0, t1, t4, t2, t3, t5 = rw_slots(c)
                kx = C[:, CK + c, 1:1 + J]
                V(vec.tensor_tensor(t1, t4, t1, ALU.mult))
                dve.wait_ge(s_["rw_e2"], c + 1)
                V(vec.tensor_tensor(AR[:, c, 0, :], t4, t0, ALU.mult))
                V(vec.tensor_tensor(C[:, CR + c, 1:1 + J], t1, t2, ALU.mult))
                for i, (a, b_) in enumerate(((0, HALF), (HALF, J))):
                    b = full_bank(dve, step, f"b{i}")
                    drain(vec.tensor_tensor(bonus[:, c, a:b_], b[:, 0:b_ - a], C[:, CV + c, 1 + a:1 + b_], ALU.mult),
                          step, f"b{i}")
                V.mark(vec.tensor_tensor(kx, kx, t2, ALU.mult), s_["rw_done"], "rw_done")
            elif k == "init0":
                V(vec.memset(sio[:, :, :], 0.0))
                V(vec.memset(ebd[:, :, :, :], 0.0))
                V(vec.memset(mcur[:, :, :, :], 0.0))
                V.mark(vec.memset(mbd[:, :, :, :, :], 0.0), s_["zeroed"], "zeroed")
            elif k == "init":
                b = full_bank(dve, step, "s")
                bv = b[:, 0:512].rearrange("p (g c k) -> p g c k", g=2, c=2)
                for g in range(2):
                    V(vec.tensor_copy(mbd[:, g, 0, :, :], bv[:, g, :, :]))
                V(vec.tensor_copy(mcur[0:64, :, :, :], bv[0:64, :, :, 0:64]))
                drain(vec.tensor_copy(mcur[64:P, :, :, :], bv[64:P, :, :, 64:P]), step, "s")
            elif k == "w":
                _, st, t, g = step
                n, j0 = TILES[t][1], first(t)
                if st in ("sb", "sk"):
                    mask = cst[0:n, K_SC:K_SC + 2 * P].rearrange("p (u i) -> p u i", u=2)[:, :, 0:n]
                    mask = mask.unsqueeze(1).broadcast_to([n, 2, 2, n])
                    f, dst = ("b", lt) if st == "sb" else ("k", gt)
                    for p in range(2):
                        b = full_bank(dve, step, f"{f}{p}")
                        o = dst[0:n, g, p::2, :].rearrange("p c (u i) -> p c u i", u=2)[:, :, :, 0:n]
                        drain(vec.tensor_tensor(o, b[0:n, 0:4 * n].rearrange("p (c u i) -> p c u i", c=2, u=2), mask,
                                                ALU.mult), step, f"{f}{p}")
                    if st == "sk":
                        continue
                    landed(dve, step, "b1")
                    m0 = cst[0:n, K_M0:K_M0 + n].unsqueeze(1).broadcast_to([n, 4, n])
                    idb = ident[0:n, 0:n].unsqueeze(1).broadcast_to([n, 4, n])
                    xt = XT[0:n, g, :, 0:n]
                    V(vec.tensor_tensor(xt, lt[0:n, g, :, 0:n], m0, ALU.mult))
                    V.mark(vec.tensor_tensor(xt, idb, xt, ALU.subtract), s_["xt_init"], "xt_init")
                elif st == "ef":
                    for ch, ln in chunks(t):
                        b = full_bank(dve, step, f"e{ch}")
                        bv = b[:, 0:2 * P].rearrange("p (c u k) -> p c u k", c=2, u=2)
                        for p in range(2):
                            lo, hi = 64 * p, 64 * p + 64
                            i64 = cst[lo:hi, K_I64:K_I64 + 64].unsqueeze(1).broadcast_to([64, 2, 64])
                            vec.tensor_tensor(ebd[lo:hi, g, ch, :, lo:hi], bv[lo:hi, :, 0, :], i64, ALU.add)
                        drain(vec.tensor_copy(ff[:, g, ch, :, :], bv[:, :, 1, :]), step, f"e{ch}")
                elif st in ("chain0", "chain1"):
                    ch = int(st[-1])
                    b = full_bank(dve, step, "c")
                    q = 2 * t + ch if t < SAMPLE else NCH
                    drain(vec.tensor_tensor(mt[:, g, :, :], b[:, 0:P].rearrange("p (c v) -> p c v", c=2), ff[:, g, ch, :, :],
                                            ALU.add), step, "c")
                    landed(dve, step, "c")
                    pe_ = pend[:, 2 * g:2 * g + 2, q:q + 1]
                    for p in range(2):
                        lo, hi = 64 * p, 64 * p + 64
                        vec.tensor_tensor(mbd[lo:hi, g, 1 - ch, :, lo:hi], mt[lo:hi, g, :, :],
                                          pe_[lo:hi].broadcast_to([64, 2, 64]), ALU.mult)
                    V.mark(vec.tensor_tensor(mcur[:, g, :, :], mt[:, g, :, :], pe_.broadcast_to([P, 2, 64]), ALU.mult),
                           s_["st_bd"], "st_bd")
                elif st == "q":
                    b = full_bank(dve, step, "q")
                    drain(vec.tensor_tensor(qT[:, g, :, 0:n], b[:, 0:2 * n].rearrange("p (c i) -> p c i", c=2),
                                            AR[:, 2 * g:2 * g + 2, 1, j0:j0 + n], ALU.add), step, "q")
            elif k == "wm":
                _, lv, t, g = step
                n = TILES[t][1]
                b = full_bank(dve, step, "m")
                mask = cst[0:n, K_LV + 64 * lv:K_LV + 64 * lv + n // 2].unsqueeze(1).broadcast_to([n, 4, n // 2])
                drain(vec.tensor_tensor(mc[0:n, g, :, 0:n // 2], b[0:n, 0:256].rearrange("p (h i) -> p h i", h=4)[:, :, 0:n // 2],
                                        mask, ALU.mult), step, "m")
            elif k == "wd":
                _, lv, t, g = step
                n = TILES[t][1]
                s = LEVELS[lv]
                b = full_bank(dve, step, "d")
                xv = X[0:n, g, :, 0:n].rearrange("p h (b u s) -> p h b u s", u=2, s=s)[:, :, :, 0, :]
                bv = b[0:n, 0:256].rearrange("p (h i) -> p h i", h=4)[:, :, 0:n // 2].rearrange("p h (b s) -> p h b s", s=s)
                drain(vec.tensor_tensor(xv, xv, bv, ALU.subtract), step, "d")
            elif k == "ymean":
                _, t, g = step
                n, j0 = TILES[t][1], first(t)
                b = full_bank(dve, step, "m")
                y = AR[:, 2 * g:2 * g + 2, 1, j0:j0 + n]
                drain(vec.scalar_tensor_tensor(out=y, in0=b[:, 0:2 * n].rearrange("p (c i) -> p c i", c=2), scalar=-1.0 / AD,
                                               in1=y, op0=ALU.mult, op1=ALU.add), step, "m")
            elif k == "yfin":
                _, t, g = step
                n, j0 = TILES[t][1], first(t)
                y, rs = (AR[:, 2 * g:2 * g + 2, u, j0:j0 + n] for u in (1, 0))
                landed(dve, ("yvar", t, g), "m")
                V(vec.reciprocal(rs, rs))
                V(vec.tensor_tensor(y, y, rs, ALU.mult))
                for c in (2 * g, 2 * g + 1):
                    yc = AR[:, c, 1, j0:j0 + n]
                    ins = vec.tensor_scalar(yc, yc, pv[:, PV_LNW + c:PV_LNW + c + 1], pv[:, PV_LNB + c:PV_LNB + c + 1],
                                            ALU.mult, ALU.add)
                V(ins)
                V(vec.tensor_tensor(y, y, bonus[:, 2 * g:2 * g + 2, j0:j0 + n], ALU.add))
                b = full_bank(dve, step, "g")
                ins = vec.tensor_tensor(y, b[:, 0:2 * n].rearrange("p (c i) -> p c i", c=2), y, ALU.mult)
                drain(ins, step, "g")
            elif k == "ysplit":
                c = step[1]
                for i, (a, b_, u) in enumerate(((0, SEQ, 0), (SEQ, TOK, JS))):
                    dve.wait_ge(s_["y_hi_done"], 2 * c + i + 1)
                    vec.tensor_tensor(y_lo[:, c, a:b_], AR[:, c, 1, u:u + b_ - a], y_hi[:, c, a:b_].bitcast(F32),
                                      ALU.subtract).then_inc(s_["y_done"], 1)
            elif k == "ztok":
                _, r, i = step
                if i == 0:
                    dve.wait_ge(s_["gain_loaded"], 16 * (2 + r))
                gi = gain[:, i * P:(i + 1) * P]
                dve.wait_ge(s_["z_sq"], 2 * (8 * r + i) + 1)
                drain(vec.tensor_tensor(z[:, 0:4, i * P:(i + 1) * P], bank(step, "z0")[:, 0:512].rearrange(
                    "p (t n) -> p t n", t=4), gi.unsqueeze(1).broadcast_to([P, 4, P]), ALU.mult), step, "z0")
                dve.wait_ge(s_["z_sq"], 2 * (8 * r + i) + 2)
                drain(vec.tensor_tensor(z[0:DEC, SAMPLE, i * P:(i + 1) * P], bank(step, "z1")[0:DEC, 0:P], gi[0:DEC],
                                        ALU.mult), step, "z1")
            elif k == "zS":
                r = step[1]
                for i, (n, a, b_) in enumerate(((P, 0, SAMPLE), (DEC, SAMPLE, NT))):
                    V.mark(vec.tensor_reduce(ssq[0:n, a:b_], zsq[0:n, a:b_, :], AX.X, ALU.add), s_["z_sum"], "z_sum")
                dve.wait_ge(s_["zrms"], 2 * r + 2)
                V(vec.reciprocal(rstd[:, 0:SAMPLE], rms[:, 0:SAMPLE]))
                V(vec.reciprocal(rstd[0:DEC, SAMPLE:NT], rms[0:DEC, SAMPLE:NT]))
            elif k in ("zA0", "zA1"):
                r, t = int(k[-1]), step[1]
                n = TILES[t][1]
                if t == 0:
                    dve.wait_ge(s_["x1_loaded"], 16 * NT)
                    landed(dve, ("ztok", r, 7), "z0")
                    landed(dve, ("ztok", r, 7), "z1")
                dst = x1 if r == 0 else z
                vec.scalar_tensor_tensor(out=dst[0:n, t, :], in0=z[0:n, t, :], scalar=rstd[0:n, t:t + 1],
                                         in1=x1[0:n, t, :], op0=ALU.mult, op1=ALU.add).then_inc(s_["zres"], 1)
            elif k == "zB":
                t = step[1]
                n = TILES[t][1]
                if t == 0:
                    dve.wait_ge(s_["gain2_loaded"], 16)
                dve.wait_ge(s_["xrms"], t + 1)
                V(vec.reciprocal(rstd[0:n, t:t + 1], rms[0:n, t:t + 1]))
                V.mark(vec.scalar_tensor_tensor(out=z[0:n, t, :], in0=x1[0:n, t, :], scalar=rstd[0:n, t:t + 1],
                                                in1=gain2[0:n, :], op0=ALU.mult, op1=ALU.mult), s_["xnorm"], "xnorm")
            elif k == "zC":
                t = step[1]
                for i in range(2):
                    low(h2_hi, h2_lo, step, f"n{i}", *TILES[t], "z_hi", 2 * t + i + 1, 4 * i)
            elif k == "ffn":
                sa, sb_ = FFN_BLOCK0 % 2, (FFN_BLOCK0 + 1) % 2
                a0, b0 = FFN_BLOCK0 // 2, (FFN_BLOCK0 + 1) // 2
                fs2 = f_s.rearrange("p (a b) -> p a b", a=2)
                ft2 = f_t.rearrange("p (a b) -> p a b", a=2)

                def pair(j, loop):
                    dve.wait_ge(s_["f_tanh"], j + 1)
                    if loop:
                        dve.wait_ge(s_["f_lo"], j)
                    vec.scalar_tensor_tensor(out=fs2, in0=ft2, scalar=1.0, in1=dps[sa][:, :, 0:HALF], op0=ALU.add,
                                             op1=ALU.mult).then_inc(dense_read[sa], 1)
                    dve.wait_ge(dense_read[sa], j + (a0 + 1))
                    dve.wait_ge(seg_done, j * 2 + (FFN_SEG0 + 2))
                    vec.tensor_tensor(fs2, fs2, dps[sb_][:, :, 0:HALF], ALU.mult).then_inc(dense_read[sb_], 1)
                    dve.wait_ge(dense_read[sb_], j + (b0 + 1))
                    dve.wait_ge(s_["f_hi"], j + 1)
                    hi = S[:, bass.ds(j, 1), 0, :] if loop else S[:, 0:1, 0, :]
                    lo = S[:, bass.ds(j, 1), 1, :] if loop else S[:, 0:1, 1, :]
                    vec.scalar_tensor_tensor(out=lo, in0=f_s.unsqueeze(1), scalar=0.5, in1=hi.bitcast(F32), op0=ALU.mult,
                                             op1=ALU.subtract).then_inc(s_["f_lo"], 1)

                pair(0, False)
                with dve.Fori(1, FT) as j:
                    pair(j, True)
            elif k == "dense":
                _, kind, i, part, parts = step
                d = (kind, i)
                if part < abs(parts) - 1 or kind in ("ug", "uv"):
                    continue
                if kind == "outB":
                    block_landed(dve, ("gB", i))
                    acc = block_full(dve, d)
                    m2 = mb[:, i, :].rearrange("p (a b) -> p a b", a=2)
                    vec.scalar_tensor_tensor(out=m2, in0=m2, scalar=1.0, in1=acc[:, :, 0:HALF], op0=ALU.add,
                                             op1=ALU.mult).then_inc(block_sem(d), 1)
                elif kind == "outA":
                    block_landed(dve, ("gA", i))
                    acc = block_full(dve, d)
                    ga2 = ga[:, i, :].rearrange("p (a b) -> p a b", a=2)
                    vec.scalar_tensor_tensor(out=ga2, in0=ga2, scalar=1.0, in1=acc[:, :, 0:HALF], op0=ALU.add,
                                             op1=ALU.mult).then_inc(block_sem(d), 1)
                    block_landed(dve, d)
                    block_landed(dve, ("outB", i))
                    V.mark(vec.tensor_tensor(mb[:, i, :], ga[:, i, :], mb[:, i, :], ALU.add), s_["mixed"], "mixed")
                    for m in [i - 1] * (i > 0) + [i] * (i == 7):
                        dve.wait_ge(s_["mix_hi"], m + 1)
                        vec.scalar_tensor_tensor(out=S[:, m, 1, :], in0=mb[:, m, :], scalar=0.5,
                                                 in1=S[:, m, 0, :].bitcast(F32), op0=ALU.mult,
                                                 op1=ALU.subtract).then_inc(s_["mix_done"], 1)

    ctx.close()


_INS = ["x_prompt", "x_sample", "cache_k", "cache_v", "state_wkv", "state_shift", "norm_mix_pre", "norm_mix_post",
        "norm_ffn_pre", "norm_ffn_post", "w_in", "b_gate", "rwkv_mu", "rwkv_w0", "rwkv_w2", "rwkv_a0", "rwkv_a2",
        "rwkv_g2", "rwkv_k_k", "rwkv_k_a", "rwkv_r_k", "rwkv_ln_w", "rwkv_ln_b", "diff_lq1", "diff_lk1", "diff_lq2",
        "diff_lk2", "diff_subln", "w_out_a", "w_out_b", "w_o", "w_ffn_in", "w_ffn_out"]
_OUTS = [("y_prompt", (1, SEQ, D)), ("y_sample", (1, DEC, D)), ("k_prompt", (1, 1, SEQ, BH, 2, BD_)),
         ("v_prompt", (1, 1, SEQ, BH, BV)), ("wkv_prompt", (1, 1, AH, AD, AD)), ("shift_prompt", (1, 1, 1, A_COLS)),
         ("k_sample", (1, 1, DEC, BH, 2, BD_)), ("v_sample", (1, 1, DEC, BH, BV)), ("wkv_sample", (1, 1, AH, AD, AD)),
         ("shift_sample", (1, 1, 1, A_COLS))]


def kernel(**inputs):
    import concourse.bacc as bacc
    from concourse.bass_utils import run_bass_kernel_spmd

    nc = bacc.Bacc("TRN2", target_bir_lowering=False, num_devices=1)
    arrays, ins, outs = {}, {}, {}
    for name in _INS:
        a = np.ascontiguousarray(inputs[name])
        arrays[f"in_{name}"] = a
        ins[name] = nc.dram_tensor(f"in_{name}", a.shape, F32, kind="ExternalInput").ap()
    arrays["in_cst"] = constants()
    ins["cst"] = nc.dram_tensor("in_cst", (P, K_N), F32, kind="ExternalInput").ap()
    for name, shape in _OUTS:
        outs[name] = nc.dram_tensor(f"out_{name}", shape, F32, kind="ExternalOutput").ap()
    encoder_kernel(nc, ins, outs)
    r = run_bass_kernel_spmd(nc, [arrays], core_ids=[0])
    return tuple(r.results[0][f"out_{name}"] for name, _ in _OUTS)
```
